# Optimizing a Trainium2 kernel written in Bass

```python
import jax, jax.numpy as jnp
from jax import lax
import numpy as np

D_MODEL = 1024
BATCH = 1
SEQ = 256
DEPTH = 2
DEC_BATCH = 8
DEC_SEQ = 4
PAST_LEN = 1024
PAGE_SIZE = 128

HEAD_DIM = 64
MIX_W = D_MODEL
CONV_CH = MIX_W // 4
CONV_WIDTH = 31
ATTN_GROUPS = ((128, 1), (512, 4), (2048, 16))
HEADS_PER_GROUP = (MIX_W - CONV_CH) // 2 // HEAD_DIM // len(ATTN_GROUPS)
ATTN_HEADS = HEADS_PER_GROUP * len(ATTN_GROUPS)
ATTN_W = ATTN_HEADS * HEAD_DIM
ATTN_SCALE = HEAD_DIM ** -0.5
RWKV_HEADS = (MIX_W - CONV_CH - ATTN_W) // HEAD_DIM
RWKV_W = RWKV_HEADS * HEAD_DIM
LORA_DECAY = 64
LORA_AAA = 64
LORA_GATE = 128
LNX_EPS = 64e-5
ROPE_THETA = 10000.0
MEM_TOKENS = 256
XATTN_HEADS = 4
XATTN_HEAD_DIM = D_MODEL // XATTN_HEADS
D_FF = 2816
NORM_EPS = 1e-6
A_COLS = 2 * CONV_CH
B_COLS = 3 * ATTN_W
C_COLS = 3 * RWKV_W + LORA_DECAY + LORA_AAA + LORA_GATE
IN_COLS = A_COLS + B_COLS + C_COLS
F32 = jnp.float32

kernel_name = 'hymba_conv_dilated_rwkv7_macaron_step'

def rmsnorm(x, g):
    xf = x.astype(F32)
    y = xf * lax.rsqrt(jnp.mean(xf * xf, axis=-1, keepdims=True) + NORM_EPS)
    return (y * g.astype(F32)).astype(x.dtype)

def swiglu_ffn(h, w_gate, w_up, w_down):
    return (jax.nn.silu(h @ w_gate) * (h @ w_up)) @ w_down

def rope(x, pos):
    half = x.shape[-1] // 2
    inv = jnp.power(ROPE_THETA, -jnp.arange(half, dtype=F32) / half)
    ang = pos.astype(F32)[:, None] * inv[None, :]
    cos = jnp.cos(ang)[None, :, None, :]
    sin = jnp.sin(ang)[None, :, None, :]
    xf = x.astype(F32)
    x1, x2 = xf[..., :half], xf[..., half:]
    return jnp.concatenate([x1 * cos - x2 * sin, x1 * sin + x2 * cos], axis=-1).astype(x.dtype)

def conv_module(u, conv_w, conv_b, ln_g, ln_b):
    y = lax.conv_general_dilated(u, conv_w[:, None, :], window_strides=(1,), padding='VALID',
                                 dimension_numbers=('NWC', 'WIO', 'NWC'),
                                 feature_group_count=CONV_CH) + conv_b
    yf = y.astype(F32)
    mu = jnp.mean(yf, axis=-1, keepdims=True)
    var = jnp.mean(jnp.square(yf - mu), axis=-1, keepdims=True)
    yn = (yf - mu) * lax.rsqrt(var + 1e-5) * ln_g.astype(F32) + ln_b.astype(F32)
    return jax.nn.silu(yn).astype(u.dtype)

def dilated_attn_prompt(q, k, v, window, dil):
    B, S, H, hd = q.shape
    nbk = window // dil
    L = S // dil
    nb = -(-L // nbk)
    Lp = nb * nbk

    def split(x):
        x = x.reshape(B, L, dil, H, hd).transpose(0, 2, 1, 3, 4)
        return jnp.pad(x, ((0, 0), (0, 0), (0, Lp - L), (0, 0), (0, 0)))

    def band(x):
        xp = jnp.pad(x, ((0, 0), (0, 0), (nbk, 0), (0, 0), (0, 0))).reshape(B, dil, nb + 1, nbk, H, hd)
        return jnp.concatenate([xp[:, :, :-1], xp[:, :, 1:]], axis=3)

    qb = split(q).reshape(B, dil, nb, nbk, H, hd)
    kb = band(split(k))
    vb = band(split(v))
    s = jnp.einsum('brnqhd,brnkhd->brnhqk', qb, kb).astype(F32) * ATTN_SCALE
    qi = jnp.arange(nbk)[:, None]
    kj = jnp.arange(2 * nbk)[None, :]
    rel = qi + nbk - kj
    blk = jnp.arange(nb)[:, None, None]
    valid = (rel >= 0) & (rel <= nbk) & (blk * nbk - nbk + kj >= 0)
    s = jnp.where(valid[None, None, :, None], s, -jnp.inf)
    m = jnp.max(s, axis=-1)
    p = jnp.exp(s - m[..., None])
    den = jnp.sum(p, axis=-1)
    o = jnp.einsum('brnhqk,brnkhd->brnqhd', p.astype(v.dtype), vb)

    def back(t):
        t = t.transpose(0, 1, 2, 4, 3).reshape(B, dil, Lp, H)[:, :, :L]
        return t.transpose(0, 2, 1, 3).reshape(B, S, H)

    o = o.reshape(B, dil, Lp, H, hd)[:, :, :L].transpose(0, 2, 1, 3, 4).reshape(B, S, H, hd)
    return o, back(m), back(den)

def dilated_attn_decode(q, kc, vc, window, dil, L):
    T = q.shape[1]
    nk = window // dil + 1
    idx = L + jnp.arange(T)[:, None] - dil * jnp.arange(nk)[None, :]
    valid = idx >= 0
    idx_c = jnp.maximum(idx, 0)
    kg = kc[:, idx_c]
    vg = vc[:, idx_c]
    s = jnp.einsum('bthd,btkhd->bthk', q, kg).astype(F32) * ATTN_SCALE
    s = jnp.where(valid[None, :, None, :], s, -jnp.inf)
    m = jnp.max(s, axis=-1)
    p = jnp.exp(s - m[..., None])
    den = jnp.sum(p, axis=-1)
    o = jnp.einsum('bthk,btkhd->bthd', p.astype(vc.dtype), vg)
    return o, m, den

def combine_dilations(parts):
    ms = jnp.stack([pt[1] for pt in parts])
    dens = jnp.stack([pt[2] for pt in parts])
    m_all = jnp.max(ms, axis=0)
    scl = jnp.exp(ms - m_all)
    wts = scl / jnp.sum(dens * scl, axis=0)
    return jnp.concatenate([pt[0] * wts[g][..., None].astype(pt[0].dtype) for g, pt in enumerate(parts)], axis=2)

def wkv_scan(S0, r, w, k, v, a, b):
    def step(S, inp):
        r_t, w_t, k_t, v_t, a_t, b_t = inp
        Sa = jnp.einsum('bhvk,bhk->bhv', S, a_t)
        S = S * w_t[:, :, None, :] + Sa[..., None] * b_t[:, :, None, :] + v_t[..., None] * k_t[:, :, None, :]
        return S, jnp.einsum('bhvk,bhk->bhv', S, r_t)
    xs = tuple(t.transpose(1, 0, 2, 3) for t in (r, w, k, v, a, b))
    S, o = lax.scan(step, S0, xs)
    return S, o.transpose(1, 0, 2, 3)

def rwkv_time_mix(cols, prev, S0, shift_mix, w0, w_up, a0, a_up, g_up, k_k, k_a, r_k, lnx_g, lnx_b):
    B, T, _ = cols.shape
    f = cols.astype(F32)
    shifted = jnp.concatenate([prev.astype(F32)[:, None], f[:, :-1]], axis=1)
    xs = f + (shifted - f) * shift_mix.astype(F32)
    r, k, v, wlo, alo, glo = jnp.split(xs, [RWKV_W, 2 * RWKV_W, 3 * RWKV_W, 3 * RWKV_W + LORA_DECAY,
                                            3 * RWKV_W + LORA_DECAY + LORA_AAA], axis=-1)
    w = -jax.nn.softplus(-(w0.astype(F32) + jnp.tanh(wlo) @ w_up.astype(F32))) - 0.5
    decay = jnp.exp(-jnp.exp(w))
    a = jax.nn.sigmoid(a0.astype(F32) + alo @ a_up.astype(F32))
    g = jax.nn.sigmoid(glo) @ g_up.astype(F32)

    def heads(t):
        return t.reshape(B, T, RWKV_HEADS, HEAD_DIM)

    kk = heads(k * k_k.astype(F32))
    kk = kk / jnp.maximum(jnp.sqrt(jnp.sum(kk * kk, axis=-1, keepdims=True)), 1e-12)
    k = k * (1.0 + (a - 1.0) * k_a.astype(F32))
    r_h, k_h, v_h, w_h, a_h = heads(r), heads(k), heads(v), heads(decay), heads(a)
    S, o = wkv_scan(S0.astype(F32), r_h, w_h, k_h, v_h, -kk, kk * a_h)
    mu = jnp.mean(o, axis=-1, keepdims=True)
    var = jnp.mean(jnp.square(o - mu), axis=-1, keepdims=True)
    o = ((o - mu) * lax.rsqrt(var + LNX_EPS)).reshape(B, T, RWKV_W) * lnx_g.astype(F32) + lnx_b.astype(F32)
    bonus = jnp.sum(r_h * k_h * r_k.astype(F32), axis=-1, keepdims=True) * v_h
    o = (o + bonus.reshape(B, T, RWKV_W)) * g
    return o.astype(cols.dtype), S

def cross_attend(h, mk, mv, w_q, w_o):
    B, T, D = h.shape
    q = (h @ w_q).reshape(B, T, XATTN_HEADS, XATTN_HEAD_DIM)
    s = jnp.einsum('bthd,bmhd->bhtm', q, mk).astype(F32) * (XATTN_HEAD_DIM ** -0.5)
    p = jax.nn.softmax(s, axis=-1).astype(mv.dtype)
    o = jnp.einsum('bhtm,bmhd->bthd', p, mv).reshape(B, T, D)
    return o @ w_o

def run_trunk(x, pos, P, mem, mem_k_cache, mem_v_cache, conv_cache, win_caches, shift_cache, wkv_cache):
    prompt = mem is not None
    B, T, D = x.shape
    n_groups = len(ATTN_GROUPS)
    conv_new, shift_new, wkv_new, memk_new, memv_new = [], [], [], [], []
    wink_new = [[] for _ in range(n_groups)]
    winv_new = [[] for _ in range(n_groups)]
    for l in range(DEPTH):
        h = rmsnorm(x, P['ffn1_norm'][l])
        x = x + 0.5 * swiglu_ffn(h, P['ffn1_w_gate'][l], P['ffn1_w_up'][l], P['ffn1_w_down'][l])

        h = rmsnorm(x, P['mix_norm'][l])
        cols = h @ P['w_in'][l]
        cols_a = cols[..., :A_COLS]
        cols_b = cols[..., A_COLS:A_COLS + B_COLS]
        cols_c = cols[..., A_COLS + B_COLS:]

        glu = cols_a[..., :CONV_CH] * jax.nn.sigmoid(cols_a[..., CONV_CH:])
        hist = jnp.zeros((B, CONV_WIDTH - 1, CONV_CH), x.dtype) if prompt else conv_cache[l]
        u = jnp.concatenate([hist, glu], axis=1)
        y_a = conv_module(u, P['conv_w'][l], P['conv_b'][l], P['conv_ln_g'][l], P['conv_ln_b'][l])
        conv_new.append(u[:, -(CONV_WIDTH - 1):])

        q, k, v = (t.reshape(B, T, ATTN_HEADS, HEAD_DIM) for t in jnp.split(cols_b, 3, axis=-1))
        q = rope(q, pos)
        k = rope(k, pos)
        parts = []
        for g, (win, dil) in enumerate(ATTN_GROUPS):
            hs = slice(g * HEADS_PER_GROUP, (g + 1) * HEADS_PER_GROUP)
            qg, kg, vg = q[:, :, hs], k[:, :, hs], v[:, :, hs]
            if prompt:
                parts.append(dilated_attn_prompt(qg, kg, vg, win, dil))
                keep = min(win, T)
                wink_new[g].append(kg[:, T - keep:])
                winv_new[g].append(vg[:, T - keep:])
            else:
                kbuf, vbuf = win_caches[g][0][l], win_caches[g][1][l]
                L = kbuf.shape[1]
                kc = jnp.concatenate([kbuf, kg], axis=1)
                vc = jnp.concatenate([vbuf, vg], axis=1)
                parts.append(dilated_attn_decode(qg, kc, vc, win, dil, L))
                wink_new[g].append(kc[:, -L:])
                winv_new[g].append(vc[:, -L:])
        y_b = combine_dilations(parts).reshape(B, T, ATTN_W)

        prev = jnp.zeros((B, C_COLS), x.dtype) if prompt else shift_cache[l]
        S0 = jnp.zeros((B, RWKV_HEADS, HEAD_DIM, HEAD_DIM), F32) if prompt else wkv_cache[l]
        y_c, S = rwkv_time_mix(cols_c, prev, S0, P['rwkv_shift_mix'][l], P['rwkv_w0'][l], P['rwkv_w_up'][l],
                               P['rwkv_a0'][l], P['rwkv_a_up'][l], P['rwkv_g_up'][l], P['rwkv_k_k'][l],
                               P['rwkv_k_a'][l], P['rwkv_r_k'][l], P['rwkv_lnx_g'][l], P['rwkv_lnx_b'][l])
        shift_new.append(cols_c[:, -1])
        wkv_new.append(S.astype(x.dtype))

        x = x + jnp.concatenate([y_a, y_b, y_c], axis=-1) @ P['w_out'][l]

        h = rmsnorm(x, P['xattn_norm'][l])
        if prompt:
            hm = rmsnorm(mem, P['mem_norm'][l])
            mk, mv = jnp.split(hm @ P['xattn_w_kv'][l], 2, axis=-1)
            mk = mk.reshape(B, mem.shape[1], XATTN_HEADS, XATTN_HEAD_DIM)
            mv = mv.reshape(B, mem.shape[1], XATTN_HEADS, XATTN_HEAD_DIM)
            memk_new.append(mk)
            memv_new.append(mv)
        else:
            mk, mv = mem_k_cache[l], mem_v_cache[l]
        x = x + cross_attend(h, mk, mv, P['xattn_w_q'][l], P['xattn_w_o'][l])

        h = rmsnorm(x, P['ffn2_norm'][l])
        x = x + 0.5 * swiglu_ffn(h, P['ffn2_w_gate'][l], P['ffn2_w_up'][l], P['ffn2_w_down'][l])

    y = rmsnorm(x, P['final_norm'])
    memk = jnp.stack(memk_new) if prompt else None
    memv = jnp.stack(memv_new) if prompt else None
    return (y, jnp.stack(conv_new),
            jnp.stack(wink_new[0]), jnp.stack(winv_new[0]),
            jnp.stack(wink_new[1]), jnp.stack(winv_new[1]),
            jnp.stack(wink_new[2]), jnp.stack(winv_new[2]),
            jnp.stack(shift_new), jnp.stack(wkv_new), memk, memv)

def setup_inputs(seed: int = 0) -> dict:
    key = jax.random.key(seed)
    keys = iter(jax.random.split(key, 64))

    def nrm(shape, scale):
        return scale * jax.random.normal(next(keys), shape, F32)

    def gain(shape):
        return 1.0 + 0.05 * jax.random.normal(next(keys), shape, F32)

    D = D_MODEL
    inp = {}
    inp['x_prompt'] = nrm((BATCH, SEQ, D), 1.0)
    inp['x_sample'] = nrm((DEC_BATCH, DEC_SEQ, D), 1.0)
    inp['cache_conv'] = nrm((DEPTH, DEC_BATCH, CONV_WIDTH - 1, CONV_CH), 0.5)
    for g, (win, dil) in enumerate(ATTN_GROUPS):
        L = min(win, PAST_LEN)
        inp['cache_win%d_k' % (g + 1)] = nrm((DEPTH, DEC_BATCH, L, HEADS_PER_GROUP, HEAD_DIM), 1.0)
        inp['cache_win%d_v' % (g + 1)] = nrm((DEPTH, DEC_BATCH, L, HEADS_PER_GROUP, HEAD_DIM), 1.0)
    inp['state_shift'] = nrm((DEPTH, DEC_BATCH, C_COLS), 1.0)
    inp['state_wkv'] = nrm((DEPTH, DEC_BATCH, RWKV_HEADS, HEAD_DIM, HEAD_DIM), 0.1)
    inp['cache_mem_k'] = nrm((DEPTH, DEC_BATCH, MEM_TOKENS, XATTN_HEADS, XATTN_HEAD_DIM), 1.0)
    inp['cache_mem_v'] = nrm((DEPTH, DEC_BATCH, MEM_TOKENS, XATTN_HEADS, XATTN_HEAD_DIM), 1.0)
    inp['mem_prompt'] = nrm((BATCH, MEM_TOKENS, D), 1.0)

    inp['ffn1_norm'] = gain((DEPTH, D))
    inp['ffn1_w_gate'] = nrm((DEPTH, D, D_FF), D ** -0.5)
    inp['ffn1_w_up'] = nrm((DEPTH, D, D_FF), D ** -0.5)
    inp['ffn1_w_down'] = nrm((DEPTH, D_FF, D), D_FF ** -0.5)
    inp['mix_norm'] = gain((DEPTH, D))
    inp['w_in'] = nrm((DEPTH, D, IN_COLS), D ** -0.5)
    inp['w_out'] = nrm((DEPTH, MIX_W, D), MIX_W ** -0.5)
    inp['conv_w'] = nrm((DEPTH, CONV_WIDTH, CONV_CH), CONV_WIDTH ** -0.5)
    inp['conv_b'] = nrm((DEPTH, CONV_CH), 0.02)
    inp['conv_ln_g'] = gain((DEPTH, CONV_CH))
    inp['conv_ln_b'] = nrm((DEPTH, CONV_CH), 0.02)
    inp['rwkv_shift_mix'] = jax.random.uniform(next(keys), (DEPTH, C_COLS), F32)
    inp['rwkv_w0'] = -1.0 + nrm((DEPTH, RWKV_W), 0.5)
    inp['rwkv_w_up'] = nrm((DEPTH, LORA_DECAY, RWKV_W), LORA_DECAY ** -0.5)
    inp['rwkv_a0'] = nrm((DEPTH, RWKV_W), 0.5)
    inp['rwkv_a_up'] = nrm((DEPTH, LORA_AAA, RWKV_W), LORA_AAA ** -0.5)
    inp['rwkv_g_up'] = nrm((DEPTH, LORA_GATE, RWKV_W), LORA_GATE ** -0.5)
    inp['rwkv_k_k'] = 0.85 + nrm((DEPTH, RWKV_W), 0.1)
    inp['rwkv_k_a'] = 1.0 + nrm((DEPTH, RWKV_W), 0.1)
    inp['rwkv_r_k'] = nrm((DEPTH, RWKV_HEADS, HEAD_DIM), 0.1)
    inp['rwkv_lnx_g'] = gain((DEPTH, RWKV_W))
    inp['rwkv_lnx_b'] = nrm((DEPTH, RWKV_W), 0.02)
    inp['xattn_norm'] = gain((DEPTH, D))
    inp['mem_norm'] = gain((DEPTH, D))
    inp['xattn_w_q'] = nrm((DEPTH, D, D), D ** -0.5)
    inp['xattn_w_kv'] = nrm((DEPTH, D, 2 * D), D ** -0.5)
    inp['xattn_w_o'] = nrm((DEPTH, D, D), D ** -0.5)
    inp['ffn2_norm'] = gain((DEPTH, D))
    inp['ffn2_w_gate'] = nrm((DEPTH, D, D_FF), D ** -0.5)
    inp['ffn2_w_up'] = nrm((DEPTH, D, D_FF), D ** -0.5)
    inp['ffn2_w_down'] = nrm((DEPTH, D_FF, D), D_FF ** -0.5)
    inp['final_norm'] = gain((D,))
    return inp

def reference(x_prompt, x_sample, cache_conv, cache_win1_k, cache_win1_v, cache_win2_k, cache_win2_v,
              cache_win3_k, cache_win3_v, state_shift, state_wkv, cache_mem_k, cache_mem_v, mem_prompt,
              ffn1_norm, ffn1_w_gate, ffn1_w_up, ffn1_w_down, mix_norm, w_in, w_out,
              conv_w, conv_b, conv_ln_g, conv_ln_b,
              rwkv_shift_mix, rwkv_w0, rwkv_w_up, rwkv_a0, rwkv_a_up, rwkv_g_up, rwkv_k_k, rwkv_k_a,
              rwkv_r_k, rwkv_lnx_g, rwkv_lnx_b,
              xattn_norm, mem_norm, xattn_w_q, xattn_w_kv, xattn_w_o,
              ffn2_norm, ffn2_w_gate, ffn2_w_up, ffn2_w_down, final_norm):
    P = dict(ffn1_norm=ffn1_norm, ffn1_w_gate=ffn1_w_gate, ffn1_w_up=ffn1_w_up, ffn1_w_down=ffn1_w_down,
             mix_norm=mix_norm, w_in=w_in, w_out=w_out,
             conv_w=conv_w, conv_b=conv_b, conv_ln_g=conv_ln_g, conv_ln_b=conv_ln_b,
             rwkv_shift_mix=rwkv_shift_mix, rwkv_w0=rwkv_w0, rwkv_w_up=rwkv_w_up, rwkv_a0=rwkv_a0,
             rwkv_a_up=rwkv_a_up, rwkv_g_up=rwkv_g_up, rwkv_k_k=rwkv_k_k, rwkv_k_a=rwkv_k_a,
             rwkv_r_k=rwkv_r_k, rwkv_lnx_g=rwkv_lnx_g, rwkv_lnx_b=rwkv_lnx_b,
             xattn_norm=xattn_norm, mem_norm=mem_norm, xattn_w_q=xattn_w_q, xattn_w_kv=xattn_w_kv,
             xattn_w_o=xattn_w_o, ffn2_norm=ffn2_norm, ffn2_w_gate=ffn2_w_gate, ffn2_w_up=ffn2_w_up,
             ffn2_w_down=ffn2_w_down, final_norm=final_norm)

    pos_p = jnp.arange(x_prompt.shape[1], dtype=jnp.int32)
    (y_prompt, conv_p, win1_k_p, win1_v_p, win2_k_p, win2_v_p, win3_k_p, win3_v_p,
     shift_p, wkv_p, mem_k_p, mem_v_p) = run_trunk(x_prompt, pos_p, P, mem_prompt, None, None,
                                                   None, None, None, None)

    pos_s = PAST_LEN + jnp.arange(x_sample.shape[1], dtype=jnp.int32)
    win_caches = [(cache_win1_k, cache_win1_v), (cache_win2_k, cache_win2_v), (cache_win3_k, cache_win3_v)]
    (y_sample, conv_s, win1_k_s, win1_v_s, win2_k_s, win2_v_s, win3_k_s, win3_v_s,
     shift_s, wkv_s, _unused_k, _unused_v) = run_trunk(x_sample, pos_s, P, None, cache_mem_k, cache_mem_v,
                                                       cache_conv, win_caches, state_shift, state_wkv)

    return (y_prompt, y_sample,
            conv_p, win1_k_p, win1_v_p, win2_k_p, win2_v_p, win3_k_p, win3_v_p, shift_p, wkv_p, mem_k_p, mem_v_p,
            conv_s, win1_k_s, win1_v_s, win2_k_s, win2_v_s, win3_k_s, win3_v_s, shift_s, wkv_s)


_drawn_inputs = setup_inputs


def setup_inputs(seed=0):
    import zlib

    import numpy as np

    out = dict(_drawn_inputs(seed))
    spreads = {}
    factors = {'conv_b': 3.171, 'conv_ln_b': 6.897, 'rwkv_lnx_b': 6.053, 'xattn_norm': 8.0}
    for name, (base, spread) in spreads.items():
        noise = np.random.default_rng([zlib.crc32(name.encode()), seed]).standard_normal(out[name].shape)
        drawn = base * np.exp(spread * noise) if base else spread * noise
        out[name] = __import__('jax').numpy.asarray(drawn.astype(out[name].dtype))
    for name, factor in factors.items():
        out[name] = (out[name] * factor).astype(out[name].dtype)
    return out
```

```python
from contextlib import ExitStack

import numpy as np

import concourse.bass as bass
from concourse import mybir

F32 = mybir.dt.float32
ALU = mybir.AluOpType
ACT = mybir.ActivationFunctionType
AX_X = mybir.AxisListType.X

P = 128
DEPTH, D_MODEL, D_FF = 2, 1024, 2816
TP, DEC_BATCH, DEC_SEQ = 256, 8, 4
TS = DEC_BATCH * DEC_SEQ
T = TP + TS
PAST_LEN = 1024
MEM = 256
KT = D_MODEL // P
FT = D_FF // P
HD = 64
TAPS = 31
HIST = TAPS - 1
GROUPS = ((128, 1), (512, 4), (2048, 16))
G = len(GROUPS)
CACHED = tuple(min(w, PAST_LEN) for w, _ in GROUPS)
ATTN_SCALE, X_SCALE = HD ** -0.5, 256 ** -0.5
NORM_EPS, CONV_EPS, LNX_EPS = 1e-6, 1e-5, 64e-5
HALF_DECAY = 0.5 * float(np.exp(-0.5))
NEG = -1e30
J = 3
LEVELS = (2, 4, 8, 16, 32, 64)

C_LO, C_G, C_K, C_R, C_V = 0, 1, 2, 5, 8
NC_TILES = 11
IN_TILES = 24

SLAB = 2048
NSLOT = 7
STAGES = (("ffn1", 33), ("in", 12), ("wink", 4), ("winv", 4), ("out", 4), ("q", 4), ("kv", 8),
          ("memk", 8), ("memv", 8), ("o", 4), ("ffn2", 33))
BASE, NSLAB = {}, 0
for _name, _n in STAGES:
    BASE[_name] = NSLAB
    NSLAB += _n
ROUNDS = NSLAB // NSLOT
REST = NSLAB - ROUNDS * NSLOT
NSTORE = 9

PAR, NPAR = {}, 0
for _name, _n in (("ffn1", 8), ("mix", 8), ("xattn", 8), ("mem", 8), ("ffn2", 8), ("final", 8), ("conv_w", 2 * TAPS),
                  ("conv_b", 2), ("conv_g", 2), ("conv_beta", 2), ("shift", NC_TILES), ("w0", J), ("a0", J),
                  ("k_k", J), ("k_a", J), ("r_k", J), ("lnx_g", J), ("lnx_b", J), ("state_shift", NC_TILES * 8),
                  ("lora", 2 * J * P)):
    PAR[_name] = NPAR
    NPAR += _n

CON, NCON = {}, 0
for _name, _n in (("ident", P), ("ones", P), ("heads", P), ("turn", P), ("cos", T), ("sin", T), ("mask", 2 * G * TP),
                  ("mask_s", G * (P + TS)), ("level1", 2 * P), ("levels", len(LEVELS) * P), ("strict", P), ("upper", P),
                  ("s_masks", 6 * TS), ("s_batch", DEC_BATCH), ("scan", J * T)):
    CON[_name] = NCON
    NCON += _n


def constants():
    c = np.zeros((P, NCON), np.float32)

    def put(name, a, rows=P):
        a = np.asarray(a, np.float32).reshape(rows, -1)
        c[:rows, CON[name]:CON[name] + a.shape[1]] = a

    i = np.arange(P)
    put("ident", np.eye(P))
    put("ones", np.ones((P, P)))
    put("heads", i[:, None] // HD == i[None] // HD)
    turn = np.zeros((P, P))
    for m in range(P):
        turn[m + 32 if m % HD < 32 else m - 32, m] = -1.0 if m % HD < 32 else 1.0
    put("turn", turn)
    half = HD // 2
    inv = np.power(np.float32(10000.0), -np.arange(half, dtype=np.float32) / np.float32(half)).astype(np.float32)
    pos = np.concatenate([np.arange(TP), np.tile(PAST_LEN + np.arange(DEC_SEQ), DEC_BATCH)]).astype(np.float32)
    ang = (inv[i % half][:, None] * pos[None]).astype(np.float32)
    put("cos", np.cos(ang))
    put("sin", np.sin(ang))
    mask = np.full((P, 2, G, TP), NEG)
    for qt in range(2):
        q = qt * P + i[:, None]
        k = np.arange(TP)[None]
        for g, (win, dil) in enumerate(GROUPS):
            mask[:, qt, g][(q >= k) & (q - k <= win) & ((q - k) % dil == 0)] = 0
    put("mask", mask)
    ms = np.full((DEC_BATCH, 2, DEC_SEQ, G, P + TS), NEG)
    key = np.arange(P)
    for b in range(DEC_BATCH):
        for t in range(DEC_SEQ):
            ms[b, :, t, 0, :P][:, key >= t] = 0
            ms[b, :, t, 1, :P] = 0
            ms[b, :, t, 2, :P][:, key // 64 == t % 2] = 0
            ms[b, :, t, 0, P + DEC_SEQ * b:P + DEC_SEQ * b + t + 1] = 0
            ms[b, :, t, 1:, P + DEC_SEQ * b + t] = 0
    put("mask_s", ms, rows=64)
    t, s = i[:, None], i[None]

    def level(m):
        return (t // (2 * m) == s // (2 * m)) & (t % (2 * m) >= m) & (s % (2 * m) < m)

    put("level1", np.concatenate([level(1), level(1).T], 1))
    put("levels", np.concatenate([level(m) for m in LEVELS], 1))
    put("strict", (t < s))
    put("upper", (t <= s))
    same = (t // DEC_SEQ == s // DEC_SEQ)
    small = [level(1), level(2), level(1).T, same & (t < s), same & (t <= s), same & (t <= s)]
    put("s_masks", np.concatenate([m[:TS, :TS] for m in small], 1), rows=TS)
    put("s_batch", i[:TS, None] // DEC_SEQ == np.arange(DEC_BATCH)[None], rows=TS)
    keep = np.ones((P, J, T))
    keep[:, :, 0:TP:P] = 0
    keep[:, :, TP::DEC_SEQ] = 0
    put("scan", keep)
    return c


class Line:

    def __init__(self, sem, known):
        self.sem, self.n, self.at, self.last = sem, 0, {}, None
        self.known, self.total = known if known else ({}, 1)

    def done(self, ins, name=None):
        if ins is not self.last:
            self.n += 1
            ins.then_inc(self.sem, 1)
            self.last = ins
        if name is not None:
            assert self.at.setdefault(name, self.n) == self.n, name
        return ins

    def begin_layer(self):
        self.n = 0

    def per_layer(self):
        return max((c for name, c in self.at.items() if name[0] != "final"), default=0)

    def value(self, l, name):
        return l * self.total + (self.total + (self.known.get(name, 1) if self.known else 1))

    def value_before(self, l, name):
        return l * self.total + (self.known.get(name, 1) if self.known else 1)

    def so_far(self, l):
        return l * self.total + (self.total + self.n)


def program(nc, x_in, mem_in, stream, small, consts, conv_hist, wkv_in, copies, outs, known=None):
    (y_out, conv_out, kv_out, shift_out, wkv_p_out, wkv_s_out, memk_out, memv_out) = outs
    known = known or {}
    with ExitStack() as ctx:
        def sb(name, shape):
            return ctx.enter_context(nc.sbuf_tensor(name, shape, F32))

        def sem(name):
            return ctx.enter_context(nc.semaphore(name))

        bank = [ctx.enter_context(nc.psum_tensor(f"bank{i}", [P, 512], F32)) for i in range(8)]

        slots = sb("slots", [P, NSLOT, SLAB])
        x = sb("x", [P, KT, T])
        h = sb("h", [P, KT, T])
        par_all = sb("par_all", [P, DEPTH, NPAR])
        par = sb("par", [P, NPAR])
        con = sb("con", [P, NCON])
        rs = sb("rs", [P, T])
        halves = sb("halves", [P, 2 * J])[:]
        tmp2 = sb("tmp2", [P, 8])
        mem_rs = sb("mem_rs", [P, MEM])
        arena = sb("arena", [P, 24900])

        def c(name, n, rows=P, at=0):
            return con[0:rows, CON[name] + at:CON[name] + at + n]

        def pr(name, i):
            return par[:, PAR[name] + i:PAR[name] + i + 1]

        ident, ones, heads = c("ident", P), c("ones", P), c("heads", P)

        top = [0]

        def take(*dims):
            n = int(np.prod(dims))
            v = arena[:, top[0]:top[0] + n]
            top[0] += n
            assert top[0] <= 24900, top[0]
            if len(dims) == 1:
                return v
            names = "abcd"[:len(dims)]
            return v.rearrange(f"p ({' '.join(names)}) -> p {' '.join(names)}",
                               **{k: d for k, d in zip(names[1:], dims[1:])})

        sq = take(KT, T)
        hid = take(FT, T)
        th = take(2, T)
        th2 = take(2, T)
        top[0] = KT * T
        qx = take(KT, T)
        ox = take(KT, T)
        kx = take(KT, MEM)
        vx = take(2, 4 * MEM)
        pxT = take(4, 2, TP)
        memx = pxT.rearrange("p a b c -> p (a b) c")
        hm = ox.rearrange("p a b -> p (a b)")[:, 0:KT * MEM].rearrange("p (a b) -> p a b", a=KT)
        px = take(9, MEM)
        sxT = take(2, P)
        pxsT = take(2, P)
        xstat = take(4, 9)
        top[0] = 0
        xs = take(NC_TILES, T)
        qkv = take(3 * G, T)
        up = take(2, HIST + TP)
        us = take(2, DEC_BATCH * (HIST + DEC_SEQ))
        a_p, b_p, k_p, r_p = (take(J, T) for _ in range(4))
        gz, bon, oT = (take(J, T) for _ in range(3))
        wend = take(J, 2 + DEC_BATCH)
        wmid1 = take(J, 1)
        mids = take(J, 2)
        vtok = take(2, G, P)
        vtok_s = take(G, P)
        shift_o = take(NC_TILES, 1 + DEC_BATCH)
        base2 = top[0]
        f = take(NC_TILES, 1 + TP + DEC_BATCH * (1 + DEC_SEQ))
        wid = 1 + TP + DEC_BATCH * (1 + DEC_SEQ)
        ld, cl, w_c, w_p, w_i = (take(J, T) for _ in range(5))
        aa, kk = (take(J, T) for _ in range(2))
        k2 = xs[:, C_K:C_K + J, :]
        tmp = take(J, T)
        top[0] = base2
        lab, tm, xm, lo, ym, lak, lrb, lrk = (take(2, J * P) for _ in range(8))
        rm, um, st = (take(J * P) for _ in range(3))
        tok = take(3, J * P)
        top[0] = base2
        wkv_s = take(J, DEC_BATCH * P)
        usel, vsel = take(DEC_BATCH, P), take(DEC_BATCH, P)
        sm = take(2, 6, J * TS)
        sy = take(2, J * TS)
        tmp_s, rm2, um2 = take(J * TS), take(J * P), take(J * P)
        tok2 = take(3, J * P)
        tmp_ln = take(J, T)
        ycv, yc2 = take(2, T), take(2, T)
        yc = ycv
        top[0] = base2
        sp_ = take(2, G * TP)
        spT = take(2, G, 2, P)
        qbd = take(G, 64)
        ss = take(G * (P + TS))
        ssT, ssn = take(G, 64), take(G, 64)
        psT, psn = take(G, 64), take(G, 64)
        astat = take(4, 6)

        us4 = us.rearrange("p a (b t) -> p a b t", b=DEC_BATCH)
        f_p = f[:, :, 0:1 + TP]
        f_s = f[:, :, 1 + TP:].rearrange("p c (b t) -> p c b t", b=DEC_BATCH)

        def bt(ap):
            return ap.rearrange("p (b t) -> p b t", t=DEC_SEQ)

        tensor_done, vector_done, scalar_done = sem("tensor_done"), sem("vector_done"), sem("scalar_done")
        slab_landed = [sem(f"slab_landed{i}") for i in range(NSLOT)]
        start_landed = sem("start_landed")
        layer_landed = sem("layer_landed")
        wkv_landed = sem("wkv_landed")
        mem_landed = sem("mem_landed")
        stored = sem("stored")
        copied = sem("copied")
        TL, VL, SL = (Line(s, known.get(n)) for s, n in ((tensor_done, "t"), (vector_done, "v"), (scalar_done, "s")))
        store_known = known.get("stores", {})
        stores = {}

        block = ctx.enter_context(nc.Block())

        @block.sync
        def _(sp):
            sp.dma_start(x[:], x_in).then_inc(start_landed, 16)
            sp.dma_start(par_all[:], small).then_inc(start_landed, 16)
            sp.dma_start(con[:], consts).then_inc(start_landed, 16)
            flat = stream.rearrange("l n p c -> (l n) p c")
            for l in range(DEPTH):
                for n in range(NSLAB):
                    if n >= NSLOT:
                        sp.wait_ge(tensor_done, TL.value(l, ("slab", n - NSLOT)))
                    else:
                        held = n + NSLOT * (ROUNDS - (n >= REST))
                        sp.wait_ge(tensor_done, TL.value_before(l, ("slab", held)))
                    sp.dma_start(slots[:, n % NSLOT, :], stream[l, n]).then_inc(slab_landed[n % NSLOT], 16)
                    if n in (40, 46, 52, 58, 64, 70):
                        src, dst = copies[(n - 40) // 6]
                        sp.dma_start(dst[l], src[l]).then_inc(copied, 16)
            sp.wait_ge(copied, 16 * 6 * DEPTH)

        @block.gpsimd
        def _(pool):
            n_stores = [0]

            def store(dst, src, name):
                pool.dma_start(dst, src).then_inc(stored, 16)
                n_stores[0] += 1
                stores[name] = n_stores[0]

            for l in range(DEPTH):
                n_stores[0] = 0
                pool.wait_ge(vector_done, VL.value(l, ("ffn1", "x", 1)))
                pool.wait_ge(tensor_done, TL.value(l, ("ffn1", "down", 1)))
                pool.dma_start(us4[:, :, :, 0:HIST], conv_hist[l]).then_inc(layer_landed, 16)
                pool.wait_ge(vector_done, VL.value(l, "roped"))
                pool.wait_ge(scalar_done, SL.value(l, ("in", IN_TILES - 1)))
                store(kv_out[l], qkv[:, G:3 * G, :], "kv")
                pool.wait_ge(vector_done, VL.value(l, ("glu", 1)))
                store(conv_out[l, :, :, 0:HIST], up[:, :, TP:TP + HIST], "conv_p")
                store(conv_out[l, :, :, HIST:].rearrange("p a (b t) -> p a b t", b=DEC_BATCH)[:, 0],
                      us4[:, 0, :, DEC_SEQ:], "conv_s0")
                store(conv_out[l, :, :, HIST:].rearrange("p a (b t) -> p a b t", b=DEC_BATCH)[:, 1],
                      us4[:, 1, :, DEC_SEQ:], "conv_s1")
                pool.wait_ge(vector_done, VL.value(l, "shift_out"))
                store(shift_out[l], shift_o, "shift")
                pool.wait_ge(vector_done, VL.value(l, ("state", 1)))
                store(wkv_p_out[l], st, "wkv_p")
                pool.wait_ge(tensor_done, TL.value(l, ("o_state", 1)))
                pool.wait_ge(stored, l * (16 * NSTORE) + 16 * n_stores[0])
                pool.dma_start(wkv_s, wkv_in[l]).then_inc(wkv_landed, 16)
                pool.wait_ge(vector_done, VL.value(l, "wkv_s"))
                store(wkv_s_out[l], wkv_s, "wkv_s")
                pool.wait_ge(vector_done, VL.value(l, ("x_out", KT - 1)))
                pool.wait_ge(stored, l * (16 * NSTORE) + 16 * n_stores[0])
                pool.dma_start(memx, mem_in).then_inc(mem_landed, 16)
                pool.wait_ge(scalar_done, SL.value(l, ("kx", KT - 1)))
                store(memk_out[l], kx, "memk")
                pool.wait_ge(scalar_done, SL.value(l, ("vx", 7)))
                store(memv_out[l], vx, "memv")
            assert n_stores[0] == NSTORE
            pool.wait_ge(vector_done, VL.value(DEPTH - 1, ("final", "h", KT - 1)))
            pool.dma_start(y_out, h[:]).then_inc(stored, 16)
            pool.wait_ge(stored, 16 * (NSTORE * DEPTH + 1))

        def store_value(l, name):
            return l * (16 * NSTORE) + 16 * store_known.get(name, 1)

        @block.tensor
        def _(pe):
            pe.sem_inc(tensor_done, TL.total)
            pe.wait_ge(start_landed, 48)
            mm = nc.tensor.matmul
            for l in range(DEPTH):
                TL.begin_layer()
                free = [None] * 8

                def after(line, name):
                    pe.wait_ge(line.sem, line.value(l, name))

                def claim(b, released_by):
                    if free[b] is not None:
                        after(*free[b])
                    free[b] = released_by

                def arrived(n):
                    s = n % NSLOT
                    per = ROUNDS + (s < REST)
                    pe.wait_ge(slab_landed[s], l * (16 * per) + 16 * (n // NSLOT + 1))
                    return slots[:, s, :]

                given = [0]

                def give_back(ins):
                    TL.done(ins, ("slab", given[0]))
                    given[0] += 1

                def sum_squares(tag, n=T):
                    for k in range(KT):
                        if k == 0:
                            claim(7, (SL, (tag, "rms")))
                        after(SL, (tag, "sq", k))
                        i = mm(bank[7][:, 0:n], ones, sq[:, k, 0:n], start=k == 0, stop=k == KT - 1)
                    TL.done(i, (tag, "ss"))

                def ffn(tag):
                    sum_squares(tag)
                    at = BASE[tag]
                    for t in range(FT):
                        gb, ub = (t % 2) * 2, (t % 2) * 2 + 1
                        claim(gb, (VL, (tag, "gated", t)))
                        claim(ub, (VL, (tag, "hid", t)))
                        for b, o in ((gb, 0), (ub, 1)):
                            n = at + 2 * (t // 2) + o
                            w = arrived(n).rearrange("p (k c) -> p k c", k=KT)
                            for k in range(KT):
                                if t == 0 and o == 0:
                                    after(VL, (tag, "h", k))
                                i = mm(bank[b][:, 0:T], w[:, k, (t % 2) * P:(t % 2 + 1) * P], h[:, k, :],
                                       start=k == 0, stop=k == KT - 1)
                            if t % 2 == 1:
                                give_back(i)
                            TL.done(i, (tag, "up" if o else "gate", t))
                    at += FT
                    for q in range(2 * FT):
                        half, t = divmod(q, FT)
                        if q % 4 == 0:
                            w = arrived(at + q // 4).rearrange("p (k c) -> p k c", k=4)
                        if half == 0:
                            after(VL, (tag, "hid", t))
                        for d in range(4):
                            b = 4 + d if half == 0 else d
                            if t == 0:
                                claim(b, (VL, (tag, "x", half)))
                            i = mm(bank[b][:, 0:T], w[:, q % 4, d * P:(d + 1) * P], hid[:, t, :],
                                   start=t == 0, stop=t == FT - 1)
                        if q % 4 == 3:
                            give_back(i)
                        if t == FT - 1:
                            TL.done(i, (tag, "down", half))

                def columns(tag, base, n_tiles, src, src_name, banks, reader):
                    for t in range(n_tiles):
                        b = banks[t % len(banks)]
                        claim(b, reader(t))
                        w = arrived(base + t // 2).rearrange("p (k c) -> p k c", k=KT)
                        for k in range(KT):
                            if t == 0:
                                after(*src_name(k))
                            i = mm(bank[b][:, 0:src.shape[2]], w[:, k, (t % 2) * P:(t % 2 + 1) * P], src[:, k, :],
                                   start=k == 0, stop=k == KT - 1)
                        if t % 2 == 1:
                            give_back(i)
                        TL.done(i, (tag, "cols", t))

                ffn("ffn1")

                sum_squares("mix")

                def in_reader(t):
                    if t in (11, 13):
                        return VL, ("glu", (t - 11) // 2)
                    return SL, ("in", t)
                columns("in", BASE["in"], IN_TILES, h, lambda k: (VL, ("mix", "h", k)), range(7), in_reader)

                lora = par[:, PAR["lora"]:PAR["lora"] + 2 * J * P]
                after(SL, "lo_tanh")
                after(VL, "lo_gate")
                for kind, rows, off, src in ((0, slice(0, 64), 0, tmp[0:64, 0, :]), (1, slice(64, P), 0, xs[64:P, C_LO, :]),
                                             (2, slice(0, P), J * P, xs[:, C_G, :])):
                    for j in range(J):
                        b = (kind * J + j) % 7
                        claim(b, (SL, ("lora", kind, j)))
                        i = mm(bank[b][:, 0:T], lora[rows, off + j * P:off + (j + 1) * P], src, start=True, stop=True)
                        TL.done(i, ("lora", kind, j))

                for i6 in range(2 * G):
                    b = (2 + i6) % 7
                    claim(b, (VL, ("rope", i6)))
                    after(SL, ("in", 15 + i6))
                    i = mm(bank[b][:, 0:T], c("turn", P), qkv[:, i6, :], start=True, stop=True)
                    TL.done(i, ("turn", i6))

                for j in range(J):
                    claim(j, (SL, ("kk_norm", j)))
                    after(SL, "kk_sq")
                    TL.done(mm(bank[j][:, 0:T], heads, tmp[:, j, :], start=True, stop=True), ("kk_ss", j))
                for j in range(J):
                    claim(3 + j, (SL, ("bonus", j)))
                    after(VL, ("rkr", J - 1))
                    TL.done(mm(bank[3 + j][:, 0:T], heads, oT[:, j, :], start=True, stop=True), ("bonus", j))

                for ct in range(3):
                    n, rows = (P, slice(ct * P, (ct + 1) * P)) if ct < 2 else (TS, slice(TP, T))
                    claim(ct, (SL, ("vtok", ct)))
                    after(SL, ("in", IN_TILES - 1))
                    for g in range(G):
                        i = nc.tensor.transpose(bank[ct][0:n, g * P:(g + 1) * P], qkv[:, 2 * G + g, rows], ident)
                    TL.done(i, ("vtok", ct))

                def vt(j, ct):
                    return xs[:, C_V + j, ct * P:(ct + 1) * P] if ct < 2 else xs[:, C_V + j, TP:T]

                def tile(a, j, ct):
                    return a[:, j, ct * P:(ct + 1) * P] if ct < 2 else a[:, j, TP:T]

                def hh_rows(a, hh):
                    return a[hh * HD:(hh + 1) * HD]

                after(VL, "primed")
                for ct in range(2):
                    for kind, (lhs, rhs) in enumerate(((a_p, b_p), (b_p, a_p), (k_p, a_p), (b_p, r_p), (k_p, r_p))):
                        for hh in range(2):
                            b = (kind * 2 + hh) % 8
                            claim(b, (VL, ("pair", ct, kind, hh)))
                            for j in range(J):
                                i = mm(bank[b][:, j * P:(j + 1) * P], hh_rows(tile(lhs, j, ct), hh),
                                       hh_rows(tile(rhs, j, ct), hh), start=True, stop=True)
                            TL.done(i, ("pair", ct, kind, hh))
                    for kind, src in enumerate((b_p, k_p, None)):
                        b = (2 + kind) % 8
                        claim(b, (SL, ("tok", ct, kind)))
                        for j in range(J):
                            s_ = vt(j, ct) if src is None else tile(src, j, ct)
                            i = nc.tensor.transpose(bank[b][:, j * P:(j + 1) * P], s_, ident)
                        TL.done(i, ("tok", ct, kind))
                    for m in range(len(LEVELS)):
                        last = m == len(LEVELS) - 1
                        for hh in range(2):
                            claim(hh, (SL, ("y", ct, m, hh)))
                            after(VL, ("lo", ct, m))
                            after(VL, ("x", ct, m - 1, hh) if m else ("x0", ct, hh))
                            for j in range(J):
                                s_ = slice(j * P, (j + 1) * P)
                                i = mm(bank[hh][:, s_], lo[:, hh, s_], xm[:, hh, s_], start=True, stop=True)
                            TL.done(i, ("y", ct, m, hh))
                        for hh in range(2):
                            claim(2 + hh, (VL, ("x", ct, m, hh)))
                            after(SL, ("y", ct, m, hh))
                            after(VL, ("t", ct, m - 1, hh) if m else ("t0", ct, hh))
                            for j in range(J):
                                s_ = slice(j * P, (j + 1) * P)
                                i = mm(bank[2 + hh][:, s_], tm[:, hh, s_], ym[:, hh, s_], start=True, stop=True)
                            TL.done(i, ("xinc", ct, m, hh))
                            if last:
                                continue
                            claim(4 + hh, (VL, ("t", ct, m, hh)))
                            for j in range(J):
                                s_ = slice(j * P, (j + 1) * P)
                                i = mm(bank[4 + hh][:, s_], ym[:, hh, s_], tm[:, hh, s_], start=True, stop=True)
                            TL.done(i, ("tinc", ct, m, hh))
                    claim(6, (SL, ("r", ct)))
                    after(SL, ("tok", ct, 2))
                    if ct:
                        after(VL, ("state", 0))
                    for j in range(J):
                        o = bank[6][:, j * P:(j + 1) * P]
                        if ct:
                            mm(o, tile(a_p, j, ct), st[:, j * P:(j + 1) * P], start=True, stop=False, skip_group_check=True)
                        for hh in range(2):
                            i = mm(o[:, hh * HD:(hh + 1) * HD], lak[:, hh, j * P:(j + 1) * P],
                                   tok[:, 2, j * P + hh * HD:j * P + (hh + 1) * HD], start=ct == 0, stop=True,
                                   skip_group_check=True)
                    TL.done(i, ("r", ct))
                    claim(7, (SL, ("u", ct)))
                    after(SL, ("r", ct))
                    after(VL, ("x", ct, len(LEVELS) - 1, 1))
                    for j in range(J):
                        for hh in range(2):
                            s_ = slice(j * P + hh * HD, j * P + (hh + 1) * HD)
                            i = mm(bank[7][:, s_], xm[:, hh, j * P:(j + 1) * P], rm[:, s_], start=True, stop=True)
                    TL.done(i, ("u", ct))
                    claim(4, (SL, ("o", ct)))
                    claim(5, (VL, ("state", ct)))
                    after(SL, ("u", ct))
                    for j in range(J):
                        o = bank[4][:, j * P:(j + 1) * P]
                        if ct:
                            mm(o, st[:, j * P:(j + 1) * P], tile(r_p, j, ct), start=True, stop=False, skip_group_check=True)
                        for hh in range(2):
                            s_ = slice(j * P + hh * HD, j * P + (hh + 1) * HD)
                            oo = bank[4][hh * HD:(hh + 1) * HD, j * P:(j + 1) * P]
                            mm(oo, um[:, s_], lrb[:, hh, j * P:(j + 1) * P], start=ct == 0, stop=False, skip_group_check=True)
                            mm(oo, tok[:, 2, s_], lrk[:, hh, j * P:(j + 1) * P], start=False, stop=True, skip_group_check=True)
                        s_ = slice(j * P, (j + 1) * P)
                        mm(bank[5][:, s_], tok[:, 0, s_], um[:, s_], start=True, stop=False)
                        i = mm(bank[5][:, s_], tok[:, 1, s_], tok[:, 2, s_], start=False, stop=True)
                    TL.done(i, ("o_state", ct))

                for hh in range(2):
                    claim(hh, (VL, ("s_pair", hh)))
                    for kind, (lhs, rhs) in enumerate(((a_p, b_p), (b_p, a_p), (k_p, a_p), (b_p, r_p), (k_p, r_p))):
                        for j in range(J):
                            o = (kind * J + j) * TS
                            i = mm(bank[hh][0:TS, o:o + TS], hh_rows(tile(lhs, j, 2), hh), hh_rows(tile(rhs, j, 2), hh),
                                   start=True, stop=True)
                    TL.done(i, ("s_pair", hh))
                for kind, src in enumerate((b_p, k_p, None)):
                    claim(2 + kind, (SL, ("tok", 2, kind)))
                    for j in range(J):
                        s_ = vt(j, 2) if src is None else tile(src, j, 2)
                        i = nc.tensor.transpose(bank[2 + kind][0:TS, j * P:(j + 1) * P], s_, ident)
                    TL.done(i, ("tok", 2, kind))
                claim(5, (SL, "s_r0"))
                pe.wait_ge(wkv_landed, 16 * l + 16)
                for j in range(J):
                    for b_ in range(DEC_BATCH):
                        col = TP + b_ * DEC_SEQ
                        i = mm(bank[5][:, j * TS + b_ * DEC_SEQ:j * TS + (b_ + 1) * DEC_SEQ],
                               wkv_s[:, j, b_ * P:(b_ + 1) * P], a_p[:, j, col:col + DEC_SEQ], start=True, stop=True)
                TL.done(i, "s_r0")
                claim(0, (SL, "s_y"))
                claim(1, (VL, "s_x"))
                for hh in range(2):
                    after(VL, ("s_masked", hh))
                for hh in range(2):
                    for j in range(J):
                        s_ = slice(j * TS, (j + 1) * TS)
                        i = mm(bank[0][0:TS, (hh * J + j) * TS:(hh * J + j + 1) * TS], sm[0:TS, hh, 1, s_], sm[0:TS, hh, 2, s_],
                               start=True, stop=True)
                TL.done(i, "s_y")
                after(SL, "s_y")
                for hh in range(2):
                    for j in range(J):
                        s_ = slice(j * TS, (j + 1) * TS)
                        i = mm(bank[1][0:TS, (hh * J + j) * TS:(hh * J + j + 1) * TS], sm[0:TS, hh, 0, s_], sy[0:TS, hh, s_],
                               start=True, stop=True)
                TL.done(i, "s_xinc")
                claim(6, (SL, ("r", 2)))
                after(SL, "s_r0")
                after(SL, ("tok", 2, 2))
                for j in range(J):
                    o = bank[6][0:TS, j * P:(j + 1) * P]
                    mm(o, tmp_s[:, j * TS:(j + 1) * TS], ident, start=True, stop=False, skip_group_check=True)
                    for hh in range(2):
                        i = mm(o[:, hh * HD:(hh + 1) * HD], sm[0:TS, hh, 3, j * TS:(j + 1) * TS],
                               tok2[0:TS, 2, j * P + hh * HD:j * P + (hh + 1) * HD], start=False, stop=True,
                               skip_group_check=True)
                TL.done(i, ("r", 2))
                claim(7, (SL, ("u", 2)))
                after(SL, ("r", 2))
                after(VL, "s_x")
                for j in range(J):
                    for hh in range(2):
                        s_ = slice(j * P + hh * HD, j * P + (hh + 1) * HD)
                        i = mm(bank[7][0:TS, s_], sm[0:TS, hh, 2, j * TS:(j + 1) * TS], rm2[0:TS, s_], start=True, stop=True)
                TL.done(i, ("u", 2))
                claim(4, (SL, ("o", 2)))
                after(SL, ("u", 2))
                for j in range(J):
                    for hh in range(2):
                        s_ = slice(j * P + hh * HD, j * P + (hh + 1) * HD)
                        oo = bank[4][hh * HD:(hh + 1) * HD, j * TS:(j + 1) * TS]
                        mm(oo, um2[0:TS, s_], sm[0:TS, hh, 4, j * TS:(j + 1) * TS], start=True, stop=False, skip_group_check=True)
                        mm(oo, tok2[0:TS, 2, s_], sm[0:TS, hh, 5, j * TS:(j + 1) * TS], start=False, stop=False,
                           skip_group_check=True)
                    for b_ in range(DEC_BATCH):
                        col = TP + b_ * DEC_SEQ
                        i = mm(bank[4][:, j * TS + b_ * DEC_SEQ:j * TS + (b_ + 1) * DEC_SEQ],
                               wkv_s[:, j, b_ * P:(b_ + 1) * P], r_p[:, j, col:col + DEC_SEQ], start=False,
                               stop=b_ == DEC_BATCH - 1, skip_group_check=True)
                TL.done(i, "s_o")
                for j in range(J):
                    after(VL, ("s_sel", j))
                    for half in range(2):
                        b = (0, 1, 2, 3, 5, 6)[2 * j + half]
                        claim(b, (VL, ("s_state", j, half)))
                        r_ = slice(half * 4, half * 4 + 4)
                        mm(bank[b][:, :], tok2[0:TS, 0, j * P:(j + 1) * P], usel[0:TS, r_, :], start=True, stop=False)
                        i = mm(bank[b][:, :], tok2[0:TS, 1, j * P:(j + 1) * P], vsel[0:TS, r_, :], start=False, stop=True)
                        TL.done(i, ("s_state", j, half))

                for step in ("mean", "var"):
                    claim(7, (VL, "conv_mean") if step == "mean" else (SL, "conv_std"))
                    after(*((VL, "conv_y") if step == "mean" else (SL, "conv_sq")))
                    for ch in range(2):
                        i = mm(bank[7][:, 0:T], ones, (yc if step == "mean" else yc2)[:, ch, :], start=ch == 0, stop=ch == 1)
                    TL.done(i, ("conv", step))

                for step in ("mu", "var"):
                    for j in range(J):
                        b = (0, 1, 2)[j] if step == "mu" else (3, 5, 6)[j]
                        claim(b, (VL if step == "mu" else SL, ("ln_" + step, j)))
                        after(SL, ("o", 2) if step == "mu" else "ln_sq")
                        i = mm(bank[b][:, 0:T], heads, (oT if step == "mu" else tmp_ln)[:, j, :], start=True, stop=True)
                        TL.done(i, ("ln_" + step, j))

                def scores(u):
                    hh, qt = divmod(u, 2)
                    n = (qt + 1) * P
                    r_ = slice(hh * HD, (hh + 1) * HD)
                    for g in range(G):
                        b = (2 * u) % 4 if qt == 0 or g < 2 else (2 * u) % 4 + 1
                        if g == 0 or (g == 2 and qt == 1):
                            claim(b, (VL, ("masked", u, int(g == 2))))
                        o = g * n if (qt == 0 or g < 2) else 0
                        i = mm(bank[b][:, o:o + n], qkv[r_, g, qt * P:(qt + 1) * P], qkv[r_, G + g, 0:n], start=True, stop=True)
                        if (qt == 1 and g == 1) or g == 2:
                            TL.done(i, ("scores", u, int(g == 2)))

                def apply_probs(u):
                    hh, qt = divmod(u, 2)
                    for kt in range(qt + 1):
                        claim(4 + kt, (SL, ("pT", u, kt)))
                        after(VL, ("probs", u))
                        for g in range(G):
                            i = nc.tensor.transpose(bank[4 + kt][:, g * P:(g + 1) * P],
                                                    sp_[:, u % 2, g * (qt + 1) * P + kt * P:g * (qt + 1) * P + (kt + 1) * P], ident)
                        TL.done(i, ("pT", u, kt))
                    b = 6 + hh
                    claim(b, (SL, ("attn", u)))
                    for g in range(G):
                        for kt in range(qt + 1):
                            after(SL, ("pT", u, kt))
                            i = mm(bank[b][hh * HD:(hh + 1) * HD, g * P:(g + 1) * P], vtok[:, kt, g, hh * HD:(hh + 1) * HD],
                                   spT[:, u % 2, g, kt, :], start=kt == 0, stop=kt == qt)
                    TL.done(i, ("attn", u))

                after(VL, "roped")
                after(VL, "wkv_s")
                for u in range(5):
                    if u < 4:
                        scores(u)
                    if u:
                        apply_probs(u - 1)
                claim(0, (SL, "sT"))
                claim(1, (SL, "sn"))
                after(VL, "qbd")
                q5 = qbd[:, :, :].rearrange("p g (b h t) -> p g b h t", b=DEC_BATCH, h=2)
                for b_ in range(DEC_BATCH):
                    if b_ % 2 == 0:
                        w = arrived(BASE["wink"] + b_ // 2)
                    kc = w[:, (b_ % 2) * 896:(b_ % 2 + 1) * 896]
                    o5 = bank[0][:, 0:G * 64].rearrange("p (g b h t) -> p g b h t", g=G, b=DEC_BATCH, h=2)
                    mm(o5[:, 0, b_], kc[:, 0:P], q5[:, 0, b_], start=True, stop=True)
                    for t in range(DEC_SEQ):
                        mm(o5[:, 1, b_, :, t], kc[:, P * (1 + t):P * (2 + t)], q5[:, 1, b_, :, t], start=True, stop=True)
                    for t in range(2):
                        i = mm(o5[:, 2, b_, :, 2 * t:2 * t + 2], kc[:, P * (5 + t):P * (6 + t)], q5[:, 2, b_, :, 2 * t:2 * t + 2],
                               start=True, stop=True)
                    if b_ % 2:
                        give_back(i)
                TL.done(i, "sT")
                for g in range(G):
                    i = mm(bank[1][0:TS, g * 64:(g + 1) * 64], qkv[:, G + g, TP:T], qbd[:, g, :], start=True, stop=True)
                TL.done(i, "sn")
                claim(2, (VL, "s_scores"))
                after(SL, "sT")
                after(SL, "sn")
                for g in range(G):
                    o = g * (P + TS)
                    nc.tensor.transpose(bank[2][0:64, o:o + P], ssT[:, g, :], ident)
                    i = nc.tensor.transpose(bank[2][0:64, o + P:o + P + TS], ssn[0:TS, g, :], ident[0:TS, 0:TS])
                TL.done(i, "s_scores")
                claim(3, (SL, "psT"))
                claim(4, (SL, "psn"))
                after(VL, "s_probs")
                for g in range(G):
                    o = g * (P + TS)
                    i = nc.tensor.transpose(bank[3][:, g * 64:(g + 1) * 64], ss[0:64, o:o + P], ident[0:64, 0:64])
                TL.done(i, "psT")
                for g in range(G):
                    o = g * (P + TS)
                    i = nc.tensor.transpose(bank[4][0:TS, g * 64:(g + 1) * 64], ss[0:64, o + P:o + P + TS], ident[0:64, 0:64])
                TL.done(i, "psn")
                claim(5, (SL, "s_attn"))
                after(SL, "psT")
                after(SL, "psn")
                for g in range(G):
                    mm(bank[5][:, g * 64:(g + 1) * 64], vtok_s[0:TS, g, :], psn[0:TS, g, :], start=g == 0, stop=False,
                       skip_group_check=True)
                p5 = psT.rearrange("p g (b h t) -> p g b h t", b=DEC_BATCH, h=2)
                o5 = bank[5][:, 0:G * 64].rearrange("p (g b h t) -> p g b h t", g=G, b=DEC_BATCH, h=2)
                for b_ in range(DEC_BATCH):
                    if b_ % 2 == 0:
                        w = arrived(BASE["winv"] + b_ // 2)
                    vc = w[:, (b_ % 2) * 896:(b_ % 2 + 1) * 896]
                    kw = dict(start=False, stop=True, skip_group_check=True)
                    mm(o5[:, 0, b_], vc[:, 0:P], p5[:, 0, b_], **kw)
                    for t in range(DEC_SEQ):
                        mm(o5[:, 1, b_, :, t], vc[:, P * (1 + t):P * (2 + t)], p5[:, 1, b_, :, t], **kw)
                    for t in range(2):
                        i = mm(o5[:, 2, b_, :, 2 * t:2 * t + 2], vc[:, P * (5 + t):P * (6 + t)], p5[:, 2, b_, :, 2 * t:2 * t + 2],
                               **kw)
                    if b_ % 2:
                        give_back(i)
                TL.done(i, "s_attn")

                def mixed(k):
                    if k == 0:
                        return VL, "conv_out"
                    if k == 1:
                        return SL, "s_attn"
                    return VL, "rwkv_out"
                columns("out", BASE["out"], KT, h, mixed, range(7), lambda t: (VL, ("x_out", t)))

                sum_squares("xattn")
                columns("q", BASE["q"], KT, h, lambda k: (VL, ("xattn", "h", k)), range(7), lambda t: (SL, ("qx", t)))
                sum_squares("mem", MEM)
                columns("k", BASE["kv"], KT, hm, lambda k: (VL, ("mem", "h", k)), range(7), lambda t: (SL, ("kx", t)))
                for n in range(4):
                    w = arrived(BASE["kv"] + 4 + n).rearrange("p (k c) -> p k c", k=KT)
                    for mt in range(2):
                        b = (n * 2 + mt) % 7
                        claim(b, (SL, ("vx", n * 2 + mt)))
                        for k in range(KT):
                            i = mm(bank[b][:, 0:256], hm[:, k, mt * P:(mt + 1) * P], w[:, k, :], start=k == 0, stop=k == KT - 1)
                        TL.done(i, ("vx", n * 2 + mt))
                    give_back(i)
                after(SL, ("vx", 7))
                for u in range(8):
                    hd, qt = divmod(u, 2)
                    if qt == 0:
                        claim(hd, (SL, ("xexp", u + 1)))
                    for dt in range(2):
                        i = mm(bank[hd][:, qt * MEM:(qt + 1) * MEM], qx[:, 2 * hd + dt, qt * P:(qt + 1) * P], kx[:, 2 * hd + dt, :],
                               start=dt == 0, stop=dt == 1)
                    TL.done(i, ("xs", u))
                claim(4, (SL, "xsT"))
                for b_ in range(DEC_BATCH):
                    w = arrived(BASE["memk"] + b_).rearrange("p (d m) -> p d m", d=KT)
                    for hd in range(4):
                        for kt in range(2):
                            o = kt * P + b_ * 16 + hd * 4
                            for dt in range(2):
                                i = mm(bank[4][:, o:o + 4], w[:, 2 * hd + dt, kt * P:(kt + 1) * P],
                                       qx[:, 2 * hd + dt, TP + 4 * b_:TP + 4 * b_ + 4], start=dt == 0, stop=dt == 1)
                    give_back(i)
                TL.done(i, "xsT")
                claim(5, (SL, ("xexp", 8)))
                after(SL, "xsT")
                for kt in range(2):
                    i = nc.tensor.transpose(bank[5][:, kt * P:(kt + 1) * P], sxT[:, kt, :], ident)
                TL.done(i, ("xs", 8))
                for u in range(9):
                    b = (6, 7)[u % 2]
                    claim(b, (SL, ("xpT", u)))
                    after(VL, ("xprobs", u))
                    for kt in range(2):
                        i = nc.tensor.transpose(bank[b][:, kt * P:(kt + 1) * P], px[:, u, kt * P:(kt + 1) * P], ident)
                    TL.done(i, ("xpT", u))
                after(SL, ("xpT", 8))
                for dt in range(8):
                    b = (0, 1, 2, 3)[dt // 2]
                    if dt % 2 == 0:
                        claim(b, (SL, ("ox", dt // 2)))
                    for kt in range(2):
                        i = mm(bank[b][:, (dt % 2) * TP:(dt % 2 + 1) * TP], vx[:, kt, dt * P:(dt + 1) * P], pxT[:, dt // 2, kt, :],
                               start=kt == 0, stop=kt == 1)
                    if dt % 2:
                        TL.done(i, ("ox", dt // 2))
                claim(4, (SL, "ox_s"))
                for b_ in range(DEC_BATCH):
                    w = arrived(BASE["memv"] + b_).rearrange("p (k c) -> p k c", k=2)
                    for dt in range(8):
                        for kt in range(2):
                            o = b_ * 16 + (dt // 2) * 4
                            i = mm(bank[4][:, dt * TS + 4 * b_:dt * TS + 4 * b_ + 4], w[:, kt, dt * P:(dt + 1) * P],
                                   pxsT[:, kt, o:o + 4], start=kt == 0, stop=kt == 1)
                    give_back(i)
                TL.done(i, "ox_s")
                columns("o", BASE["o"], KT, ox, lambda k: (SL, "ox_s"), (5, 6, 7, 0, 1, 2, 3), lambda t: (VL, ("x_o", t)))
                ffn("ffn2")
            l = DEPTH - 1
            for k in range(KT):
                after(SL, ("final", "sq", k))
                i = mm(bank[7][:, 0:T], ones, sq[:, k, :], start=k == 0, stop=k == KT - 1)
            TL.done(i, ("final", "ss"))

        @block.scalar
        def _(act):
            act.sem_inc(scalar_done, SL.total)
            act.wait_ge(start_landed, 48)
            fn = nc.scalar.activation

            for l in range(DEPTH):
                SL.begin_layer()
                def after(line, name):
                    act.wait_ge(line.sem, line.value(l, name))

                def copy(out, in_, name=None):
                    return SL.done(nc.scalar.copy(out, in_), name)

                def rms(tag, src, rs_, n, ready):
                    for k in range(KT):
                        ready(k)
                        SL.done(fn(sq[:, k, 0:n], src[:, k, 0:n], ACT.Square), (tag, "sq", k))
                    after(TL, (tag, "ss"))
                    SL.done(fn(rs_[:, 0:n], bank[7][:, 0:n], ACT.Sqrt, bias=NORM_EPS, scale=1.0 / D_MODEL), (tag, "rms"))

                def ffn(tag, ready):
                    rms(tag, x, rs, T, ready)
                    for t in range(FT):
                        after(TL, (tag, "gate", t))
                        if t >= 2:
                            after(VL, (tag, "gated", t - 2))
                        SL.done(fn(th[:, t % 2, :], bank[(t % 2) * 2][:, 0:T], ACT.Tanh, scale=0.5), (tag, "tanh", t))

                ffn("ffn1", lambda k: act.wait_ge(vector_done, VL.value_before(l, ("ffn2", "x", 1))))

                rms("mix", x, rs, T, lambda k: after(VL, ("ffn1", "x", k // 4)))
                for t in range(IN_TILES):
                    b = t % 7
                    if t in (11, 13):
                        continue
                    after(TL, ("in", "cols", t))
                    if t < NC_TILES:
                        copy(f_p[:, t, 1:], bank[b][:, 0:TP])
                        copy(f_s[:, t, :, 1:], bt(bank[b][:, TP:T]), ("in", t))
                    elif t in (12, 14):
                        SL.done(fn(w_i[:, (t - 12) // 2, :], bank[b][:, 0:T], ACT.Tanh, scale=0.5), ("in", t))
                    else:
                        copy(qkv[:, t - 15, :], bank[b][:, 0:T], ("in", t))
                after(VL, ("xs", C_G))
                SL.done(fn(tmp[:, 1, :], xs[:, C_G, :], ACT.Tanh, scale=0.5), "g_tanh")
                SL.done(fn(tmp[0:64, 0, :], xs[0:64, C_LO, :], ACT.Tanh), "lo_tanh")
                after(VL, "halves")
                for kind in range(3):
                    for j in range(J):
                        b = (kind * J + j) % 7
                        after(TL, ("lora", kind, j))
                        if kind == 2:
                            copy(gz[:, j, :], bank[b][:, 0:T], ("lora", kind, j))
                        else:
                            SL.done(fn((ld, aa)[kind][:, j, :], bank[b][:, 0:T], ACT.Tanh, scale=0.5,
                                       bias=halves[:, kind * J + j:kind * J + j + 1]), ("lora", kind, j))
                after(VL, "kk")
                SL.done(fn(tmp, kk, ACT.Square), "kk_sq")
                for j in range(J):
                    after(TL, ("kk_ss", j))
                    SL.done(fn(tmp[:, j, :], bank[j][:, 0:T], ACT.Sqrt), ("kk_norm", j))
                for j in range(J):
                    after(TL, ("bonus", j))
                    copy(bon[:, j, :], bank[3 + j][:, 0:T], ("bonus", j))
                for ct in range(3):
                    after(TL, ("vtok", ct))
                    if ct < 2:
                        copy(vtok[:, ct], bank[ct][:, 0:G * P].rearrange("p (g c) -> p g c", g=G), ("vtok", ct))
                    else:
                        copy(vtok_s[0:TS], bank[ct][0:TS, 0:G * P].rearrange("p (g c) -> p g c", g=G), ("vtok", ct))
                after(VL, "centred")
                SL.done(fn(w_c, cl, ACT.Exp), "w_c")
                SL.done(fn(w_i, cl, ACT.Exp, scale=-1.0), "w_i")
                after(VL, "before")
                SL.done(fn(w_p, ld, ACT.Exp), "w_p")
                SL.done(fn(wmid1, mids[:, :, 1:2], ACT.Exp), "w_mid")
                for ct in range(2):
                    for kind in range(3):
                        after(TL, ("tok", ct, kind))
                        if kind == 0 and ct == 0:
                            after(VL, "primed")
                        copy(tok[:, kind], bank[(2 + kind) % 8][:, 0:J * P], ("tok", ct, kind))
                    for m in range(len(LEVELS)):
                        for hh in range(2):
                            after(TL, ("y", ct, m, hh))
                            copy(ym[:, hh], bank[hh][:, 0:J * P], ("y", ct, m, hh))
                    after(TL, ("r", ct))
                    copy(rm, bank[6][:, 0:J * P], ("r", ct))
                    after(TL, ("u", ct))
                    copy(um, bank[7][:, 0:J * P], ("u", ct))
                    after(TL, ("o_state", ct))
                    copy(oT[:, :, ct * P:(ct + 1) * P], bank[4][:, 0:J * P].rearrange("p (j t) -> p j t", j=J), ("o", ct))
                for kind in range(3):
                    after(TL, ("tok", 2, kind))
                    if kind == 0:
                        act.wait_ge(wkv_landed, 16 * l + 16)
                    copy(tok2[0:TS, kind], bank[2 + kind][0:TS, 0:J * P], ("tok", 2, kind))
                after(TL, "s_r0")
                copy(tmp_s, bank[5][:, 0:J * TS], "s_r0")
                after(TL, "s_y")
                copy(sy[0:TS], bank[0][0:TS, 0:2 * J * TS].rearrange("p (h c) -> p h c", h=2), "s_y")
                after(TL, ("r", 2))
                copy(rm2[0:TS], bank[6][0:TS, 0:J * P], ("r", 2))
                after(TL, ("u", 2))
                copy(um2[0:TS], bank[7][0:TS, 0:J * P], ("u", 2))
                after(TL, "s_o")
                copy(oT[:, :, TP:T], bank[4][:, 0:J * TS].rearrange("p (j t) -> p j t", j=J), ("o", 2))
                after(VL, "conv_mean")
                SL.done(fn(yc2, yc, ACT.Square), "conv_sq")
                after(TL, ("conv", "var"))
                SL.done(fn(yc2[:, 0, :], bank[7][:, 0:T], ACT.Sqrt, bias=CONV_EPS, scale=1.0 / 256), "conv_std")
                after(VL, "conv_norm")
                SL.done(fn(yc2, yc, ACT.Tanh, scale=0.5), "conv_tanh")
                after(VL, ("ln_mu", J - 1))
                SL.done(fn(tmp_ln, oT, ACT.Square), "ln_sq")
                for j in range(J):
                    after(TL, ("ln_var", j))
                    SL.done(fn(tmp_ln[:, j, :], bank[(3, 5, 6)[j]][:, 0:T], ACT.Sqrt, bias=LNX_EPS, scale=1.0 / HD), ("ln_var", j))
                def probs(u):
                    qt = u % 2
                    n = G * (qt + 1) * P
                    after(VL, ("nmax", u))
                    SL.done(fn(sp_[:, qt, 0:n], sp_[:, qt, 0:n], ACT.Exp, scale=ATTN_SCALE, bias=astat[:, 1, u:u + 1],
                               accum_out=astat[:, 2, u:u + 1]), ("exp", u))

                for u in range(5):
                    if u < 4:
                        probs(u)
                    if u:
                        v = u - 1
                        hh, qt = divmod(v, 2)
                        for kt in range(qt + 1):
                            after(TL, ("pT", v, kt))
                            copy(spT[:, v % 2, :, kt, :], bank[4 + kt][:, 0:G * P].rearrange("p (g c) -> p g c", g=G), ("pT", v, kt))
                        after(TL, ("attn", v))
                        r_ = slice(hh * HD, (hh + 1) * HD)
                        copy(h[r_, 2:2 + G, qt * P:(qt + 1) * P], bank[6 + hh][r_, 0:G * P].rearrange("p (g c) -> p g c", g=G),
                             ("attn", v))
                after(TL, "sT")
                copy(ssT, bank[0][:, 0:G * 64].rearrange("p (g c) -> p g c", g=G), "sT")
                after(TL, "sn")
                copy(ssn[0:TS], bank[1][0:TS, 0:G * 64].rearrange("p (g c) -> p g c", g=G), "sn")
                after(VL, ("nmax", 4))
                SL.done(fn(ss[0:64], ss[0:64], ACT.Exp, scale=ATTN_SCALE, bias=astat[0:64, 1, 4:5],
                           accum_out=astat[0:64, 2, 4:5]), ("exp", 4))
                after(TL, "psT")
                copy(psT, bank[3][:, 0:G * 64].rearrange("p (g c) -> p g c", g=G), "psT")
                after(TL, "psn")
                copy(psn[0:TS], bank[4][0:TS, 0:G * 64].rearrange("p (g c) -> p g c", g=G), "psn")
                after(TL, "s_attn")
                for hh in range(2):
                    r_ = slice(hh * HD, (hh + 1) * HD)
                    o4 = bank[5][r_, 0:G * 64].rearrange("p (g b h t) -> p g b h t", g=G, b=DEC_BATCH, h=2)
                    for g in range(G):
                        copy(bt(h[r_, 2 + g, TP:T]), o4[:, g, :, hh, :], "s_attn" if (hh, g) == (1, G - 1) else None)

                rms("xattn", x, rs, T, lambda k: after(VL, ("x_out", k)))
                act.wait_ge(stored, store_value(l, "wkv_s"))
                for t in range(KT):
                    after(TL, ("q", "cols", t))
                    copy(qx[:, t, :], bank[t % 7][:, 0:T], ("qx", t))
                act.wait_ge(mem_landed, 16 * l + 16)
                rms("mem", memx, mem_rs, MEM, lambda k: None)
                for t in range(KT):
                    after(TL, ("k", "cols", t))
                    copy(kx[:, t, :], bank[t % 7][:, 0:MEM], ("kx", t))
                for n in range(8):
                    after(TL, ("vx", n))
                    copy(vx[:, n % 2, (n // 2) * 256:(n // 2 + 1) * 256], bank[n % 7][:, 0:256], ("vx", n))

                def xexp(u):
                    src = bank[u // 2][:, (u % 2) * MEM:(u % 2 + 1) * MEM] if u < 8 else bank[5][:, 0:MEM]
                    after(VL, ("xnmax", u))
                    SL.done(fn(px[:, u, :], src, ACT.Exp, scale=X_SCALE, bias=xstat[:, 1, u:u + 1],
                               accum_out=xstat[:, 2, u:u + 1]), ("xexp", u))

                for u in range(8):
                    xexp(u)
                after(TL, "xsT")
                copy(sxT, bank[4][:, 0:2 * P].rearrange("p (k c) -> p k c", k=2), "xsT")
                xexp(8)
                for u in range(9):
                    after(TL, ("xpT", u))
                    out = pxT[:, u // 2, :, (u % 2) * P:(u % 2 + 1) * P] if u < 8 else pxsT
                    copy(out, bank[6 + u % 2][:, 0:2 * P].rearrange("p (k c) -> p k c", k=2), ("xpT", u))
                for d in range(4):
                    after(TL, ("ox", d))
                    copy(ox[:, 2 * d:2 * d + 2, 0:TP], bank[d][:, :].rearrange("p (a c) -> p a c", a=2), ("ox", d))
                after(TL, "ox_s")
                copy(ox[:, :, TP:T], bank[4][:, 0:KT * TS].rearrange("p (a c) -> p a c", a=KT), "ox_s")

                def ready2(k):
                    after(VL, ("x_o", k))
                    if k == 0:
                        act.wait_ge(stored, store_value(l, "memv"))
                ffn("ffn2", ready2)
            l = DEPTH - 1
            rms("final", x, rs, T, lambda k: after(VL, ("ffn2", "x", k // 4)))

        @block.vector
        def _(dve):
            dve.sem_inc(vector_done, VL.total)
            dve.wait_ge(start_landed, 48)
            tt, ts, stt = nc.vector.tensor_tensor, nc.vector.tensor_scalar, nc.vector.scalar_tensor_tensor
            cp = nc.vector.tensor_copy

            for l in range(DEPTH):
                VL.begin_layer()
                def after(line, name):
                    dve.wait_ge(line.sem, line.value(l, name))

                def settle():
                    dve.wait_ge(vector_done, VL.so_far(l))

                D = VL.done

                def normalise(tag, src, dst, rs_, n):
                    after(SL, (tag, "rms"))
                    D(nc.vector.reciprocal(rs_[:, 0:n], rs_[:, 0:n]))
                    settle()
                    for k in range(KT):
                        D(stt(dst[:, k, 0:n], src[:, k, 0:n], pr(tag, k), rs_[:, 0:n], ALU.mult, ALU.mult), (tag, "h", k))

                def ffn(tag):
                    normalise(tag, x, h, rs, T)
                    for t in range(FT):
                        after(SL, (tag, "tanh", t))
                        D(stt(th2[:, t % 2, :], th[:, t % 2, :], 1.0, bank[(t % 2) * 2][:, 0:T], ALU.add, ALU.mult),
                          (tag, "gated", t))
                        settle()
                        after(TL, (tag, "up", t))
                        D(tt(hid[:, t, :], th2[:, t % 2, :], bank[(t % 2) * 2 + 1][:, 0:T], ALU.mult), (tag, "hid", t))
                    for half in range(2):
                        after(TL, (tag, "down", half))
                        for d in range(4):
                            k = 4 * half + d
                            D(stt(x[:, k, :], bank[4 + d if half == 0 else d][:, 0:T], 0.25, x[:, k, :], ALU.mult, ALU.add),
                              (tag, "x", half) if d == 3 else None)

                D(cp(par[:], par_all[:, l, :]))
                settle()
                ffn("ffn1")

                D(ts(halves, par[:, PAR["w0"]:PAR["w0"] + 2 * J], 0.5, None, ALU.mult), "halves")
                normalise("mix", x, h, rs, T)
                D(nc.vector.memset(f_p[:, :, 0:1], 0.0))
                D(cp(f_s[:, :, :, 0], par[:, PAR["state_shift"]:PAR["state_shift"] + NC_TILES * 8]
                     .rearrange("p (c b) -> p c b", b=DEC_BATCH)))
                D(nc.vector.memset(up[:, :, 0:HIST], 0.0))
                settle()
                for t in range(NC_TILES):
                    after(SL, ("in", t))
                    D(tt(xs[:, t, 0:TP], f_p[:, t, 0:TP], f_p[:, t, 1:], ALU.subtract))
                    D(tt(bt(xs[:, t, TP:T]), f_s[:, t, :, 0:DEC_SEQ], f_s[:, t, :, 1:], ALU.subtract))
                    settle()
                    D(stt(xs[:, t, 0:TP], xs[:, t, 0:TP], pr("shift", t), f_p[:, t, 1:], ALU.mult, ALU.add))
                    D(stt(bt(xs[:, t, TP:T]), bt(xs[:, t, TP:T]), pr("shift", t), f_s[:, t, :, 1:], ALU.mult, ALU.add), ("xs", t))
                D(cp(shift_o[:, :, 0:1], f_p[:, :, TP:TP + 1]))
                D(cp(shift_o[:, :, 1:], f_s[:, :, :, DEC_SEQ]), "shift_out")
                for ch in range(2):
                    after(SL, ("in", 12 + 2 * ch))
                    D(ts(w_i[:, ch, :], w_i[:, ch, :], 0.5, 0.5, ALU.mult, ALU.add))
                    settle()
                    b = 11 + 2 * ch
                    after(TL, ("in", "cols", b))
                    if ch == 0:
                        dve.wait_ge(layer_landed, 16 * l + 16)
                    D(tt(up[:, ch, HIST:], w_i[:, ch, 0:TP], bank[b % 7][:, 0:TP], ALU.mult))
                    D(tt(us4[:, ch, :, HIST:], bt(w_i[:, ch, TP:T]), bt(bank[b % 7][:, TP:T]), ALU.mult), ("glu", ch))
                after(SL, "g_tanh")
                D(ts(xs[:, C_G, :], tmp[:, 1, :], 0.5, 0.5, ALU.mult, ALU.add), "lo_gate")
                for j in range(J):
                    D(ts(kk[:, j, :], xs[:, C_K + j, :], pr("k_k", j), None, ALU.mult), "kk" if j == J - 1 else None)
                for j in range(J):
                    after(SL, ("lora", 0, j))
                D(ts(ld, ld, -HALF_DECAY, -HALF_DECAY, ALU.mult, ALU.add))
                settle()
                fl = lambda a: a.rearrange("p j t -> p (j t)")
                D(nc.vector.tensor_tensor_scan(fl(cl), c("scan", J * T), fl(ld), 0.0, ALU.mult, ALU.add))
                settle()
                for ct in range(2):
                    D(cp(mids[:, :, ct:ct + 1], cl[:, :, ct * P + 63:ct * P + 64]))
                settle()
                for ct in range(2):
                    for j in range(J):
                        D(ts(cl[:, j, ct * P:(ct + 1) * P], cl[:, j, ct * P:(ct + 1) * P], mids[:, j, ct:ct + 1], None, ALU.subtract))
                settle()
                D(cp(tmp2[:, 0:1], mids[:, 0, 0:1]), "centred")
                D(tt(ld, cl, ld, ALU.subtract), "before")
                for j in range(J):
                    after(SL, ("lora", 1, j))
                D(ts(aa, aa, 0.5, 0.5, ALU.mult, ALU.add))
                settle()
                for j in range(J):
                    D(ts(a_p[:, j, :], aa[:, j, :], -1.0, pr("k_a", j), ALU.add, ALU.mult))
                settle()
                D(stt(k2, a_p, 1.0, k2, ALU.add, ALU.mult))
                settle()
                for j in range(J):
                    D(stt(oT[:, j, :], xs[:, C_R + j, :], pr("r_k", j), k2[:, j, :], ALU.mult, ALU.mult), ("rkr", j))
                for i6 in range(2 * G):
                    after(TL, ("turn", i6))
                    D(tt(a_p[:, 0, :], bank[(2 + i6) % 7][:, 0:T], c("sin", T), ALU.mult), ("rope", i6))
                    D(tt(qkv[:, i6, :], qkv[:, i6, :], c("cos", T), ALU.mult))
                    settle()
                    D(tt(qkv[:, i6, :], qkv[:, i6, :], a_p[:, 0, :], ALU.add), "roped" if i6 == 5 else None)
                    settle()
                for j in range(J):
                    after(SL, ("kk_norm", j))
                D(ts(tmp, tmp, 1e-12, None, ALU.max))
                settle()
                D(nc.vector.reciprocal(tmp, tmp))
                settle()
                D(tt(kk, kk, tmp, ALU.mult))
                settle()
                after(SL, "w_p")
                D(stt(a_p, kk, -1.0, w_p, ALU.mult, ALU.mult))
                D(tt(b_p, kk, aa, ALU.mult))
                D(tt(k_p, k2, w_i, ALU.mult))
                D(tt(r_p, xs[:, C_R:C_R + J, :], w_c, ALU.mult))
                settle()
                D(tt(b_p, b_p, w_i, ALU.mult))
                after(SL, "w_mid")
                D(tt(wend[:, :, 0:1], w_c[:, :, P - 1:P], wmid1, ALU.mult))
                D(cp(wend[:, :, 1:2], w_c[:, :, TP - 1:TP]))
                D(cp(wend[:, :, 2:], w_c[:, :, TP + DEC_SEQ - 1:T:DEC_SEQ]))
                settle()
                D(cp(tmp2[:, 0:1], mids[:, 0, 0:1]), "primed")

                def b3(mask, n=J):
                    return mask.unsqueeze(1).to_broadcast([mask.shape[0], n, mask.shape[1]])

                def j3(a):
                    return a.rearrange("p (j s) -> p j s", j=J)

                for ct in range(2):
                    for kind in range(5):
                        for hh in range(2):
                            src = j3(bank[(kind * 2 + hh) % 8][:, 0:J * P])
                            after(TL, ("pair", ct, kind, hh))
                            if kind == 0:
                                D(cp(lab[:, hh], bank[hh][:, 0:J * P]))
                                D(tt(j3(tm[:, hh]), src, b3(c("level1", P)), ALU.mult), ("pair", ct, kind, hh))
                            elif kind == 1:
                                D(tt(j3(xm[:, hh]), src, b3(c("level1", P, at=P)), ALU.mult), ("pair", ct, kind, hh))
                            else:
                                D(tt(j3((lak, lrb, lrk)[kind - 2][:, hh]), src, b3(c("strict" if kind == 2 else "upper", P)), ALU.mult),
                                  ("pair", ct, kind, hh))
                        if kind == 1:
                            settle()
                            for hh in range(2):
                                D(tt(j3(tm[:, hh]), j3(tm[:, hh]), b3(ident), ALU.add), ("t0", ct, hh))
                                D(tt(j3(xm[:, hh]), j3(xm[:, hh]), b3(ident), ALU.add), ("x0", ct, hh))
                    lab6, lo6 = (a.rearrange("p h (j s) -> p (h j) s", j=J) for a in (lab, lo))
                    for m in range(len(LEVELS)):
                        if m:
                            after(TL, ("y", ct, m - 1, 1))
                        D(tt(lo6, lab6, b3(c("levels", P, at=m * P), 2 * J), ALU.mult), ("lo", ct, m))
                        for hh in range(2):
                            after(TL, ("xinc", ct, m, hh))
                            D(tt(xm[:, hh], xm[:, hh], bank[2 + hh][:, 0:J * P], ALU.add), ("x", ct, m, hh))
                            if m < len(LEVELS) - 1:
                                after(TL, ("tinc", ct, m, hh))
                                D(tt(tm[:, hh], tm[:, hh], bank[4 + hh][:, 0:J * P], ALU.add), ("t", ct, m, hh))
                    after(TL, ("o_state", ct))
                    if ct:
                        D(tt(st, st, bank[5][:, 0:J * P], ALU.add))
                        settle()
                    for j in range(J):
                        s_ = slice(j * P, (j + 1) * P)
                        D(stt(st[:, s_], st[:, s_] if ct else bank[5][:, s_], wend[:, j, ct:ct + 1], heads, ALU.mult, ALU.mult),
                          ("state", ct) if j == J - 1 else None)

                dve.wait_ge(wkv_landed, 16 * l + 16)
                sm_mask = c("s_masks", 6 * TS, rows=TS).rearrange("p (k s) -> p k s", k=6)
                i32 = ident[0:TS, 0:TS]
                for hh in range(2):
                    after(TL, ("s_pair", hh))
                    pv = bank[hh][0:TS, 0:5 * J * TS].rearrange("p (k j s) -> p k j s", k=5, j=J)
                    so = sm[0:TS, hh].rearrange("p k (j s) -> p k j s", j=J)
                    D(tt(so[:, 0], pv[:, 0], b3(sm_mask[:, 0]), ALU.mult))
                    D(tt(so[:, 1], pv[:, 0], b3(sm_mask[:, 1]), ALU.mult))
                    D(tt(so[:, 2:6], pv[:, 1:5], sm_mask[:, 2:6].unsqueeze(2).to_broadcast([TS, 4, J, TS]), ALU.mult), ("s_pair", hh))
                    settle()
                    D(tt(so[:, 0], so[:, 0], b3(i32), ALU.add))
                    D(tt(so[:, 2], so[:, 2], b3(i32), ALU.add), ("s_masked", hh))
                settle()
                after(TL, "s_xinc")
                D(tt(sm[0:TS, :, 2], sm[0:TS, :, 2], bank[1][0:TS, 0:2 * J * TS].rearrange("p (h c) -> p h c", h=2), ALU.add), "s_x")
                after(SL, ("u", 2))
                sel = c("s_batch", DEC_BATCH, rows=TS).unsqueeze(2).to_broadcast([TS, DEC_BATCH, P])
                for j in range(J):
                    if j:
                        after(TL, ("s_state", j - 1, 1))
                    s_ = slice(j * P, (j + 1) * P)
                    D(tt(usel[0:TS], b3(um2[0:TS, s_], DEC_BATCH), sel, ALU.mult))
                    D(tt(vsel[0:TS], b3(tok2[0:TS, 2, s_], DEC_BATCH), sel, ALU.mult), ("s_sel", j))
                    for half in range(2):
                        after(TL, ("s_state", j, half))
                        w = wkv_s[:, j, half * 512:(half + 1) * 512]
                        D(tt(w, w, bank[(0, 1, 2, 3, 5, 6)[2 * j + half]][:, :], ALU.add), ("s_state", j, half))
                    settle()
                    w = wkv_s[:, j].rearrange("p (b v) -> p b v", b=DEC_BATCH)
                    D(tt(w, w, wend[:, j, 2:].unsqueeze(2).to_broadcast([P, DEC_BATCH, P]), ALU.mult), "wkv_s" if j == J - 1 else None)
                dve.wait_ge(stored, store_value(l, "wkv_s"))
                after(SL, ("o", 2))

                for tap in range(TAPS):
                    for ch in range(2):
                        w = pr("conv_w", ch * TAPS + tap)
                        win_p, win_s = up[:, ch, tap:tap + TP], us4[:, ch, :, tap:tap + DEC_SEQ]
                        yp, ys = ycv[:, ch, 0:TP], bt(ycv[:, ch, TP:T])
                        if tap == 0:
                            D(ts(yp, win_p, w, pr("conv_b", ch), ALU.mult, ALU.add))
                            D(ts(ys, win_s, w, pr("conv_b", ch), ALU.mult, ALU.add))
                        else:
                            D(stt(yp, win_p, w, yp, ALU.mult, ALU.add))
                            D(stt(ys, win_s, w, ys, ALU.mult, ALU.add))
                    settle()
                D(cp(tmp2[:, 0:1], mids[:, 0, 0:1]), "conv_y")
                after(TL, ("conv", "mean"))
                for ch in range(2):
                    D(stt(ycv[:, ch, :], bank[7][:, 0:T], -1.0 / 256, ycv[:, ch, :], ALU.mult, ALU.add),
                      "conv_mean" if ch else None)
                after(SL, "conv_std")
                D(nc.vector.reciprocal(yc2[:, 0, :], yc2[:, 0, :]))
                settle()
                for ch in range(2):
                    D(tt(ycv[:, ch, :], ycv[:, ch, :], yc2[:, 0, :], ALU.mult))
                settle()
                for ch in range(2):
                    D(ts(ycv[:, ch, :], ycv[:, ch, :], pr("conv_g", ch), pr("conv_beta", ch), ALU.mult, ALU.add),
                      "conv_norm" if ch else None)
                after(SL, "conv_tanh")
                D(ts(yc2, yc2, 0.5, 0.5, ALU.mult, ALU.add))
                settle()
                D(tt(h[:, 0:2, :], yc2, ycv, ALU.mult), "conv_out")
                for j in range(J):
                    after(TL, ("ln_mu", j))
                    D(stt(oT[:, j, :], bank[j][:, 0:T], -1.0 / HD, oT[:, j, :], ALU.mult, ALU.add), ("ln_mu", j))
                for j in range(J):
                    after(SL, ("ln_var", j))
                D(nc.vector.reciprocal(tmp_ln, tmp_ln))
                D(tt(bon, bon, xs[:, C_V:C_V + J, :], ALU.mult))
                settle()
                D(tt(oT, oT, tmp_ln, ALU.mult))
                settle()
                for j in range(J):
                    D(ts(oT[:, j, :], oT[:, j, :], pr("lnx_g", j), pr("lnx_b", j), ALU.mult, ALU.add))
                settle()
                D(tt(oT, oT, bon, ALU.add))
                settle()
                D(tt(h[:, 5:5 + J, :], oT, gz, ALU.mult), "rwkv_out")
                settle()

                D(nc.vector.memset(qbd, 0.0))
                settle()
                q5 = qbd.rearrange("p g (b h t) -> p g b h t", b=DEC_BATCH, h=2)
                for hh in range(2):
                    r_ = slice(hh * HD, (hh + 1) * HD)
                    for g in range(G):
                        D(cp(q5[r_, g, :, hh, :], bt(qkv[r_, g, TP:T])), "qbd" if (hh, g) == (1, G - 1) else None)
                mask = c("mask", 2 * G * TP).rearrange("p (q g k) -> p q g k", q=2, g=G)

                def softmax_in(u, s_, rows=P):
                    settle()
                    D(nc.vector.tensor_reduce(astat[0:rows, 0, u:u + 1], s_, AX_X, ALU.max))
                    settle()
                    D(ts(astat[0:rows, 1, u:u + 1], astat[0:rows, 0, u:u + 1], -ATTN_SCALE, None, ALU.mult), ("nmax", u))

                def softmax_out(u, s_, name, rows=P):
                    after(SL, ("exp", u))
                    D(nc.vector.reciprocal(astat[0:rows, 3, u:u + 1], astat[0:rows, 2, u:u + 1]))
                    settle()
                    D(ts(s_, s_, astat[0:rows, 3, u:u + 1], None, ALU.mult), name)

                def unit(u):
                    qt = u % 2
                    return sp_[:, qt, 0:G * (qt + 1) * P]

                for u in range(4):
                    qt = u % 2
                    b = (2 * u) % 4
                    if u >= 2:
                        after(TL, ("pT", u - 2, (u - 2) % 2))
                    if qt == 0:
                        after(TL, ("scores", u, 1))
                        D(tt(unit(u).rearrange("p (g k) -> p g k", g=G), bank[b][:, 0:G * P].rearrange("p (g k) -> p g k", g=G),
                             mask[:, 0, :, 0:P], ALU.add), ("masked", u, 0))
                    else:
                        after(TL, ("scores", u, 0))
                        D(tt(sp_[:, 1, 0:2 * TP], bank[b][:, :], mask[:, 1, 0:2, :].rearrange("p g k -> p (g k)"), ALU.add),
                          ("masked", u, 0))
                        after(TL, ("scores", u, 1))
                        D(tt(sp_[:, 1, 2 * TP:], bank[b + 1][:, 0:TP], mask[:, 1, 2, :], ALU.add), ("masked", u, 1))
                    softmax_in(u, unit(u))
                    softmax_out(u, unit(u), ("probs", u))
                after(TL, "s_scores")
                D(tt(ss[0:64], bank[2][0:64, 0:G * (P + TS)], c("mask_s", G * (P + TS), rows=64), ALU.add), "s_scores")
                softmax_in(4, ss[0:64], 64)
                softmax_out(4, ss[0:64], "s_probs", 64)

                for t in range(KT):
                    after(TL, ("out", "cols", t))
                    D(tt(x[:, t, :], bank[t % 7][:, 0:T], x[:, t, :], ALU.add), ("x_out", t))

                normalise("xattn", x, h, rs, T)
                dve.wait_ge(mem_landed, 16 * l + 16)
                normalise("mem", memx, hm, mem_rs, MEM)
                for u in range(9):
                    src = bank[u // 2][:, (u % 2) * MEM:(u % 2 + 1) * MEM] if u < 8 else bank[5][:, 0:MEM]
                    after(TL, ("xs", u | 1 if u < 8 else u))
                    D(nc.vector.tensor_reduce(xstat[:, 0, u:u + 1], src, AX_X, ALU.max))
                    settle()
                    D(ts(xstat[:, 1, u:u + 1], xstat[:, 0, u:u + 1], -X_SCALE, None, ALU.mult), ("xnmax", u))
                    after(SL, ("xexp", u))
                    D(nc.vector.reciprocal(xstat[:, 3, u:u + 1], xstat[:, 2, u:u + 1]))
                    settle()
                    D(ts(px[:, u, :], px[:, u, :], xstat[:, 3, u:u + 1], None, ALU.mult), ("xprobs", u))
                for t in range(KT):
                    after(TL, ("o", "cols", t))
                    b = (5, 6, 7, 0, 1, 2, 3)[t % 7]
                    D(tt(x[:, t, :], bank[b][:, 0:T], x[:, t, :], ALU.add), ("x_o", t))
                ffn("ffn2")
            l = DEPTH - 1
            normalise("final", x, h, rs, T)

        return {"t": (TL.at, TL.per_layer()), "v": (VL.at, VL.per_layer()), "s": (SL.at, SL.per_layer()), "stores": stores}


def pack_columns(w):
    n = w.shape[1] // 256
    return w.reshape(KT, P, n, 256).transpose(2, 1, 0, 3).reshape(n, P, SLAB)


def pack_down(w):
    return w.reshape(FT, P, 2, 512).transpose(2, 0, 1, 3).reshape(FT // 2, 4, P, 512).transpose(0, 2, 1, 3).reshape(-1, P, SLAB)


def pack_ffn(i, l, tag):
    gate, up = pack_columns(i[tag + "_w_gate"][l]), pack_columns(i[tag + "_w_up"][l])
    both = np.stack([gate, up], 1).reshape(-1, P, SLAB)
    return np.concatenate([both, pack_down(i[tag + "_w_down"][l])], 0)


def in_order():
    conv, attn, rwkv = 0, 512, 512 + 1152
    starts = [rwkv + 1152, rwkv + 1280] + [rwkv + 384 + P * j for j in range(J)] + [rwkv + P * j for j in range(J)]
    starts += [rwkv + 768 + P * j for j in range(J)] + [conv, conv + 256, conv + 128, conv + 384]
    starts += [attn + P * j for j in range(9)]
    return np.concatenate([np.arange(s, s + P) for s in starts])


def pad(a):
    return np.concatenate([a, np.zeros(a.shape[:-1] + (SLAB - a.shape[-1],), a.dtype)], -1)


def pack_layer(i, l):
    k, v = ([i[f"cache_win{g}_{n}"][l] for g in (1, 2, 3)] for n in "kv")
    B = DEC_BATCH

    def phases(a, dil):
        return a.reshape(B, a.shape[1] // dil, dil, 2, HD).transpose(0, 2, 1, 3, 4)[:, :4]
    kc = np.concatenate([a.reshape(B, -1, P) for a in (k[0], phases(k[1], 4), phases(k[2], 16))], 1)
    vc = np.concatenate([a.reshape(B, -1, P) for a in (v[0], phases(v[1], 4), phases(v[2], 16))], 1)
    kc = kc.transpose(0, 2, 1).reshape(B // 2, 2, P, 896).transpose(0, 2, 1, 3).reshape(B // 2, P, 1792)
    vc = vc.reshape(B // 2, 2, 7, P, P).transpose(0, 3, 1, 2, 4).reshape(B // 2, P, 1792)
    memk = i["cache_mem_k"][l].reshape(B, MEM, KT, P).transpose(0, 3, 2, 1).reshape(B, P, SLAB)
    memv = i["cache_mem_v"][l].reshape(B, 2, P, D_MODEL).transpose(0, 2, 1, 3).reshape(B, P, SLAB)
    parts = {"ffn1": pack_ffn(i, l, "ffn1"), "in": pack_columns(i["w_in"][l][:, in_order()]), "wink": pad(kc), "winv": pad(vc),
             "out": pack_columns(i["w_out"][l]), "q": pack_columns(i["xattn_w_q"][l]), "kv": pack_columns(i["xattn_w_kv"][l]),
             "memk": memk, "memv": memv, "o": pack_columns(i["xattn_w_o"][l]), "ffn2": pack_ffn(i, l, "ffn2")}
    return np.concatenate([parts[name] for name, _ in STAGES], 0)


def pack_small(i, l):
    c0 = in_order()[:NC_TILES * P] - 1664

    def cols(v):
        return v.reshape(-1, P).T
    lora = np.concatenate([np.concatenate([i["rwkv_w_up"][l], i["rwkv_a_up"][l]], 0), i["rwkv_g_up"][l]], 1)
    parts = [cols(i["ffn1_norm"][l]), cols(i["mix_norm"][l]), cols(i["xattn_norm"][l]), cols(i["mem_norm"][l]),
             cols(i["ffn2_norm"][l]), cols(i["final_norm"]), i["conv_w"][l].reshape(TAPS, 2, P).transpose(2, 1, 0).reshape(P, -1),
             cols(i["conv_b"][l]), cols(i["conv_ln_g"][l]), cols(i["conv_ln_b"][l]), cols(i["rwkv_shift_mix"][l][c0]),
             cols(i["rwkv_w0"][l]), cols(i["rwkv_a0"][l]), cols(i["rwkv_k_k"][l]), cols(i["rwkv_k_a"][l]),
             cols(i["rwkv_r_k"][l].reshape(-1)), cols(i["rwkv_lnx_g"][l]), cols(i["rwkv_lnx_b"][l]),
             i["state_shift"][l][:, c0].reshape(DEC_BATCH, NC_TILES, P).transpose(2, 1, 0).reshape(P, -1), lora]
    return np.concatenate(parts, 1)


def tokens(xp, xs_):
    both = np.concatenate([xp.reshape(TP, D_MODEL), xs_.reshape(TS, D_MODEL)], 0)
    return both.T.reshape(KT, P, T).transpose(1, 0, 2)


def pack(inputs):
    i = {k: np.asarray(v) for k, v in inputs.items()}
    wkv = np.zeros((DEPTH, J, 2, HD, DEC_BATCH, 2, HD), np.float32)
    s = i["state_wkv"].reshape(DEPTH, DEC_BATCH, J, 2, HD, HD)
    for hh in range(2):
        wkv[:, :, hh, :, :, hh, :] = s[:, :, :, hh].transpose(0, 2, 4, 1, 3)
    arrays = {
        "x_in": tokens(i["x_prompt"], i["x_sample"]),
        "mem_in": i["mem_prompt"].reshape(MEM, KT, P).transpose(2, 1, 0),
        "stream": np.stack([pack_layer(i, l) for l in range(DEPTH)]),
        "small": np.stack([pack_small(i, l) for l in range(DEPTH)], 1),
        "consts": constants(),
        "conv_hist": i["cache_conv"].reshape(DEPTH, DEC_BATCH, HIST, 2, P).transpose(0, 4, 3, 1, 2),
        "wkv_in": wkv.reshape(DEPTH, J, P, DEC_BATCH * P).transpose(0, 2, 1, 3),
    }
    for g in (1, 2, 3):
        for n in "kv":
            arrays[f"win{g}{n}"] = i[f"cache_win{g}_{n}"].reshape(DEPTH, DEC_BATCH, -1)
    return {k: np.ascontiguousarray(v) for k, v in arrays.items()}


SHAPES_OUT = {
    "y": (P, KT, T), "conv": (DEPTH, P, 2, HIST + DEC_BATCH * HIST), "kv": (DEPTH, P, 2 * G, T),
    "shift": (DEPTH, P, NC_TILES, 1 + DEC_BATCH), "wkv_p": (DEPTH, P, J * P), "wkv_s": (DEPTH, P, J, DEC_BATCH * P),
    "memk": (DEPTH, P, KT, MEM), "memv": (DEPTH, P, 2, D_MODEL),
}


def build(nc, arrays, known):
    ap = {k: nc.dram_tensor(k, a.shape, F32, kind="ExternalInput").ap() for k, a in arrays.items()}
    outs = {k: nc.dram_tensor("out_" + k, s, F32, kind="ExternalOutput").ap() for k, s in SHAPES_OUT.items()}
    copies = []
    for g in (1, 2, 3):
        for n in "kv":
            size = (CACHED[g - 1] - DEC_SEQ) * P
            dst = nc.dram_tensor(f"out_win{g}{n}", (DEPTH, DEC_BATCH, size), F32, kind="ExternalOutput").ap()
            copies.append((ap[f"win{g}{n}"][:, :, DEC_SEQ * P:], dst))
    return program(nc, ap["x_in"], ap["mem_in"], ap["stream"], ap["small"], ap["consts"], ap["conv_hist"], ap["wkv_in"],
                   copies, tuple(outs.values()), known)


def unpack(r):
    B, L = DEC_BATCH, DEPTH
    y = r["out_y"].transpose(2, 1, 0).reshape(T, D_MODEL)
    conv = r["out_conv"].transpose(0, 3, 2, 1).reshape(L, HIST + B * HIST, 256)
    kv = r["out_kv"].reshape(L, 2, HD, 2, G, T).transpose(3, 4, 0, 5, 1, 2)
    shift = r["out_shift"].transpose(0, 3, 2, 1).reshape(L, 1 + B, NC_TILES * P)
    c0 = in_order()[:NC_TILES * P] - 1664
    shift_ref = np.empty_like(shift)
    shift_ref[:, :, c0] = shift

    def states(a):
        n = a.shape[3]
        a = a.reshape(L, 2, HD, J, n, 2, HD)
        a = np.stack([a[:, hh, :, :, :, hh] for hh in range(2)], 1)
        return a.transpose(0, 4, 3, 1, 5, 2).reshape(L, n, 2 * J, HD, HD)
    wins_p, wins_s = [], []
    for g in range(G):
        for n in range(2):
            new = kv[n, g]
            keep = min(GROUPS[g][0], TP)
            wins_p.append(new[:, None, TP - keep:TP])
            old = r[f"out_win{g + 1}{'kv'[n]}"].reshape(L, B, -1, 2, HD)
            wins_s.append(np.concatenate([old, new[:, TP:].reshape(L, B, DEC_SEQ, 2, HD)], 2))
    memk = r["out_memk"].transpose(0, 3, 2, 1).reshape(L, 1, MEM, 4, 256)
    memv = r["out_memv"].transpose(0, 2, 1, 3).reshape(L, 1, MEM, 4, 256)
    out = (y[:TP].reshape(1, TP, D_MODEL), y[TP:].reshape(B, DEC_SEQ, D_MODEL), conv[:, None, :HIST], *wins_p,
           shift_ref[:, :1], states(r["out_wkv_p"].reshape(L, P, J, 1, P)), memk, memv,
           conv[:, HIST:].reshape(L, B, HIST, 256), *wins_s, shift_ref[:, 1:],
           states(r["out_wkv_s"].reshape(L, P, J, B, P)))
    return tuple(np.ascontiguousarray(a) for a in out)


def kernel(**inputs):
    import concourse.bacc as bacc
    from concourse.bass_utils import run_bass_kernel_spmd

    arrays = pack(inputs)
    known = build(bacc.Bacc("TRN2", target_bir_lowering=False, num_devices=1), arrays, None)
    nc = bacc.Bacc("TRN2", target_bir_lowering=False, num_devices=1)
    build(nc, arrays, known)
    r = run_bass_kernel_spmd(nc, [arrays], core_ids=[0])
    return unpack(r.results[0])
```

```python
from contextlib import ExitStack

import numpy as np

import concourse.bass as bass
from concourse import mybir

F32 = mybir.dt.float32
F32R = mybir.dt.float32r
ALU = mybir.AluOpType
ACT = mybir.ActivationFunctionType
AX_X = mybir.AxisListType.X

P = 128
DEPTH, D_MODEL, D_FF = 2, 1024, 2816
TP, DEC_BATCH, DEC_SEQ = 256, 8, 4
TS = DEC_BATCH * DEC_SEQ
T = TP + TS
PAST_LEN = 1024
MEM = 256
KT = D_MODEL // P
FT = D_FF // P
HD = 64
TAPS = 31
HIST = TAPS - 1
GROUPS = ((128, 1), (512, 4), (2048, 16))
G = len(GROUPS)
CACHED = tuple(min(w, PAST_LEN) for w, _ in GROUPS)
ATTN_SCALE, X_SCALE = HD ** -0.5, 256 ** -0.5
NORM_EPS, CONV_EPS, LNX_EPS = 1e-6, 1e-5, 64e-5
HALF_DECAY = 0.5 * float(np.exp(-0.5))
NEG = -1e30
J = 3
LEVELS = (2, 4, 8, 16, 32, 64)

K_BANKS = (0, 1, 2, 3, 6, 7)
V_BANKS = (6, 7, 6, 7, 0, 1, 2, 3)
IN_CUT = (18, 20)
C_LO, C_G, C_K, C_R, C_V = 0, 1, 2, 5, 8
NC_TILES = 11
IN_TILES = 24

SLAB = 2048
NSLOT = 4
MEMK_EARLY = 6
STAGES = (("ffn1", 33), ("in", 12), ("wink", 4), ("winv", 4), ("out", 4), ("q", 4), ("kv", 8),
          ("memk", 8), ("memv", 8), ("o", 4), ("ffn2", 33))
UNIT = SLAB // 2
NW = 3
CACHES = ("wink", "winv", "memk", "memv")
ORDER = [(_name, _i) for _name, _n in STAGES for _i in range(_n)]
for _i in range(MEMK_EARLY):
    ORDER.remove(("memk", _i))
    ORDER.insert(ORDER.index(("kv", _i + 1)) + 1, ("memk", _i))
SLAB_AT = {key: n for n, key in enumerate(ORDER)}
NSLAB = len(ORDER)
UNITS, NUNIT, UNIT_OF_SLAB = {}, 0, {}
for _n, (_name, _i) in enumerate(ORDER):
    if _name not in CACHES:
        UNITS.setdefault(_name, NUNIT)
        UNIT_OF_SLAB[_n] = NUNIT
        NUNIT += 2
SLAB_OF_UNIT = {u + half: (n, half) for n, u in UNIT_OF_SLAB.items() for half in range(2)}
RUN_ENDS = (UNITS["out"], UNITS["o"], NUNIT)
ROUNDS = NSLAB // NSLOT
REST = NSLAB - ROUNDS * NSLOT
ARENA = 23910
NSTORE = 9

PAR, NPAR = {}, 0
for _name, _n in (("ffn1", 8), ("mix", 8), ("xattn", 8), ("mem", 8), ("ffn2", 8), ("final", 8), ("conv_w", 2 * TAPS),
                  ("conv_b", 2), ("conv_g", 2), ("conv_beta", 2), ("shift", NC_TILES), ("w0", J), ("a0", J),
                  ("k_k", J), ("k_a", J), ("r_k", J), ("lnx_g", J), ("lnx_b", J), ("state_shift", NC_TILES * 8),
                  ("lora", 2 * J * P)):
    PAR[_name] = NPAR
    NPAR += _n

CON, NCON = {}, 0
for _name, _n in (("ident", P), ("ones", P), ("heads", P), ("turn", P), ("cos", T), ("sin", T), ("mask", 2 * G * TP),
                  ("mask_s", G * (P + TS)), ("level1", 2 * P), ("levels", len(LEVELS) * P), ("strict", P), ("upper", P),
                  ("s_masks", 6 * TS), ("s_batch", DEC_BATCH), ("scan", J * T)):
    CON[_name] = NCON
    NCON += _n


def constants():
    c = np.zeros((P, NCON), np.float32)

    def put(name, a, rows=P):
        a = np.asarray(a, np.float32).reshape(rows, -1)
        c[:rows, CON[name]:CON[name] + a.shape[1]] = a

    i = np.arange(P)
    put("ident", np.eye(P))
    put("ones", np.ones((P, P)))
    put("heads", i[:, None] // HD == i[None] // HD)
    turn = np.zeros((P, P))
    for m in range(P):
        turn[m + 32 if m % HD < 32 else m - 32, m] = -1.0 if m % HD < 32 else 1.0
    put("turn", turn)
    half = HD // 2
    inv = np.power(np.float32(10000.0), -np.arange(half, dtype=np.float32) / np.float32(half)).astype(np.float32)
    pos = np.concatenate([np.arange(TP), np.tile(PAST_LEN + np.arange(DEC_SEQ), DEC_BATCH)]).astype(np.float32)
    ang = (inv[i % half][:, None] * pos[None]).astype(np.float32)
    put("cos", np.cos(ang))
    put("sin", np.sin(ang))
    mask = np.full((P, 2, G, TP), NEG)
    for qt in range(2):
        q = qt * P + i[:, None]
        k = np.arange(TP)[None]
        for g, (win, dil) in enumerate(GROUPS):
            mask[:, qt, g][(q >= k) & (q - k <= win) & ((q - k) % dil == 0)] = 0
    put("mask", mask)
    ms = np.full((DEC_BATCH, 2, DEC_SEQ, G, P + TS), NEG)
    key = np.arange(P)
    for b in range(DEC_BATCH):
        for t in range(DEC_SEQ):
            ms[b, :, t, 0, :P][:, key >= t] = 0
            ms[b, :, t, 1, :P] = 0
            ms[b, :, t, 2, :P][:, key // 64 == t % 2] = 0
            ms[b, :, t, 0, P + DEC_SEQ * b:P + DEC_SEQ * b + t + 1] = 0
            ms[b, :, t, 1:, P + DEC_SEQ * b + t] = 0
    put("mask_s", ms, rows=64)
    t, s = i[:, None], i[None]

    def level(m):
        return (t // (2 * m) == s // (2 * m)) & (t % (2 * m) >= m) & (s % (2 * m) < m)

    put("level1", np.concatenate([level(1), level(1).T], 1))
    put("levels", np.concatenate([level(m) for m in LEVELS], 1))
    put("strict", (t < s))
    put("upper", (t <= s))
    same = (t // DEC_SEQ == s // DEC_SEQ)
    small = [level(1), level(2), level(1).T, same & (t < s), same & (t <= s), same & (t <= s)]
    put("s_masks", np.concatenate([m[:TS, :TS] for m in small], 1), rows=TS)
    put("s_batch", i[:TS, None] // DEC_SEQ == np.arange(DEC_BATCH)[None], rows=TS)
    keep = np.ones((P, J, T))
    keep[:, :, 0:TP:P] = 0
    keep[:, :, TP::DEC_SEQ] = 0
    put("scan", keep)
    return c


class Line:

    def __init__(self, sem, known):
        self.sem, self.n, self.at, self.last = sem, 0, {}, None
        self.known, self.total = known if known else ({}, 1)

    def done(self, ins, name=None):
        if ins is not self.last:
            self.n += 1
            ins.then_inc(self.sem, 1)
            self.last = ins
        if name is not None:
            assert self.at.setdefault(name, self.n) == self.n, name
        return ins

    def begin_layer(self):
        self.n = 0

    def per_layer(self):
        return max((c for name, c in self.at.items() if name[0] != "final"), default=0)

    def value(self, l, name):
        return l * self.total + (self.total + (self.known.get(name, 1) if self.known else 1))

    def value_before(self, l, name):
        return l * self.total + (self.known.get(name, 1) if self.known else 1)

    def so_far(self, l):
        return l * self.total + (self.total + self.n)


def program(nc, x_in, mem_in, stream, small, consts, conv_hist, wkv_in, copies, outs, known=None):
    (y_out, conv_out, kv_out, shift_out, wkv_p_out, wkv_s_out, memk_out, memv_out) = outs
    known = known or {}
    with ExitStack() as ctx:
        def sb(name, shape):
            return ctx.enter_context(nc.sbuf_tensor(name, shape, F32))

        def sem(name):
            return ctx.enter_context(nc.semaphore(name))

        bank = [ctx.enter_context(nc.psum_tensor(f"bank{i}", [P, 512], F32)) for i in range(8)]

        slots = sb("slots", [P, NSLOT, SLAB])
        x = sb("x", [P, KT, T])

        def split_at(name, shape, offset):
            return nc.alloc_sbuf_tensor_at(name, shape, F32R, offset=offset)

        h_mem = sb("h_mem", [P, 2, KT, T])
        h_at = nc.sbuf_base - 2 * KT * T * 4
        h, h_free = h_mem[:, 0], h_mem[:, 1]
        h_lo, h_hi = split_at("h_lo", [P, KT, T], h_at), split_at("h_hi", [P, KT, T], h_at + KT * T * 4)
        w_hi = ctx.enter_context(nc.sbuf_tensor("w_hi", [P, NW, UNIT], F32R))
        w_lo = ctx.enter_context(nc.sbuf_tensor("w_lo", [P, NW, UNIT], F32R))
        par_all = sb("par_all", [P, DEPTH, NPAR])
        con = sb("con", [P, NCON])
        rs = sb("rs", [P, T])
        halves = sb("halves", [P, 2 * J])[:]
        warm = sb("warm", [P, 1])[:]
        mem_rs = sb("mem_rs", [P, MEM])
        arena = sb("arena", [P, ARENA])
        arena_at = nc.sbuf_base - ARENA * 4

        def c(name, n, rows=P, at=0):
            return con[0:rows, CON[name] + at:CON[name] + at + n]

        ident, ones, heads = c("ident", P), c("ones", P), c("heads", P)

        top = [0]

        def take(*dims):
            n = int(np.prod(dims))
            v = arena[:, top[0]:top[0] + n]
            top[0] += n
            assert top[0] <= ARENA, top[0]
            if len(dims) == 1:
                return v
            names = "abcd"[:len(dims)]
            return v.rearrange(f"p ({' '.join(names)}) -> p {' '.join(names)}",
                               **{k: d for k, d in zip(names[1:], dims[1:])})

        def over(name, view_start, *dims):
            return split_at(name, [P, *dims], arena_at + view_start * 4)

        sq = take(KT, T)
        hid_hi = over("hid_hi", top[0], FT, T)
        top[0] += FT * T
        hid_lo = over("hid_lo", top[0], FT, T)
        hid = take(FT, T)
        th = take(2, T)
        th2 = take(2, T)
        top[0] = KT * T
        qx = take(KT, T)
        ox_hi, hm_hi = over("ox_hi", top[0], KT, T), over("hm_hi", top[0], KT, MEM)
        top[0] += KT * T
        ox_lo, hm_lo = over("ox_lo", top[0], KT, T), over("hm_lo", top[0], KT, MEM)
        hm = take(KT * T)[:, 0:KT * MEM].rearrange("p (a b) -> p a b", a=KT)
        kx = take(KT, MEM)
        vx = take(2, 4 * MEM)
        pxT = take(4, 2, TP)
        memx = pxT.rearrange("p a b c -> p (a b) c")
        px = take(10, MEM)
        qz = take(KT, DEC_BATCH, 32)
        pxsT = take(2, 2, P)
        oxs = take(2, D_MODEL)
        xstat = take(4, 10)
        top[0] = 0
        xs = take(NC_TILES, T)
        qkv = take(3 * G, T)
        up = take(2, HIST + TP)
        us = take(2, DEC_BATCH * (HIST + DEC_SEQ))
        a_p, b_p, k_p, r_p = (take(J, T) for _ in range(4))
        gz, oT = (take(J, T) for _ in range(2))
        turned, bon = h_free[:, 0:J, :], h_free[:, J:2 * J, :]
        wend = take(J, 2 + DEC_BATCH)
        wmid1 = take(J, 1)
        mids = take(J, 2)
        shift_o = take(NC_TILES, 1 + DEC_BATCH)
        base2 = top[0]
        f = take(NC_TILES, 1 + TP + DEC_BATCH * (1 + DEC_SEQ))
        wid = 1 + TP + DEC_BATCH * (1 + DEC_SEQ)
        ld, cl, w_c, w_p, w_i = (take(J, T) for _ in range(5))
        aa, kk = (take(J, T) for _ in range(2))
        k2 = xs[:, C_K:C_K + J, :]
        top[0] = base2
        tmp = take(J, T)
        top[0] = base2
        lab, tm, xm, lo, ym, lak, lrb, lrk = (take(2, J * P) for _ in range(8))
        rm, um, st = (take(J * P) for _ in range(3))
        tok = take(3, J * P)
        wkv_s = take(J, DEC_BATCH, HD)
        ycv, prod = take(2, T), take(2, 2, T)
        top[0] = base2
        usel, vsel = take(DEC_BATCH, P), take(DEC_BATCH, P)
        sm = take(2, 6, J * TS)
        sy = take(2, J * TS)
        tmp_s, rm2, um2 = take(J * TS), take(J * P), take(J * P)
        tok2 = take(3, J * P)
        tmp_ln = take(J, T)
        yc2 = take(2, T)
        assert top[0] <= base2 + 18 * J * P
        top[0] = base2
        vtok = take(2, G, P)
        vtok_s = take(G, P)
        sp_ = take(2, G * TP)
        spT = take(2, G, 2, P)
        qbd = take(G, 64)
        ss = take(G * (P + TS))
        ssT, ssn = take(G, 64), take(G, 64)
        psT, psn = take(G, 64), take(G, 64)
        astat = take(4, 6)
        assert top[0] <= base2 + 18 * J * P

        us4 = us.rearrange("p a (b t) -> p a b t", b=DEC_BATCH)
        f_p = f[:, :, 0:1 + TP]
        f_s = f[:, :, 1 + TP:].rearrange("p c (b t) -> p c b t", b=DEC_BATCH)

        def bt(ap):
            return ap.rearrange("p (b t) -> p b t", t=DEC_SEQ)

        tensor_done, vector_done, scalar_done = sem("tensor_done"), sem("vector_done"), sem("scalar_done")
        pool_done = sem("pool_done")
        slab_landed = [sem(f"slab_landed{i}") for i in range(NSLOT)]
        start_landed = sem("start_landed")
        con_landed = sem("con_landed")
        layer_landed = sem("layer_landed")
        wkv_landed = sem("wkv_landed")
        mem_landed = sem("mem_landed")
        stored = sem("stored")
        copied = sem("copied")
        TL, VL, SL, PL = (Line(s, known.get(n)) for s, n in ((tensor_done, "t"), (vector_done, "v"), (scalar_done, "s"),
                                                             (pool_done, "p")))
        store_known = known.get("stores", {})
        stores = {}

        block = ctx.enter_context(nc.Block())

        @block.sync
        def _(sp):
            sp.dma_start(x[:], x_in).then_inc(start_landed, 16)
            sp.dma_start(par_all[:], small).then_inc(start_landed, 16)
            first = CON["turn"]
            sp.dma_start(con[:, 0:first], consts[:, 0:first]).then_inc(start_landed, 16)
            flat = stream.rearrange("l n p c -> (l n) p c")
            for l in range(DEPTH):
                for n in range(NSLAB):
                    held = n - NSLOT if n >= NSLOT else n + NSLOT * (ROUNDS - (n >= REST))
                    line, name = (VL, ("lo", UNIT_OF_SLAB[held] + 1)) if held in UNIT_OF_SLAB else (TL, ("slab", held))
                    sp.wait_ge(line.sem, line.value(l, name) if n >= NSLOT else line.value_before(l, name))
                    sp.dma_start(slots[:, n % NSLOT, :], stream[l, n]).then_inc(slab_landed[n % NSLOT], 16)
                    if l == 0 and n == NSLOT + 4:
                        sp.dma_start(con[:, first:], consts[:, first:]).then_inc(con_landed, 16)
                    if n % 5 == 4 and n // 5 < len(copies):
                        src, dst = copies[n // 5]
                        sp.dma_start(dst[l], src[l]).then_inc(copied, 16)
            sp.wait_ge(copied, 16 * 6 * DEPTH)

        @block.gpsimd
        def _(pool):
            n_stores = [0]

            def store(dst, src, name):
                pool.dma_start(dst, src).then_inc(stored, 16)
                n_stores[0] += 1
                stores[name] = n_stores[0]

            pool.sem_inc(pool_done, PL.total)
            pool.wait_ge(start_landed, 48)
            for l in range(DEPTH):
                n_stores[0] = 0
                PL.begin_layer()
                pool.wait_ge(vector_done, VL.value(l, ("ffn1", "x", 1)))
                pool.wait_ge(tensor_done, TL.value(l, ("ffn1", "down", 1)))
                pool.dma_start(us4[:, :, :, 0:HIST], conv_hist[l]).then_inc(layer_landed, 16)

                pool.wait_ge(vector_done, VL.value(l, ("glu", 1)))
                par = par_all[:, l, :]

                def products(tap):
                    for ch in range(2):
                        w = par[:, PAR["conv_w"] + ch * TAPS + tap:PAR["conv_w"] + ch * TAPS + tap + 1]
                        bias = par[:, PAR["conv_b"] + ch:PAR["conv_b"] + ch + 1]
                        out = prod[:, tap % 2, ch, :] if tap else ycv[:, ch, :]
                        for o, i in ((out[:, 0:TP], up[:, ch, tap:tap + TP]), (bt(out[:, TP:T]), us4[:, ch, :, tap:tap + DEC_SEQ])):
                            if tap:
                                p_ = nc.gpsimd.tensor_scalar(o, i, w, None, ALU.mult)
                            else:
                                p_ = nc.gpsimd.tensor_scalar(o, i, w, bias, ALU.mult, ALU.add)
                            PL.done(p_)
                    PL.done(p_, ("products", tap))

                products(0)
                products(1)
                for tap in range(1, TAPS):
                    if tap + 1 < TAPS:
                        if tap > 1:
                            pool.wait_ge(pool_done, PL.value(l, ("summed", tap - 1)))
                        products(tap + 1)
                    pool.wait_ge(pool_done, PL.value(l, ("products", tap)))
                    if tap > 1:
                        pool.wait_ge(pool_done, PL.value(l, ("summed", tap - 1)))
                    PL.done(nc.gpsimd.tensor_tensor(ycv, ycv, prod[:, tap % 2], ALU.add), ("summed", tap))

                store(conv_out[l, :, :, 0:HIST], up[:, :, TP:TP + HIST], "conv_p")
                store(conv_out[l, :, :, HIST:].rearrange("p a (b t) -> p a b t", b=DEC_BATCH)[:, 0],
                      us4[:, 0, :, DEC_SEQ:], "conv_s0")
                store(conv_out[l, :, :, HIST:].rearrange("p a (b t) -> p a b t", b=DEC_BATCH)[:, 1],
                      us4[:, 1, :, DEC_SEQ:], "conv_s1")
                store(shift_out[l], shift_o, "shift")
                pool.wait_ge(vector_done, VL.value(l, "roped"))
                pool.wait_ge(scalar_done, SL.value(l, ("in", IN_TILES - 1)))
                store(kv_out[l], qkv[:, G:3 * G, :], "kv")
                pool.wait_ge(vector_done, VL.value(l, ("state", 1)))
                store(wkv_p_out[l], st, "wkv_p")
                pool.wait_ge(vector_done, VL.value(l, "wkv_s"))
                store(wkv_s_out[l], wkv_s, "wkv_s")
                pool.wait_ge(vector_done, VL.value(l, ("x_out", KT - 1)))
                pool.wait_ge(stored, l * (16 * NSTORE) + 16 * n_stores[0])
                pool.dma_start(memx, mem_in).then_inc(mem_landed, 16)
                pool.wait_ge(scalar_done, SL.value(l, ("kx", KT - 1)))
                store(memk_out[l], kx, "memk")
                pool.wait_ge(scalar_done, SL.value(l, ("vx", 7)))
                store(memv_out[l], vx, "memv")
            assert n_stores[0] == NSTORE
            pool.wait_ge(vector_done, VL.value(DEPTH - 1, ("final", "h", KT - 1)))
            pool.dma_start(y_out, h[:]).then_inc(stored, 16)
            pool.wait_ge(stored, 16 * (NSTORE * DEPTH + 1))

        def landed(l, n):
            s = n % NSLOT
            per = ROUNDS + (s < REST)
            return slab_landed[s], l * (16 * per) + 16 * (n // NSLOT + 1)

        def raw_unit(u):
            n, half = SLAB_OF_UNIT[u]
            return slots[:, n % NSLOT, half * UNIT:(half + 1) * UNIT]

        def next_unit(u):
            return u + NW if all(not u < end <= u + NW for end in RUN_ENDS) else None

        def unit_head(u):
            return u // 2 if u < 8 else u - 4

        def sample_out(a, half, hd):
            o = TP + half * TS // 2
            return a[:, 2 * hd:2 * hd + 2, o:o + TS // 2].rearrange("p a (b t) -> p a b t", t=DEC_SEQ)

        def head_columns(half, hd):
            a = bank[2 * half + hd // 2][:, (hd % 2) * 2 * P:(hd % 2 + 1) * 2 * P]
            return a.rearrange("p (a b c) -> p a b c", a=2, b=4)[:, :, :, 4 * hd:4 * hd + 4]

        def reached(l, line, name):
            return line.sem, line.value(l, name)

        def store_value(l, name):
            return l * (16 * NSTORE) + 16 * store_known.get(name, 1)

        @block.tensor
        def _(pe):
            pe.sem_inc(tensor_done, TL.total)
            pe.wait_ge(start_landed, 48)
            mm = nc.tensor.matmul
            for l in range(DEPTH):
                TL.begin_layer()
                free = [None] * 8

                def claim(b, released_by):
                    if free[b] is not None:
                        pe.wait_ge(*reached(l, *free[b]))
                    free[b] = released_by

                def arrived(n):
                    pe.wait_ge(*landed(l, n))
                    return slots[:, n % NSLOT, :]

                def split(u, k):
                    pe.wait_ge(vector_done, VL.value(l, ("lo", u)))
                    return tuple(w[:, u % NW, :].rearrange("p (k c) -> p k c", k=k) for w in (w_hi, w_lo))

                def mm3(out, lhs, rhs, start, stop):
                    mm(out, lhs[0], rhs[0], start=start, stop=False)
                    mm(out, lhs[0], rhs[1], start=False, stop=False)
                    return mm(out, lhs[1], rhs[0], start=False, stop=stop)

                def sum_squares(tag, n=T):
                    for k in range(KT):
                        if k == 0:
                            claim(7, (SL, (tag, "rms")))
                        pe.wait_ge(scalar_done, SL.value(l, (tag, "sq", k)))
                        i = mm(bank[7][:, 0:n], ones, sq[:, k, 0:n], start=k == 0, stop=k == KT - 1)
                    TL.done(i, (tag, "ss"))

                def ffn(tag):
                    sum_squares(tag)
                    for t in range(FT):
                        gb, ub = (t % 2) * 2, (t % 2) * 2 + 1
                        claim(gb, (VL, (tag, "gated", t)))
                        claim(ub, (VL, (tag, "hid", t)))
                        for b, o in ((gb, 0), (ub, 1)):
                            u = UNITS[tag] + 2 * t + o
                            hi, lo_ = split(u, KT)
                            for k in range(KT):
                                if t == 0 and o == 0:
                                    pe.wait_ge(vector_done, VL.value(l, (tag, "h_lo", k)))
                                i = mm3(bank[b][:, 0:T], (hi[:, k, :], lo_[:, k, :]), (h_hi[:, k, :], h_lo[:, k, :]),
                                        k == 0, k == KT - 1)
                            TL.done(i, ("unit", u))
                            TL.done(i, (tag, "up" if o else "gate", t))
                    for q in range(2 * FT):
                        half, t = divmod(q, FT)
                        u = UNITS[tag] + 2 * FT + q // 2
                        if q % 2 == 0:
                            hi, lo_ = split(u, 2)
                        if half == 0:
                            pe.wait_ge(vector_done, VL.value(l, (tag, "hid_lo", t)))
                        for d in range(4):
                            b = 4 + d if half == 0 else d
                            if t == 0:
                                claim(b, (VL, (tag, "x", half)))
                            s_ = slice(d * P, (d + 1) * P)
                            i = mm3(bank[b][:, 0:T], (hi[:, q % 2, s_], lo_[:, q % 2, s_]), (hid_hi[:, t, :], hid_lo[:, t, :]),
                                    t == 0, t == FT - 1)
                        if q % 2 == 1:
                            TL.done(i, ("unit", u))
                        if t == FT - 1:
                            TL.done(i, (tag, "down", half))

                def columns(tag, first, tiles, src, src_name, banks, reader):
                    for t in tiles:
                        b = banks[t % len(banks)]
                        claim(b, reader(t))
                        hi, lo_ = split(first + t, KT)
                        for k in range(KT):
                            if t == 0:
                                pe.wait_ge(*reached(l, *src_name(k)))
                            i = mm3(bank[b][:, 0:src[0].shape[2]], (hi[:, k, :], lo_[:, k, :]), (src[0][:, k, :], src[1][:, k, :]),
                                    k == 0, k == KT - 1)
                        TL.done(i, ("unit", first + t))
                        TL.done(i, (tag, "cols", t))

                ffn("ffn1")

                pe.wait_ge(con_landed, 16)

                sum_squares("mix")

                def in_reader(t):
                    if t in (11, 13):
                        return VL, ("glu", (t - 11) // 2)
                    return SL, ("in", t)

                def project(tiles):
                    columns("in", UNITS["in"], tiles, (h_hi, h_lo), lambda k: (VL, ("mix", "h_lo", k)), range(7), in_reader)

                project(range(IN_CUT[0]))

                lora = par_all[:, l, PAR["lora"]:PAR["lora"] + 2 * J * P]
                pe.wait_ge(scalar_done, SL.value(l, "lo_tanh"))
                pe.wait_ge(vector_done, VL.value(l, "lo_gate"))
                for kind, rows, off, src in ((0, slice(0, 64), 0, tmp[0:64, 0, :]), (1, slice(64, P), 0, xs[64:P, C_LO, :]),
                                             (2, slice(0, P), J * P, xs[:, C_G, :])):
                    for j in range(J):
                        b = (kind * J + j) % 7
                        claim(b, (SL, ("lora", kind, j)))
                        i = mm(bank[b][:, 0:T], lora[rows, off + j * P:off + (j + 1) * P], src, start=True, stop=True)
                        TL.done(i, ("lora", kind, j))

                project(range(IN_CUT[0], IN_CUT[1]))
                for j in range(J):
                    claim(j, (SL, ("kk_norm", j)))
                    pe.wait_ge(scalar_done, SL.value(l, "kk_sq"))
                    TL.done(mm(bank[j][:, 0:T], heads, tmp[:, j, :], start=True, stop=True), ("kk_ss", j))
                project(range(IN_CUT[1], IN_TILES))
                for j in range(J):
                    claim(3 + j, (SL, ("bonus", j)))
                    pe.wait_ge(vector_done, VL.value(l, ("rkr", J - 1)))
                    TL.done(mm(bank[3 + j][:, 0:T], heads, oT[:, j, :], start=True, stop=True), ("bonus", j))

                def vt(j, ct):
                    return xs[:, C_V + j, ct * P:(ct + 1) * P] if ct < 2 else xs[:, C_V + j, TP:T]

                def tile(a, j, ct):
                    return a[:, j, ct * P:(ct + 1) * P] if ct < 2 else a[:, j, TP:T]

                def hh_rows(a, hh):
                    return a[hh * HD:(hh + 1) * HD]

                pe.wait_ge(vector_done, VL.value(l, "primed"))
                for ct in range(2):
                    for kind, (lhs, rhs) in enumerate(((a_p, b_p), (b_p, a_p), (k_p, a_p), (b_p, r_p), (k_p, r_p))):
                        for hh in range(2):
                            b = (kind * 2 + hh) % 8
                            claim(b, (VL, ("pair", ct, kind, hh)))
                            for j in range(J):
                                i = mm(bank[b][:, j * P:(j + 1) * P], hh_rows(tile(lhs, j, ct), hh),
                                       hh_rows(tile(rhs, j, ct), hh), start=True, stop=True)
                            TL.done(i, ("pair", ct, kind, hh))
                    for kind, src in enumerate((b_p, k_p, None)):
                        b = (2 + kind) % 8
                        claim(b, (SL, ("tok", ct, kind)))
                        for j in range(J):
                            s_ = vt(j, ct) if src is None else tile(src, j, ct)
                            i = nc.tensor.transpose(bank[b][:, j * P:(j + 1) * P], s_, ident)
                        TL.done(i, ("tok", ct, kind))
                    for m in range(len(LEVELS)):
                        last = m == len(LEVELS) - 1
                        for hh in range(2):
                            claim(hh, (SL, ("y", ct, m, hh)))
                            pe.wait_ge(vector_done, VL.value(l, ("lo", ct, m)))
                            pe.wait_ge(vector_done, VL.value(l, ("x", ct, m - 1, hh) if m else ("x0", ct, hh)))
                            for j in range(J):
                                s_ = slice(j * P, (j + 1) * P)
                                i = mm(bank[hh][:, s_], lo[:, hh, s_], xm[:, hh, s_], start=True, stop=True)
                            TL.done(i, ("y", ct, m, hh))
                        for hh in range(2):
                            claim(2 + hh, (VL, ("x", ct, m, hh)))
                            pe.wait_ge(scalar_done, SL.value(l, ("y", ct, m, hh)))
                            pe.wait_ge(vector_done, VL.value(l, ("t", ct, m - 1, hh) if m else ("t0", ct, hh)))
                            for j in range(J):
                                s_ = slice(j * P, (j + 1) * P)
                                i = mm(bank[2 + hh][:, s_], tm[:, hh, s_], ym[:, hh, s_], start=True, stop=True)
                            TL.done(i, ("xinc", ct, m, hh))
                            if last:
                                continue
                            claim(4 + hh, (VL, ("t", ct, m, hh)))
                            for j in range(J):
                                s_ = slice(j * P, (j + 1) * P)
                                i = mm(bank[4 + hh][:, s_], ym[:, hh, s_], tm[:, hh, s_], start=True, stop=True)
                            TL.done(i, ("tinc", ct, m, hh))
                        if ct == 0:
                            claim(6 + m % 2, (VL, ("rope", m)))
                            pe.wait_ge(scalar_done, SL.value(l, ("in", IN_TILES - 1)))
                            i = mm(bank[6 + m % 2][:, 0:T], c("turn", P), qkv[:, m, :], start=True, stop=True)
                            TL.done(i, ("turn", m))
                    claim(6, (SL, ("r", ct)))
                    pe.wait_ge(scalar_done, SL.value(l, ("tok", ct, 2)))
                    if ct:
                        pe.wait_ge(vector_done, VL.value(l, ("state", 0)))
                    for j in range(J):
                        o = bank[6][:, j * P:(j + 1) * P]
                        if ct:
                            mm(o, tile(a_p, j, ct), st[:, j * P:(j + 1) * P], start=True, stop=False, skip_group_check=True)
                        for hh in range(2):
                            i = mm(o[:, hh * HD:(hh + 1) * HD], lak[:, hh, j * P:(j + 1) * P],
                                   tok[:, 2, j * P + hh * HD:j * P + (hh + 1) * HD], start=ct == 0, stop=True,
                                   skip_group_check=True)
                    TL.done(i, ("r", ct))
                    claim(7, (SL, ("u", ct)))
                    pe.wait_ge(scalar_done, SL.value(l, ("r", ct)))
                    pe.wait_ge(vector_done, VL.value(l, ("x", ct, len(LEVELS) - 1, 1)))
                    for j in range(J):
                        for hh in range(2):
                            s_ = slice(j * P + hh * HD, j * P + (hh + 1) * HD)
                            i = mm(bank[7][:, s_], xm[:, hh, j * P:(j + 1) * P], rm[:, s_], start=True, stop=True)
                    TL.done(i, ("u", ct))
                    claim(4, (SL, ("o", ct)))
                    claim(5, (VL, ("state", ct)))
                    pe.wait_ge(scalar_done, SL.value(l, ("u", ct)))
                    for j in range(J):
                        o = bank[4][:, j * P:(j + 1) * P]
                        if ct:
                            mm(o, st[:, j * P:(j + 1) * P], tile(r_p, j, ct), start=True, stop=False, skip_group_check=True)
                        for hh in range(2):
                            s_ = slice(j * P + hh * HD, j * P + (hh + 1) * HD)
                            oo = bank[4][hh * HD:(hh + 1) * HD, j * P:(j + 1) * P]
                            mm(oo, um[:, s_], lrb[:, hh, j * P:(j + 1) * P], start=ct == 0, stop=False, skip_group_check=True)
                            mm(oo, tok[:, 2, s_], lrk[:, hh, j * P:(j + 1) * P], start=False, stop=True, skip_group_check=True)
                        s_ = slice(j * P, (j + 1) * P)
                        mm(bank[5][:, s_], tok[:, 0, s_], um[:, s_], start=True, stop=False)
                        i = mm(bank[5][:, s_], tok[:, 1, s_], tok[:, 2, s_], start=False, stop=True)
                    TL.done(i, ("o_state", ct))

                for hh in range(2):
                    claim(hh, (VL, ("s_pair", hh)))
                    for kind, (lhs, rhs) in enumerate(((a_p, b_p), (b_p, a_p), (k_p, a_p), (b_p, r_p), (k_p, r_p))):
                        for j in range(J):
                            o = (kind * J + j) * TS
                            i = mm(bank[hh][0:TS, o:o + TS], hh_rows(tile(lhs, j, 2), hh), hh_rows(tile(rhs, j, 2), hh),
                                   start=True, stop=True)
                    TL.done(i, ("s_pair", hh))
                for kind, src in enumerate((b_p, k_p, None)):
                    claim(2 + kind, (SL, ("tok", 2, kind)))
                    for j in range(J):
                        s_ = vt(j, 2) if src is None else tile(src, j, 2)
                        i = nc.tensor.transpose(bank[2 + kind][0:TS, j * P:(j + 1) * P], s_, ident)
                    TL.done(i, ("tok", 2, kind))
                claim(5, (SL, "s_r0"))
                pe.wait_ge(wkv_landed, 16 * l + 16)
                for j in range(J):
                    for b_ in range(DEC_BATCH):
                        col = TP + b_ * DEC_SEQ
                        for hh in range(2):
                            i = mm(bank[5][hh * HD:(hh + 1) * HD, j * TS + b_ * DEC_SEQ:j * TS + (b_ + 1) * DEC_SEQ],
                                   hh_rows(wkv_s[:, j, b_], hh), hh_rows(a_p[:, j, col:col + DEC_SEQ], hh), start=True, stop=True)
                TL.done(i, "s_r0")
                claim(0, (SL, "s_y"))
                claim(1, (VL, "s_x"))
                for hh in range(2):
                    pe.wait_ge(vector_done, VL.value(l, ("s_masked", hh)))
                for hh in range(2):
                    for j in range(J):
                        s_ = slice(j * TS, (j + 1) * TS)
                        i = mm(bank[0][0:TS, (hh * J + j) * TS:(hh * J + j + 1) * TS], sm[0:TS, hh, 1, s_], sm[0:TS, hh, 2, s_],
                               start=True, stop=True)
                TL.done(i, "s_y")
                pe.wait_ge(scalar_done, SL.value(l, "s_y"))
                for hh in range(2):
                    for j in range(J):
                        s_ = slice(j * TS, (j + 1) * TS)
                        i = mm(bank[1][0:TS, (hh * J + j) * TS:(hh * J + j + 1) * TS], sm[0:TS, hh, 0, s_], sy[0:TS, hh, s_],
                               start=True, stop=True)
                TL.done(i, "s_xinc")
                claim(6, (SL, ("r", 2)))
                pe.wait_ge(scalar_done, SL.value(l, "s_r0"))
                pe.wait_ge(scalar_done, SL.value(l, ("tok", 2, 2)))
                for j in range(J):
                    o = bank[6][0:TS, j * P:(j + 1) * P]
                    mm(o, tmp_s[:, j * TS:(j + 1) * TS], ident, start=True, stop=False, skip_group_check=True)
                    for hh in range(2):
                        i = mm(o[:, hh * HD:(hh + 1) * HD], sm[0:TS, hh, 3, j * TS:(j + 1) * TS],
                               tok2[0:TS, 2, j * P + hh * HD:j * P + (hh + 1) * HD], start=False, stop=True,
                               skip_group_check=True)
                TL.done(i, ("r", 2))
                claim(7, (SL, ("u", 2)))
                pe.wait_ge(scalar_done, SL.value(l, ("r", 2)))
                pe.wait_ge(vector_done, VL.value(l, "s_x"))
                for j in range(J):
                    for hh in range(2):
                        s_ = slice(j * P + hh * HD, j * P + (hh + 1) * HD)
                        i = mm(bank[7][0:TS, s_], sm[0:TS, hh, 2, j * TS:(j + 1) * TS], rm2[0:TS, s_], start=True, stop=True)
                TL.done(i, ("u", 2))
                claim(4, (SL, ("o", 2)))
                pe.wait_ge(scalar_done, SL.value(l, ("u", 2)))
                for j in range(J):
                    for hh in range(2):
                        s_ = slice(j * P + hh * HD, j * P + (hh + 1) * HD)
                        oo = bank[4][hh * HD:(hh + 1) * HD, j * TS:(j + 1) * TS]
                        mm(oo, um2[0:TS, s_], sm[0:TS, hh, 4, j * TS:(j + 1) * TS], start=True, stop=False, skip_group_check=True)
                        mm(oo, tok2[0:TS, 2, s_], sm[0:TS, hh, 5, j * TS:(j + 1) * TS], start=False, stop=False,
                           skip_group_check=True)
                    for b_ in range(DEC_BATCH):
                        col = TP + b_ * DEC_SEQ
                        for hh in range(2):
                            i = mm(bank[4][hh * HD:(hh + 1) * HD, j * TS + b_ * DEC_SEQ:j * TS + (b_ + 1) * DEC_SEQ],
                                   hh_rows(wkv_s[:, j, b_], hh), hh_rows(r_p[:, j, col:col + DEC_SEQ], hh), start=False,
                                   stop=b_ == DEC_BATCH - 1, skip_group_check=True)
                TL.done(i, "s_o")

                def next_states(j):
                    pe.wait_ge(vector_done, VL.value(l, ("s_sel", j)))
                    b = (0, 1, 2)[j]
                    claim(b, (VL, ("s_state", j)))
                    for hh in range(2):
                        o, s_ = bank[b][hh * HD:(hh + 1) * HD, :], slice(j * P + hh * HD, j * P + (hh + 1) * HD)
                        mm(o, tok2[0:TS, 0, s_], usel[0:TS, :, hh * HD:(hh + 1) * HD], start=True, stop=False, skip_group_check=True)
                        i = mm(o, tok2[0:TS, 1, s_], vsel[0:TS, :, hh * HD:(hh + 1) * HD], start=False, stop=True,
                               skip_group_check=True)
                    TL.done(i, ("s_state", j))

                def conv_sum(step):
                    claim(7, (VL, "conv_mean") if step == "mean" else (SL, "conv_std"))
                    if step == "mean":
                        pe.wait_ge(pool_done, PL.value(l, ("summed", TAPS - 1)))
                    else:
                        pe.wait_ge(scalar_done, SL.value(l, "conv_sq"))
                    for ch in range(2):
                        i = mm(bank[7][:, 0:T], ones, (ycv if step == "mean" else yc2)[:, ch, :], start=ch == 0, stop=ch == 1)
                    TL.done(i, ("conv", step))

                def ln_sum(step):
                    for j in range(J):
                        b = (3, 5, 6)[j]
                        claim(b, (VL if step == "mu" else SL, ("ln_" + step, j)))
                        pe.wait_ge(scalar_done, SL.value(l, ("o", 2) if step == "mu" else "ln_sq"))
                        i = mm(bank[b][:, 0:T], heads, (oT if step == "mu" else tmp_ln)[:, j, :], start=True, stop=True)
                        TL.done(i, ("ln_" + step, j))

                conv_sum("mean")
                ln_sum("mu")
                next_states(0)
                conv_sum("var")
                ln_sum("var")
                next_states(1)
                next_states(2)

                def scores(u):
                    hh, qt = divmod(u, 2)
                    n = (qt + 1) * P
                    r_ = slice(hh * HD, (hh + 1) * HD)
                    for g in range(G):
                        b = (2 * u) % 4 if qt == 0 or g < 2 else (2 * u) % 4 + 1
                        if g == 0 or (g == 2 and qt == 1):
                            claim(b, (VL, ("masked", u, int(g == 2))))
                        o = g * n if (qt == 0 or g < 2) else 0
                        i = mm(bank[b][:, o:o + n], qkv[r_, g, qt * P:(qt + 1) * P], qkv[r_, G + g, 0:n], start=True, stop=True)
                        if (qt == 1 and g == 1) or g == 2:
                            TL.done(i, ("scores", u, int(g == 2)))

                def apply_probs(u):
                    hh, qt = divmod(u, 2)
                    for kt in range(qt + 1):
                        claim(4 + kt, (SL, ("pT", u, kt)))
                        pe.wait_ge(vector_done, VL.value(l, ("probs", u)))
                        for g in range(G):
                            i = nc.tensor.transpose(bank[4 + kt][:, g * P:(g + 1) * P],
                                                    sp_[:, u % 2, g * (qt + 1) * P + kt * P:g * (qt + 1) * P + (kt + 1) * P], ident)
                        TL.done(i, ("pT", u, kt))
                    b = 6 + hh
                    claim(b, (SL, ("attn", u)))
                    for g in range(G):
                        for kt in range(qt + 1):
                            pe.wait_ge(scalar_done, SL.value(l, ("pT", u, kt)))
                            i = mm(bank[b][hh * HD:(hh + 1) * HD, g * P:(g + 1) * P], vtok[:, kt, g, hh * HD:(hh + 1) * HD],
                                   spT[:, u % 2, g, kt, :], start=kt == 0, stop=kt == qt)
                    TL.done(i, ("attn", u))

                pe.wait_ge(vector_done, VL.value(l, "wkv_s"))
                for ct in range(3):
                    n, rows = (P, slice(ct * P, (ct + 1) * P)) if ct < 2 else (TS, slice(TP, T))
                    claim(4 + ct, (SL, ("vtok", ct)))
                    for g in range(G):
                        i = nc.tensor.transpose(bank[4 + ct][0:n, g * P:(g + 1) * P], qkv[:, 2 * G + g, rows], ident)
                    TL.done(i, ("vtok", ct))
                q5 = qbd[:, :, :].rearrange("p g (b h t) -> p g b h t", b=DEC_BATCH, h=2)

                def cache_scores(pair):
                    if pair == 0:
                        claim(1, (SL, "sT"))
                        pe.wait_ge(vector_done, VL.value(l, "qbd"))
                    w = arrived(SLAB_AT["wink", pair])
                    for b_ in (2 * pair, 2 * pair + 1):
                        kc = w[:, (b_ % 2) * 896:(b_ % 2 + 1) * 896]
                        o5 = bank[1][:, 0:G * 64].rearrange("p (g b h t) -> p g b h t", g=G, b=DEC_BATCH, h=2)
                        mm(o5[:, 0, b_], kc[:, 0:P], q5[:, 0, b_], start=True, stop=True)
                        for t in range(DEC_SEQ):
                            mm(o5[:, 1, b_, :, t], kc[:, P * (1 + t):P * (2 + t)], q5[:, 1, b_, :, t], start=True, stop=True)
                        for t in range(2):
                            i = mm(o5[:, 2, b_, :, 2 * t:2 * t + 2], kc[:, P * (5 + t):P * (6 + t)], q5[:, 2, b_, :, 2 * t:2 * t + 2],
                                   start=True, stop=True)
                    TL.done(i, ("slab", SLAB_AT["wink", pair]))
                    if pair == 3:
                        for g in range(G):
                            i = mm(bank[1][0:TS, (G + g) * 64:(G + g + 1) * 64], qkv[:, G + g, TP:T], qbd[:, g, :], start=True, stop=True)
                        TL.done(i, "sT")

                pe.wait_ge(vector_done, VL.value(l, "roped"))
                for u in range(5):
                    if u < 4:
                        scores(u)
                        cache_scores(u)
                    if u:
                        apply_probs(u - 1)
                claim(2, (VL, "s_scores"))
                pe.wait_ge(scalar_done, SL.value(l, "sT"))
                for g in range(G):
                    o = g * (P + TS)
                    nc.tensor.transpose(bank[2][0:64, o:o + P], ssT[:, g, :], ident)
                    i = nc.tensor.transpose(bank[2][0:64, o + P:o + P + TS], ssn[0:TS, g, :], ident[0:TS, 0:TS])
                TL.done(i, "s_scores")
                claim(3, (SL, "psT"))
                claim(4, (SL, "psn"))
                pe.wait_ge(vector_done, VL.value(l, "s_probs"))
                for g in range(G):
                    o = g * (P + TS)
                    i = nc.tensor.transpose(bank[3][:, g * 64:(g + 1) * 64], ss[0:64, o:o + P], ident[0:64, 0:64])
                TL.done(i, "psT")
                for g in range(G):
                    o = g * (P + TS)
                    i = nc.tensor.transpose(bank[4][0:TS, g * 64:(g + 1) * 64], ss[0:64, o + P:o + P + TS], ident[0:64, 0:64])
                TL.done(i, "psn")
                claim(5, (SL, "s_attn"))
                pe.wait_ge(scalar_done, SL.value(l, "psT"))
                pe.wait_ge(scalar_done, SL.value(l, "psn"))
                for g in range(G):
                    mm(bank[5][:, g * 64:(g + 1) * 64], vtok_s[0:TS, g, :], psn[0:TS, g, :], start=g == 0, stop=False,
                       skip_group_check=True)
                p5 = psT.rearrange("p g (b h t) -> p g b h t", b=DEC_BATCH, h=2)
                o5 = bank[5][:, 0:G * 64].rearrange("p (g b h t) -> p g b h t", g=G, b=DEC_BATCH, h=2)
                for b_ in range(DEC_BATCH):
                    if b_ % 2 == 0:
                        w = arrived(SLAB_AT["winv", b_ // 2])
                    vc = w[:, (b_ % 2) * 896:(b_ % 2 + 1) * 896]
                    kw = dict(start=False, stop=True, skip_group_check=True)
                    mm(o5[:, 0, b_], vc[:, 0:P], p5[:, 0, b_], **kw)
                    for t in range(DEC_SEQ):
                        mm(o5[:, 1, b_, :, t], vc[:, P * (1 + t):P * (2 + t)], p5[:, 1, b_, :, t], **kw)
                    for t in range(2):
                        i = mm(o5[:, 2, b_, :, 2 * t:2 * t + 2], vc[:, P * (5 + t):P * (6 + t)], p5[:, 2, b_, :, 2 * t:2 * t + 2],
                               **kw)
                    if b_ % 2:
                        TL.done(i, ("slab", SLAB_AT["winv", b_ // 2]))
                TL.done(i, "s_attn")

                columns("out", UNITS["out"], range(KT), (h_hi, h_lo), lambda k: (VL, "attn_lo"), range(7), lambda t: (VL, ("x_out", t)))

                sum_squares("xattn")
                columns("q", UNITS["q"], range(KT), (h_hi, h_lo), lambda k: (VL, ("xattn", "h_lo", k)), range(7), lambda t: (SL, ("qx", t)))
                sum_squares("mem", MEM)

                def sample_scores(b_):
                    half, q4 = divmod(b_, 4)
                    if q4 == 0:
                        claim(4 + half, (SL, ("xexp", 8 + half)))
                    w = arrived(SLAB_AT["memk", b_]).rearrange("p (d m) -> p d m", d=KT)
                    for dt in range(KT):
                        i = mm(bank[4 + half][q4 * 32:(q4 + 1) * 32, 0:MEM], qz[:, dt, b_, :], w[:, dt, :], start=dt == 0,
                               stop=dt == KT - 1, skip_group_check=True)
                    TL.done(i, ("slab", SLAB_AT["memk", b_]))
                    if q4 == 3:
                        TL.done(i, ("xs", 8 + half))

                for n in range(4):
                    columns("k", UNITS["kv"], (2 * n, 2 * n + 1), (hm_hi, hm_lo), lambda k: (VL, ("mem", "h_lo", k)), K_BANKS,
                            lambda t: (SL, ("kx", t)))
                    if n:
                        sample_scores(n - 1)
                pe.wait_ge(scalar_done, SL.value(l, ("kx", KT - 1)))
                for u in range(8):
                    hd, qt = divmod(u, 2)
                    if qt == 0:
                        claim(hd, (SL, ("xexp", u + 1)))
                    for dt in range(2):
                        i = mm(bank[hd][:, qt * MEM:(qt + 1) * MEM], qx[:, 2 * hd + dt, qt * P:(qt + 1) * P], kx[:, 2 * hd + dt, :],
                               start=dt == 0, stop=dt == 1)
                    TL.done(i, ("xs", u))
                for n in range(4):
                    for mt in range(2):
                        claim(V_BANKS[n * 2 + mt], (SL, ("vx", n * 2 + mt)))
                    for half in range(2):
                        u = UNITS["kv"] + KT + 2 * n + half
                        hi, lo_ = split(u, KT // 2)
                        for mt in range(2):
                            for k4 in range(KT // 2):
                                k, s_ = half * (KT // 2) + k4, slice(mt * P, (mt + 1) * P)
                                i = mm3(bank[V_BANKS[n * 2 + mt]][:, 0:256], (hm_hi[:, k, s_], hm_lo[:, k, s_]),
                                        (hi[:, k4, :], lo_[:, k4, :]), k == 0, k == KT - 1)
                            if mt:
                                TL.done(i, ("unit", u))
                            if half:
                                TL.done(i, ("vx", n * 2 + mt))
                    if n + 3 < MEMK_EARLY:
                        sample_scores(n + 3)
                for b_ in range(MEMK_EARLY, DEC_BATCH):
                    sample_scores(b_)
                def probs_T(u):
                    b = (6, 7)[u % 2]
                    claim(b, (SL, ("xpT", u)))
                    pe.wait_ge(vector_done, VL.value(l, ("xprobs", unit_head(u))))
                    for kt in range(2):
                        i = nc.tensor.transpose(bank[b][:, kt * P:(kt + 1) * P], px[:, u, kt * P:(kt + 1) * P], ident)
                    TL.done(i, ("xpT", u))

                def prompt_out(hd):
                    claim(hd, (VL, ("ox_lo", hd)))
                    pe.wait_ge(scalar_done, SL.value(l, ("xpT", 2 * hd + 1)))
                    if hd == 0:
                        pe.wait_ge(scalar_done, SL.value(l, ("vx", 7)))
                    for dt in (2 * hd, 2 * hd + 1):
                        for kt in range(2):
                            i = mm(bank[hd][:, (dt % 2) * TP:(dt % 2 + 1) * TP], vx[:, kt, dt * P:(dt + 1) * P], pxT[:, hd, kt, :],
                                   start=kt == 0, stop=kt == 1)
                    TL.done(i, ("ox", hd))

                for hd in range(4):
                    probs_T(2 * hd)
                    probs_T(2 * hd + 1)
                    if hd:
                        prompt_out(hd - 1)
                probs_T(8)
                prompt_out(3)
                probs_T(9)
                pe.wait_ge(scalar_done, SL.value(l, ("xpT", 9)))

                def channels_back(half):
                    for n in range(2):
                        b = 2 * half + n
                        claim(b, (VL, ("oxs_lo", half, n)))
                        pe.wait_ge(scalar_done, SL.value(l, ("oxs", half, n)))
                        for d in range(4):
                            dt = 4 * n + d
                            i = nc.tensor.transpose(bank[b][:, d * P:(d + 1) * P], oxs[:, half, dt * P:(dt + 1) * P], ident)
                        TL.done(i, ("oxsT", half, n))

                for b_ in range(DEC_BATCH):
                    half, q4 = divmod(b_, 4)
                    w = arrived(SLAB_AT["memv", b_]).rearrange("p (k c) -> p k c", k=2)
                    for n in range(2):
                        b = 4 + 2 * half + n
                        if q4 == 0:
                            claim(b, (SL, ("oxs", half, n)))
                        for kt in range(2):
                            i = mm(bank[b][q4 * 32:(q4 + 1) * 32, :], pxsT[:, kt, half, q4 * 32:(q4 + 1) * 32],
                                   w[:, kt, n * 512:(n + 1) * 512], start=kt == 0, stop=kt == 1, skip_group_check=True)
                        if n == 1:
                            TL.done(i, ("slab", SLAB_AT["memv", b_]))
                        if q4 == 3:
                            TL.done(i, ("oxs", half, n))
                    if b_ == 5:
                        channels_back(0)
                channels_back(1)
                columns("o", UNITS["o"], range(KT), (ox_hi, ox_lo), lambda k: (VL, ("oxs_lo", 1, 1)),
                        (5, 6, 7, 0, 1, 2, 3), lambda t: (VL, ("x_o", t)))
                ffn("ffn2")
            l = DEPTH - 1
            for k in range(KT):
                pe.wait_ge(scalar_done, SL.value(l, ("final", "sq", k)))
                i = mm(bank[7][:, 0:T], ones, sq[:, k, :], start=k == 0, stop=k == KT - 1)
            TL.done(i, ("final", "ss"))

        @block.scalar
        def _(act):
            act.sem_inc(scalar_done, SL.total)
            act.wait_ge(start_landed, 48)
            fn = nc.scalar.activation

            for l in range(DEPTH):
                SL.begin_layer()

                def copy(out, in_, name=None):
                    return SL.done(nc.scalar.copy(out, in_), name)

                def split(u):
                    if u is None:
                        return
                    act.wait_ge(*landed(l, SLAB_OF_UNIT[u][0]))
                    if u >= NW:
                        act.wait_ge(tensor_done, TL.value(l, ("unit", u - NW)))
                    else:
                        held = max(v for v in range(NUNIT) if v % NW == u % NW)
                        act.wait_ge(tensor_done, TL.value_before(l, ("unit", held)))
                    copy(w_hi[:, u % NW, :], raw_unit(u), ("hi", u))

                def rms(tag, src, rs_, n, ready, between=lambda: None, hi=None):
                    for k in range(KT):
                        ready(k)
                        SL.done(fn(sq[:, k, 0:n], src[:, k, 0:n], ACT.Square), (tag, "sq", k))
                    between()
                    SL.done(fn(warm, con[:, CON["ones"]:CON["ones"] + 1], ACT.Sqrt))
                    act.wait_ge(tensor_done, TL.value(l, (tag, "ss")))
                    SL.done(fn(rs_[:, 0:n], bank[7][:, 0:n], ACT.Sqrt, bias=NORM_EPS, scale=1.0 / D_MODEL), (tag, "rms"))
                    if hi is not None:
                        for k in range(KT):
                            act.wait_ge(vector_done, VL.value(l, (tag, "h", k)))
                            copy(hi[:, k, 0:n], (h if hi is h_hi else hm)[:, k, 0:n], (tag, "h_hi", k))

                def ffn(tag, ready, between=lambda: None):
                    first = UNITS[tag]
                    rms(tag, x, rs, T, ready, between, h_hi)
                    for t in range(FT):
                        act.wait_ge(tensor_done, TL.value(l, (tag, "gate", t)))
                        if t >= 2:
                            act.wait_ge(vector_done, VL.value(l, (tag, "gated", t - 2)))
                        SL.done(fn(th[:, t % 2, :], bank[(t % 2) * 2][:, 0:T], ACT.Tanh, scale=0.5), (tag, "tanh", t))
                        split(next_unit(first + 2 * t))
                        split(next_unit(first + 2 * t + 1))
                        act.wait_ge(vector_done, VL.value(l, (tag, "hid", t)))
                        copy(hid_hi[:, t, :], hid[:, t, :], (tag, "hid_hi", t))
                    for u in range(first + 2 * FT, first + 3 * FT):
                        split(next_unit(u))

                ffn("ffn1", lambda k: act.wait_ge(vector_done, VL.value_before(l, ("ffn2", "x", 1))),
                    lambda: [split(u) for u in range(NW)])

                rms("mix", x, rs, T, lambda k: act.wait_ge(vector_done, VL.value(l, ("ffn1", "x", k // 4))), hi=h_hi)
                def project(t):
                    b = t % 7
                    if t in (11, 13):
                        split(next_unit(UNITS["in"] + t))
                        return
                    act.wait_ge(tensor_done, TL.value(l, ("in", "cols", t)))
                    if t < NC_TILES:
                        copy(f_p[:, t, 1:], bank[b][:, 0:TP])
                        copy(f_s[:, t, :, 1:], bt(bank[b][:, TP:T]), ("in", t))
                    elif t in (12, 14):
                        SL.done(fn(w_i[:, (t - 12) // 2, :], bank[b][:, 0:T], ACT.Tanh, scale=0.5), ("in", t))
                    else:
                        copy(qkv[:, t - 15, :], bank[b][:, 0:T], ("in", t))
                    split(next_unit(UNITS["in"] + t))
                for t in range(IN_CUT[0]):
                    project(t)
                act.wait_ge(vector_done, VL.value(l, "shift_out"))
                SL.done(fn(tmp[:, 1, :], xs[:, C_G, :], ACT.Tanh, scale=0.5), "g_tanh")
                SL.done(fn(tmp[0:64, 0, :], xs[0:64, C_LO, :], ACT.Tanh), "lo_tanh")
                act.wait_ge(vector_done, VL.value(l, "halves"))
                for kind in range(3):
                    for j in range(J):
                        b = (kind * J + j) % 7
                        act.wait_ge(tensor_done, TL.value(l, ("lora", kind, j)))
                        if kind == 2:
                            copy(gz[:, j, :], bank[b][:, 0:T], ("lora", kind, j))
                        else:
                            SL.done(fn((ld, aa)[kind][:, j, :], bank[b][:, 0:T], ACT.Tanh, scale=0.5,
                                       bias=halves[:, kind * J + j:kind * J + j + 1]), ("lora", kind, j))
                for t in range(IN_CUT[0], IN_CUT[1]):
                    project(t)
                act.wait_ge(vector_done, VL.value(l, "kk"))
                SL.done(fn(tmp, kk, ACT.Square), "kk_sq")
                for j in range(J):
                    act.wait_ge(tensor_done, TL.value(l, ("kk_ss", j)))
                    SL.done(fn(tmp[:, j, :], bank[j][:, 0:T], ACT.Sqrt), ("kk_norm", j))
                project(IN_CUT[1])
                act.wait_ge(vector_done, VL.value(l, "centred"))
                SL.done(fn(w_c, cl, ACT.Exp), "w_c")
                SL.done(fn(w_i, cl, ACT.Exp, scale=-1.0), "w_i")
                act.wait_ge(vector_done, VL.value(l, "before"))
                SL.done(fn(w_p, ld, ACT.Exp), "w_p")
                SL.done(fn(wmid1, mids[:, :, 1:2], ACT.Exp), "w_mid")
                for t in range(IN_CUT[1] + 1, IN_TILES):
                    project(t)
                for j in range(J):
                    act.wait_ge(tensor_done, TL.value(l, ("bonus", j)))
                    copy(bon[:, j, :], bank[3 + j][:, 0:T], ("bonus", j))
                act.wait_ge(vector_done, VL.value(l, "primed"))
                act.dma_start(wkv_s, wkv_in[l]).then_inc(wkv_landed, 16)
                for ct in range(2):
                    for kind in range(3):
                        act.wait_ge(tensor_done, TL.value(l, ("tok", ct, kind)))
                        copy(tok[:, kind], bank[(2 + kind) % 8][:, 0:J * P], ("tok", ct, kind))
                    for m in range(len(LEVELS)):
                        for hh in range(2):
                            act.wait_ge(tensor_done, TL.value(l, ("y", ct, m, hh)))
                            copy(ym[:, hh], bank[hh][:, 0:J * P], ("y", ct, m, hh))
                    act.wait_ge(tensor_done, TL.value(l, ("r", ct)))
                    copy(rm, bank[6][:, 0:J * P], ("r", ct))
                    act.wait_ge(tensor_done, TL.value(l, ("u", ct)))
                    copy(um, bank[7][:, 0:J * P], ("u", ct))
                    act.wait_ge(tensor_done, TL.value(l, ("o_state", ct)))
                    copy(oT[:, :, ct * P:(ct + 1) * P], bank[4][:, 0:J * P].rearrange("p (j t) -> p j t", j=J), ("o", ct))
                for kind in range(3):
                    act.wait_ge(tensor_done, TL.value(l, ("tok", 2, kind)))
                    copy(tok2[0:TS, kind], bank[2 + kind][0:TS, 0:J * P], ("tok", 2, kind))
                act.wait_ge(tensor_done, TL.value(l, "s_r0"))
                copy(tmp_s, bank[5][:, 0:J * TS], "s_r0")
                act.wait_ge(tensor_done, TL.value(l, "s_y"))
                copy(sy[0:TS], bank[0][0:TS, 0:2 * J * TS].rearrange("p (h c) -> p h c", h=2), "s_y")
                act.wait_ge(tensor_done, TL.value(l, ("r", 2)))
                copy(rm2[0:TS], bank[6][0:TS, 0:J * P], ("r", 2))
                act.wait_ge(tensor_done, TL.value(l, ("u", 2)))
                copy(um2[0:TS], bank[7][0:TS, 0:J * P], ("u", 2))
                act.wait_ge(tensor_done, TL.value(l, "s_o"))
                copy(oT[:, :, TP:T], bank[4][:, 0:J * TS].rearrange("p (j t) -> p j t", j=J), ("o", 2))
                act.wait_ge(vector_done, VL.value(l, "conv_mean"))
                SL.done(fn(yc2, ycv, ACT.Square), "conv_sq")
                act.wait_ge(vector_done, VL.value(l, ("ln_mu", J - 1)))
                SL.done(fn(tmp_ln, oT, ACT.Square), "ln_sq")
                act.wait_ge(tensor_done, TL.value(l, ("conv", "var")))
                SL.done(fn(yc2[:, 0, :], bank[7][:, 0:T], ACT.Sqrt, bias=CONV_EPS, scale=1.0 / 256), "conv_std")
                for j in range(J):
                    act.wait_ge(tensor_done, TL.value(l, ("ln_var", j)))
                    SL.done(fn(tmp_ln[:, j, :], bank[(3, 5, 6)[j]][:, 0:T], ACT.Sqrt, bias=LNX_EPS, scale=1.0 / HD), ("ln_var", j))
                act.wait_ge(vector_done, VL.value(l, "conv_norm"))
                SL.done(fn(yc2, ycv, ACT.Tanh, scale=0.5), "conv_tanh")
                act.wait_ge(vector_done, VL.value(l, "rwkv_out"))
                copy(h_hi[:, 0:2, :], h[:, 0:2, :])
                copy(h_hi[:, 5:5 + J, :], h[:, 5:5 + J, :], "mix_hi")

                for ct in range(3):
                    act.wait_ge(tensor_done, TL.value(l, ("vtok", ct)))
                    if ct < 2:
                        copy(vtok[:, ct], bank[4 + ct][:, 0:G * P].rearrange("p (g c) -> p g c", g=G), ("vtok", ct))
                    else:
                        copy(vtok_s[0:TS], bank[4 + ct][0:TS, 0:G * P].rearrange("p (g c) -> p g c", g=G), ("vtok", ct))

                def probs(u):
                    qt = u % 2
                    n = G * (qt + 1) * P
                    act.wait_ge(vector_done, VL.value(l, ("nmax", u)))
                    SL.done(fn(sp_[:, qt, 0:n], sp_[:, qt, 0:n], ACT.Exp, scale=ATTN_SCALE, bias=astat[:, 1, u:u + 1],
                               accum_out=astat[:, 2, u:u + 1]), ("exp", u))

                for u in range(5):
                    if u < 4:
                        probs(u)
                    if u:
                        v = u - 1
                        hh, qt = divmod(v, 2)
                        for kt in range(qt + 1):
                            act.wait_ge(tensor_done, TL.value(l, ("pT", v, kt)))
                            copy(spT[:, v % 2, :, kt, :], bank[4 + kt][:, 0:G * P].rearrange("p (g c) -> p g c", g=G), ("pT", v, kt))
                        act.wait_ge(tensor_done, TL.value(l, ("attn", v)))
                        r_ = slice(hh * HD, (hh + 1) * HD)
                        copy(h[r_, 2:2 + G, qt * P:(qt + 1) * P], bank[6 + hh][r_, 0:G * P].rearrange("p (g c) -> p g c", g=G),
                             ("attn", v))
                act.wait_ge(tensor_done, TL.value(l, "sT"))
                copy(ssT, bank[1][:, 0:G * 64].rearrange("p (g c) -> p g c", g=G))
                copy(ssn[0:TS], bank[1][0:TS, G * 64:2 * G * 64].rearrange("p (g c) -> p g c", g=G), "sT")
                act.wait_ge(vector_done, VL.value(l, ("nmax", 4)))
                SL.done(fn(ss[0:64], ss[0:64], ACT.Exp, scale=ATTN_SCALE, bias=astat[0:64, 1, 4:5],
                           accum_out=astat[0:64, 2, 4:5]), ("exp", 4))
                act.wait_ge(tensor_done, TL.value(l, "psT"))
                copy(psT, bank[3][:, 0:G * 64].rearrange("p (g c) -> p g c", g=G), "psT")
                act.wait_ge(tensor_done, TL.value(l, "psn"))
                copy(psn[0:TS], bank[4][0:TS, 0:G * 64].rearrange("p (g c) -> p g c", g=G), "psn")
                for u in range(NW):
                    split(UNITS["out"] + u)
                act.wait_ge(tensor_done, TL.value(l, "s_attn"))
                for hh in range(2):
                    r_ = slice(hh * HD, (hh + 1) * HD)
                    o4 = bank[5][r_, 0:G * 64].rearrange("p (g b h t) -> p g b h t", g=G, b=DEC_BATCH, h=2)
                    for g in range(G):
                        copy(bt(h[r_, 2 + g, TP:T]), o4[:, g, :, hh, :], "s_attn" if (hh, g) == (1, G - 1) else None)

                act.wait_ge(scalar_done, SL.value(l, "s_attn"))
                copy(h_hi[:, 2:2 + G, :], h[:, 2:2 + G, :], "attn_hi")

                def out_done(k):
                    split(next_unit(UNITS["out"] + k))
                    act.wait_ge(vector_done, VL.value(l, ("x_out", k)))
                rms("xattn", x, rs, T, out_done, hi=h_hi)
                act.wait_ge(stored, store_value(l, "wkv_s"))
                for t in range(KT):
                    act.wait_ge(tensor_done, TL.value(l, ("q", "cols", t)))
                    copy(qx[:, t, :], bank[t % 7][:, 0:T])
                    if t == 0:
                        act.wait_ge(vector_done, VL.value(l, "qz_clear"))
                    copy(qz[:, t, :, 4 * (t // 2):4 * (t // 2) + 4], bt(bank[t % 7][:, TP:T]), ("qx", t))
                    split(next_unit(UNITS["q"] + t))
                act.wait_ge(mem_landed, 16 * l + 16)
                rms("mem", memx, mem_rs, MEM, lambda k: None, hi=hm_hi)
                for t in range(KT):
                    act.wait_ge(tensor_done, TL.value(l, ("k", "cols", t)))
                    copy(kx[:, t, :], bank[K_BANKS[t % 6]][:, 0:MEM], ("kx", t))
                    split(next_unit(UNITS["kv"] + t))
                def xexp(u):
                    src = bank[u // 2][:, (u % 2) * MEM:(u % 2 + 1) * MEM] if u < 8 else bank[u - 4][:, 0:MEM]
                    act.wait_ge(vector_done, VL.value(l, ("xnmax", unit_head(u))))
                    SL.done(fn(px[:, u, :], src, ACT.Exp, scale=X_SCALE, bias=xstat[:, 1, u:u + 1],
                               accum_out=xstat[:, 2, u:u + 1]), ("xexp", u))

                for n in range(4):
                    xexp(2 * n)
                    split(next_unit(UNITS["kv"] + KT + 2 * n))
                    xexp(2 * n + 1)
                    for mt in range(2):
                        m = 2 * n + mt
                        act.wait_ge(tensor_done, TL.value(l, ("vx", m)))
                        copy(vx[:, mt, n * 256:(n + 1) * 256], bank[V_BANKS[m]][:, 0:256], ("vx", m))
                    split(next_unit(UNITS["kv"] + KT + 2 * n + 1))
                xexp(8)
                xexp(9)

                def probs_T(u):
                    act.wait_ge(tensor_done, TL.value(l, ("xpT", u)))
                    out = pxT[:, u // 2, :, (u % 2) * P:(u % 2 + 1) * P] if u < 8 else pxsT[:, :, u - 8, :]
                    copy(out, bank[6 + u % 2][:, 0:2 * P].rearrange("p (k c) -> p k c", k=2), ("xpT", u))

                def prompt_out(hd):
                    act.wait_ge(tensor_done, TL.value(l, ("ox", hd)))
                    copy(ox_hi[:, 2 * hd:2 * hd + 2, 0:TP], bank[hd][:, :].rearrange("p (a c) -> p a c", a=2), ("ox", hd))

                for hd in range(4):
                    probs_T(2 * hd)
                    probs_T(2 * hd + 1)
                    if hd:
                        prompt_out(hd - 1)
                probs_T(8)
                probs_T(9)
                prompt_out(3)
                for half in range(2):
                    for n in range(2):
                        act.wait_ge(tensor_done, TL.value(l, ("oxs", half, n)))
                        copy(oxs[:, half, n * 512:(n + 1) * 512], bank[4 + 2 * half + n][:, :], ("oxs", half, n))
                    for n in range(2):
                        act.wait_ge(tensor_done, TL.value(l, ("oxsT", half, n)))
                        for hd in (2 * n, 2 * n + 1):
                            copy(sample_out(ox_hi, half, hd), head_columns(half, hd), ("oxs_hi", half, hd))
                    if half == 0:
                        for u in range(NW):
                            split(UNITS["o"] + u)

                def ready2(k):
                    split(next_unit(UNITS["o"] + k))
                    act.wait_ge(vector_done, VL.value(l, ("x_o", k)))
                    if k == 0:
                        act.wait_ge(stored, store_value(l, "memv"))
                ffn("ffn2", ready2)
            l = DEPTH - 1
            rms("final", x, rs, T, lambda k: act.wait_ge(vector_done, VL.value(l, ("ffn2", "x", k // 4))))

        @block.vector
        def _(dve):
            dve.sem_inc(vector_done, VL.total)
            dve.wait_ge(start_landed, 48)
            tt, ts, stt = nc.vector.tensor_tensor, nc.vector.tensor_scalar, nc.vector.scalar_tensor_tensor
            cp = nc.vector.tensor_copy

            for l in range(DEPTH):
                VL.begin_layer()

                def settle():
                    dve.wait_ge(vector_done, VL.so_far(l))

                D = VL.done
                par = par_all[:, l, :]

                def pr(name, i):
                    return par[:, PAR[name] + i:PAR[name] + i + 1]

                def low(out, src, hi, name=None):
                    D(tt(out, src, hi.bitcast(F32), ALU.subtract), name)

                def split(u):
                    if u is not None:
                        dve.wait_ge(scalar_done, SL.value(l, ("hi", u)))
                        low(w_lo[:, u % NW, :], raw_unit(u), w_hi[:, u % NW, :], ("lo", u))

                def normalise(tag, src, dst, rs_, n, parts=None):
                    dve.wait_ge(scalar_done, SL.value(l, (tag, "rms")))
                    D(nc.vector.reciprocal(rs_[:, 0:n], rs_[:, 0:n]))
                    settle()
                    for k in range(KT + 1):
                        if k < KT:
                            D(stt(dst[:, k, 0:n], src[:, k, 0:n], pr(tag, k), rs_[:, 0:n], ALU.mult, ALU.mult), (tag, "h", k))
                        if k and parts:
                            dve.wait_ge(scalar_done, SL.value(l, (tag, "h_hi", k - 1)))
                            low(parts[1][:, k - 1, 0:n], dst[:, k - 1, 0:n], parts[0][:, k - 1, 0:n], (tag, "h_lo", k - 1))

                def ffn(tag):
                    first = UNITS[tag]
                    normalise(tag, x, h, rs, T, (h_hi, h_lo))
                    for t in range(FT):
                        dve.wait_ge(scalar_done, SL.value(l, (tag, "tanh", t)))
                        D(stt(th2[:, t % 2, :], th[:, t % 2, :], 1.0, bank[(t % 2) * 2][:, 0:T], ALU.add, ALU.mult),
                          (tag, "gated", t))
                        split(next_unit(first + 2 * t))
                        settle()
                        dve.wait_ge(tensor_done, TL.value(l, (tag, "up", t)))
                        D(tt(hid[:, t, :], th2[:, t % 2, :], bank[(t % 2) * 2 + 1][:, 0:T], ALU.mult), (tag, "hid", t))
                        split(next_unit(first + 2 * t + 1))
                        dve.wait_ge(scalar_done, SL.value(l, (tag, "hid_hi", t)))
                        low(hid_lo[:, t, :], hid[:, t, :], hid_hi[:, t, :], (tag, "hid_lo", t))
                    for half in range(2):
                        for u in range(first + 2 * FT + half * FT // 2, first + 2 * FT + (half + 1) * FT // 2):
                            split(next_unit(u))
                        dve.wait_ge(tensor_done, TL.value(l, (tag, "down", half)))
                        for d in range(4):
                            k = 4 * half + d
                            D(stt(x[:, k, :], bank[4 + d if half == 0 else d][:, 0:T], 0.25, x[:, k, :], ALU.mult, ALU.add),
                              (tag, "x", half) if d == 3 else None)

                for u in range(NW):
                    split(u)
                ffn("ffn1")

                dve.wait_ge(con_landed, 16)
                D(ts(halves, par[:, PAR["w0"]:PAR["w0"] + 2 * J], 0.5, None, ALU.mult), "halves")
                normalise("mix", x, h, rs, T, (h_hi, h_lo))
                D(nc.vector.memset(f_p[:, :, 0:1], 0.0))
                D(cp(f_s[:, :, :, 0], par[:, PAR["state_shift"]:PAR["state_shift"] + NC_TILES * 8]
                     .rearrange("p (c b) -> p c b", b=DEC_BATCH)))
                D(nc.vector.memset(up[:, :, 0:HIST], 0.0))
                settle()
                for t in range(NC_TILES):
                    dve.wait_ge(scalar_done, SL.value(l, ("in", t)))
                    D(tt(xs[:, t, 0:TP], f_p[:, t, 0:TP], f_p[:, t, 1:], ALU.subtract))
                    D(tt(bt(xs[:, t, TP:T]), f_s[:, t, :, 0:DEC_SEQ], f_s[:, t, :, 1:], ALU.subtract))
                    settle()
                    D(stt(xs[:, t, 0:TP], xs[:, t, 0:TP], pr("shift", t), f_p[:, t, 1:], ALU.mult, ALU.add))
                    D(stt(bt(xs[:, t, TP:T]), bt(xs[:, t, TP:T]), pr("shift", t), f_s[:, t, :, 1:], ALU.mult, ALU.add), ("xs", t))
                    split(next_unit(UNITS["in"] + t))
                D(cp(shift_o[:, :, 0:1], f_p[:, :, TP:TP + 1]))
                D(cp(shift_o[:, :, 1:], f_s[:, :, :, DEC_SEQ]), "shift_out")
                for ch in range(2):
                    split(next_unit(UNITS["in"] + 11 + 2 * ch))
                    dve.wait_ge(scalar_done, SL.value(l, ("in", 12 + 2 * ch)))
                    D(ts(w_i[:, ch, :], w_i[:, ch, :], 0.5, 0.5, ALU.mult, ALU.add))
                    settle()
                    b = 11 + 2 * ch
                    dve.wait_ge(tensor_done, TL.value(l, ("in", "cols", b)))
                    if ch == 0:
                        dve.wait_ge(layer_landed, 16 * l + 16)
                    D(tt(up[:, ch, HIST:], w_i[:, ch, 0:TP], bank[b % 7][:, 0:TP], ALU.mult))
                    D(tt(us4[:, ch, :, HIST:], bt(w_i[:, ch, TP:T]), bt(bank[b % 7][:, TP:T]), ALU.mult), ("glu", ch))
                    split(next_unit(UNITS["in"] + 12 + 2 * ch))
                split(next_unit(UNITS["in"] + 15))
                split(next_unit(UNITS["in"] + 16))
                split(next_unit(UNITS["in"] + 17))
                dve.wait_ge(scalar_done, SL.value(l, "g_tanh"))
                D(ts(xs[:, C_G, :], tmp[:, 1, :], 0.5, 0.5, ALU.mult, ALU.add), "lo_gate")
                for j in range(J):
                    D(ts(kk[:, j, :], xs[:, C_K + j, :], pr("k_k", j), None, ALU.mult), "kk" if j == J - 1 else None)
                for j in range(J):
                    dve.wait_ge(scalar_done, SL.value(l, ("lora", 0, j)))
                D(ts(ld, ld, -HALF_DECAY, -HALF_DECAY, ALU.mult, ALU.add))
                settle()
                fl = lambda a: a.rearrange("p j t -> p (j t)")
                D(nc.vector.tensor_tensor_scan(fl(cl), c("scan", J * T), fl(ld), 0.0, ALU.mult, ALU.add))
                settle()
                for ct in range(2):
                    D(cp(mids[:, :, ct:ct + 1], cl[:, :, ct * P + 63:ct * P + 64]))
                settle()
                for ct in range(2):
                    for j in range(J):
                        D(ts(cl[:, j, ct * P:(ct + 1) * P], cl[:, j, ct * P:(ct + 1) * P], mids[:, j, ct:ct + 1], None, ALU.subtract),
                          "centred" if (ct, j) == (1, J - 1) else None)
                settle()
                D(tt(ld, cl, ld, ALU.subtract), "before")
                split(next_unit(UNITS["in"] + IN_CUT[0]))
                split(next_unit(UNITS["in"] + IN_CUT[0] + 1))
                for j in range(J):
                    dve.wait_ge(scalar_done, SL.value(l, ("lora", 1, j)))
                D(ts(aa, aa, 0.5, 0.5, ALU.mult, ALU.add))
                settle()
                for j in range(J):
                    D(ts(a_p[:, j, :], aa[:, j, :], -1.0, pr("k_a", j), ALU.add, ALU.mult))
                settle()
                D(stt(k2, a_p, 1.0, k2, ALU.add, ALU.mult))
                settle()
                for j in range(J):
                    D(stt(oT[:, j, :], xs[:, C_R + j, :], pr("r_k", j), k2[:, j, :], ALU.mult, ALU.mult), ("rkr", j))
                split(next_unit(UNITS["in"] + IN_CUT[1]))
                for j in range(J):
                    dve.wait_ge(scalar_done, SL.value(l, ("kk_norm", j)))
                D(ts(tmp, tmp, 1e-12, None, ALU.max))
                settle()
                D(nc.vector.reciprocal(tmp, tmp))
                settle()
                D(tt(kk, kk, tmp, ALU.mult))
                settle()
                dve.wait_ge(scalar_done, SL.value(l, "w_p"))
                D(stt(a_p, kk, -1.0, w_p, ALU.mult, ALU.mult))
                D(tt(b_p, kk, aa, ALU.mult))
                D(tt(k_p, k2, w_i, ALU.mult))
                D(tt(r_p, xs[:, C_R:C_R + J, :], w_c, ALU.mult))
                settle()
                D(tt(b_p, b_p, w_i, ALU.mult))
                dve.wait_ge(scalar_done, SL.value(l, "w_mid"))
                D(tt(wend[:, :, 0:1], w_c[:, :, P - 1:P], wmid1, ALU.mult))
                D(cp(wend[:, :, 1:2], w_c[:, :, TP - 1:TP]))
                D(cp(wend[:, :, 2:], w_c[:, :, TP + DEC_SEQ - 1:T:DEC_SEQ]), "primed")

                def b3(mask, n=J):
                    return mask.unsqueeze(1).to_broadcast([mask.shape[0], n, mask.shape[1]])

                def j3(a):
                    return a.rearrange("p (j s) -> p j s", j=J)

                for ct in range(2):
                    for kind in range(5):
                        for hh in range(2):
                            src = j3(bank[(kind * 2 + hh) % 8][:, 0:J * P])
                            dve.wait_ge(tensor_done, TL.value(l, ("pair", ct, kind, hh)))
                            if kind == 0:
                                D(cp(lab[:, hh], bank[hh][:, 0:J * P]))
                                D(tt(j3(tm[:, hh]), src, b3(c("level1", P)), ALU.mult), ("pair", ct, kind, hh))
                            elif kind == 1:
                                D(tt(j3(xm[:, hh]), src, b3(c("level1", P, at=P)), ALU.mult), ("pair", ct, kind, hh))
                            else:
                                D(tt(j3((lak, lrb, lrk)[kind - 2][:, hh]), src, b3(c("strict" if kind == 2 else "upper", P)), ALU.mult),
                                  ("pair", ct, kind, hh))
                        if kind == 1:
                            settle()
                            for hh in range(2):
                                D(tt(j3(tm[:, hh]), j3(tm[:, hh]), b3(ident), ALU.add), ("t0", ct, hh))
                                D(tt(j3(xm[:, hh]), j3(xm[:, hh]), b3(ident), ALU.add), ("x0", ct, hh))
                    lab6, lo6 = (a.rearrange("p h (j s) -> p (h j) s", j=J) for a in (lab, lo))
                    for m in range(len(LEVELS)):
                        if m:
                            dve.wait_ge(tensor_done, TL.value(l, ("y", ct, m - 1, 1)))
                        D(tt(lo6, lab6, b3(c("levels", P, at=m * P), 2 * J), ALU.mult), ("lo", ct, m))
                        for hh in range(2):
                            dve.wait_ge(tensor_done, TL.value(l, ("xinc", ct, m, hh)))
                            D(tt(xm[:, hh], xm[:, hh], bank[2 + hh][:, 0:J * P], ALU.add), ("x", ct, m, hh))
                            if m < len(LEVELS) - 1:
                                dve.wait_ge(tensor_done, TL.value(l, ("tinc", ct, m, hh)))
                                D(tt(tm[:, hh], tm[:, hh], bank[4 + hh][:, 0:J * P], ALU.add), ("t", ct, m, hh))
                        if ct == 0:
                            dve.wait_ge(tensor_done, TL.value(l, ("turn", m)))
                            D(tt(turned[:, m % 3, :], bank[6 + m % 2][:, 0:T], c("sin", T), ALU.mult), ("rope", m))
                            D(tt(qkv[:, m, :], qkv[:, m, :], c("cos", T), ALU.mult))
                            settle()
                            D(tt(qkv[:, m, :], qkv[:, m, :], turned[:, m % 3, :], ALU.add), "roped" if m == 2 * G - 1 else None)
                    dve.wait_ge(tensor_done, TL.value(l, ("o_state", ct)))
                    if ct:
                        D(tt(st, st, bank[5][:, 0:J * P], ALU.add))
                        settle()
                    for j in range(J):
                        s_ = slice(j * P, (j + 1) * P)
                        D(stt(st[:, s_], st[:, s_] if ct else bank[5][:, s_], wend[:, j, ct:ct + 1], heads, ALU.mult, ALU.mult),
                          ("state", ct) if j == J - 1 else None)

                sm_mask = c("s_masks", 6 * TS, rows=TS).rearrange("p (k s) -> p k s", k=6)
                i32 = ident[0:TS, 0:TS]
                for hh in range(2):
                    dve.wait_ge(tensor_done, TL.value(l, ("s_pair", hh)))
                    pv = bank[hh][0:TS, 0:5 * J * TS].rearrange("p (k j s) -> p k j s", k=5, j=J)
                    so = sm[0:TS, hh].rearrange("p k (j s) -> p k j s", j=J)
                    D(tt(so[:, 0], pv[:, 0], b3(sm_mask[:, 0]), ALU.mult))
                    D(tt(so[:, 1], pv[:, 0], b3(sm_mask[:, 1]), ALU.mult))
                    D(tt(so[:, 2:6], pv[:, 1:5], sm_mask[:, 2:6].unsqueeze(2).to_broadcast([TS, 4, J, TS]), ALU.mult), ("s_pair", hh))
                    settle()
                    D(tt(so[:, 0], so[:, 0], b3(i32), ALU.add))
                    D(tt(so[:, 2], so[:, 2], b3(i32), ALU.add), ("s_masked", hh))
                settle()
                dve.wait_ge(tensor_done, TL.value(l, "s_xinc"))
                D(tt(sm[0:TS, :, 2], sm[0:TS, :, 2], bank[1][0:TS, 0:2 * J * TS].rearrange("p (h c) -> p h c", h=2), ALU.add), "s_x")
                sel = c("s_batch", DEC_BATCH, rows=TS).unsqueeze(2).to_broadcast([TS, DEC_BATCH, P])

                def select(j):
                    s_ = slice(j * P, (j + 1) * P)
                    if j:
                        dve.wait_ge(tensor_done, TL.value(l, ("s_state", j - 1)))
                    D(tt(vsel[0:TS], b3(tok2[0:TS, 2, s_], DEC_BATCH), sel, ALU.mult))
                    dve.wait_ge(scalar_done, SL.value(l, ("u", 2)))
                    D(tt(usel[0:TS], b3(um2[0:TS, s_], DEC_BATCH), sel, ALU.mult), ("s_sel", j))

                def next_states(j):
                    dve.wait_ge(tensor_done, TL.value(l, ("s_state", j)))
                    w = wkv_s[:, j]
                    D(tt(w, w, bank[j][:, :].rearrange("p (b v) -> p b v", b=DEC_BATCH), ALU.add), ("s_state", j))
                    settle()
                    D(tt(w, w, wend[:, j, 2:].unsqueeze(2).to_broadcast([P, DEC_BATCH, HD]), ALU.mult), "wkv_s" if j == J - 1 else None)

                dve.wait_ge(scalar_done, SL.value(l, ("tok", 2, 2)))
                select(0)
                dve.wait_ge(tensor_done, TL.value(l, ("conv", "mean")))
                for ch in range(2):
                    D(stt(ycv[:, ch, :], bank[7][:, 0:T], -1.0 / 256, ycv[:, ch, :], ALU.mult, ALU.add),
                      "conv_mean" if ch else None)
                for j in range(J):
                    dve.wait_ge(tensor_done, TL.value(l, ("ln_mu", j)))
                    D(stt(oT[:, j, :], bank[(3, 5, 6)[j]][:, 0:T], -1.0 / HD, oT[:, j, :], ALU.mult, ALU.add), ("ln_mu", j))
                next_states(0)
                select(1)
                dve.wait_ge(scalar_done, SL.value(l, "conv_std"))
                D(nc.vector.reciprocal(yc2[:, 0, :], yc2[:, 0, :]))
                settle()
                for ch in range(2):
                    D(tt(ycv[:, ch, :], ycv[:, ch, :], yc2[:, 0, :], ALU.mult))
                settle()
                for ch in range(2):
                    D(ts(ycv[:, ch, :], ycv[:, ch, :], pr("conv_g", ch), pr("conv_beta", ch), ALU.mult, ALU.add),
                      "conv_norm" if ch else None)
                next_states(1)
                select(2)
                for j in range(J):
                    dve.wait_ge(scalar_done, SL.value(l, ("ln_var", j)))
                D(nc.vector.reciprocal(tmp_ln, tmp_ln))
                D(tt(bon, bon, xs[:, C_V:C_V + J, :], ALU.mult))
                settle()
                D(tt(oT, oT, tmp_ln, ALU.mult))
                settle()
                for j in range(J):
                    D(ts(oT[:, j, :], oT[:, j, :], pr("lnx_g", j), pr("lnx_b", j), ALU.mult, ALU.add))
                settle()
                D(tt(oT, oT, bon, ALU.add))
                next_states(2)
                dve.wait_ge(scalar_done, SL.value(l, "conv_tanh"))
                D(ts(yc2, yc2, 0.5, 0.5, ALU.mult, ALU.add))
                D(tt(h[:, 5:5 + J, :], oT, gz, ALU.mult))
                settle()
                D(tt(h[:, 0:2, :], yc2, ycv, ALU.mult), "rwkv_out")
                settle()
                dve.wait_ge(scalar_done, SL.value(l, "mix_hi"))
                low(h_lo[:, 0:2, :], h[:, 0:2, :], h_hi[:, 0:2, :])
                low(h_lo[:, 5:5 + J, :], h[:, 5:5 + J, :], h_hi[:, 5:5 + J, :])

                D(nc.vector.memset(qbd, 0.0))
                settle()
                q5 = qbd.rearrange("p g (b h t) -> p g b h t", b=DEC_BATCH, h=2)
                for hh in range(2):
                    r_ = slice(hh * HD, (hh + 1) * HD)
                    for g in range(G):
                        D(cp(q5[r_, g, :, hh, :], bt(qkv[r_, g, TP:T])), "qbd" if (hh, g) == (1, G - 1) else None)
                mask = c("mask", 2 * G * TP).rearrange("p (q g k) -> p q g k", q=2, g=G)

                def softmax_in(u, s_, rows=P):
                    settle()
                    D(nc.vector.tensor_reduce(astat[0:rows, 0, u:u + 1], s_, AX_X, ALU.max))
                    settle()
                    D(ts(astat[0:rows, 1, u:u + 1], astat[0:rows, 0, u:u + 1], -ATTN_SCALE, None, ALU.mult), ("nmax", u))

                def softmax_out(u, s_, name, rows=P):
                    dve.wait_ge(scalar_done, SL.value(l, ("exp", u)))
                    D(nc.vector.reciprocal(astat[0:rows, 3, u:u + 1], astat[0:rows, 2, u:u + 1]))
                    settle()
                    D(ts(s_, s_, astat[0:rows, 3, u:u + 1], None, ALU.mult), name)

                def unit(u):
                    qt = u % 2
                    return sp_[:, qt, 0:G * (qt + 1) * P]

                for u in range(4):
                    qt = u % 2
                    b = (2 * u) % 4
                    if u >= 2:
                        dve.wait_ge(tensor_done, TL.value(l, ("pT", u - 2, (u - 2) % 2)))
                    if qt == 0:
                        dve.wait_ge(tensor_done, TL.value(l, ("scores", u, 1)))
                        D(tt(unit(u).rearrange("p (g k) -> p g k", g=G), bank[b][:, 0:G * P].rearrange("p (g k) -> p g k", g=G),
                             mask[:, 0, :, 0:P], ALU.add), ("masked", u, 0))
                    else:
                        dve.wait_ge(tensor_done, TL.value(l, ("scores", u, 0)))
                        D(tt(sp_[:, 1, 0:2 * TP], bank[b][:, :], mask[:, 1, 0:2, :].rearrange("p g k -> p (g k)"), ALU.add),
                          ("masked", u, 0))
                        dve.wait_ge(tensor_done, TL.value(l, ("scores", u, 1)))
                        D(tt(sp_[:, 1, 2 * TP:], bank[b + 1][:, 0:TP], mask[:, 1, 2, :], ALU.add), ("masked", u, 1))
                    softmax_in(u, unit(u))
                    softmax_out(u, unit(u), ("probs", u))
                dve.wait_ge(tensor_done, TL.value(l, "s_scores"))
                D(tt(ss[0:64], bank[2][0:64, 0:G * (P + TS)], c("mask_s", G * (P + TS), rows=64), ALU.add), "s_scores")
                softmax_in(4, ss[0:64], 64)
                softmax_out(4, ss[0:64], "s_probs", 64)
                for u in range(NW):
                    split(UNITS["out"] + u)
                dve.wait_ge(scalar_done, SL.value(l, "attn_hi"))
                low(h_lo[:, 2:2 + G, :], h[:, 2:2 + G, :], h_hi[:, 2:2 + G, :], "attn_lo")

                for t in range(KT):
                    split(next_unit(UNITS["out"] + t))
                    dve.wait_ge(tensor_done, TL.value(l, ("out", "cols", t)))
                    D(tt(x[:, t, :], bank[t % 7][:, 0:T], x[:, t, :], ALU.add), ("x_out", t))

                dve.wait_ge(stored, store_value(l, "wkv_s"))
                D(nc.vector.memset(qz, 0.0), "qz_clear")
                normalise("xattn", x, h, rs, T, (h_hi, h_lo))
                for t in range(KT):
                    split(next_unit(UNITS["q"] + t))
                dve.wait_ge(mem_landed, 16 * l + 16)
                normalise("mem", memx, hm, mem_rs, MEM, (hm_hi, hm_lo))
                for t in range(KT):
                    split(next_unit(UNITS["kv"] + t))
                def two_units(hd):
                    if hd < 4:
                        return bank[hd][:, :].rearrange("p (q m) -> p q m", q=2), slice(2 * hd, 2 * hd + 2)
                    return bank[hd][:, 0:MEM].unsqueeze(1), slice(hd + 4, hd + 5)

                def row_max(hd):
                    src, u = two_units(hd)
                    dve.wait_ge(tensor_done, TL.value(l, ("xs", u.stop - 1)))
                    D(nc.vector.tensor_reduce(xstat[:, 0, u], src, AX_X, ALU.max))
                    settle()
                    D(ts(xstat[:, 1, u], xstat[:, 0, u], -X_SCALE, None, ALU.mult), ("xnmax", hd))

                def weigh(hd):
                    src, u = two_units(hd)
                    n = u.stop - u.start
                    dve.wait_ge(scalar_done, SL.value(l, ("xexp", u.stop - 1)))
                    D(nc.vector.reciprocal(xstat[:, 3, u], xstat[:, 2, u]))
                    settle()
                    D(tt(px[:, u, :], px[:, u, :], xstat[:, 3, u].unsqueeze(2).to_broadcast([P, n, MEM]), ALU.mult), ("xprobs", hd))

                row_max(0)
                for u in range(8):
                    if u % 2 == 0 and u < 6:
                        row_max(u // 2 + 1)
                    split(next_unit(UNITS["kv"] + KT + u))
                    if u % 2:
                        weigh(u // 2)
                for hd in (4, 5):
                    row_max(hd)
                    weigh(hd)
                for d in range(4):
                    dve.wait_ge(scalar_done, SL.value(l, ("ox", d)))
                    low(ox_lo[:, 2 * d:2 * d + 2, 0:TP], bank[d][:, :].rearrange("p (a c) -> p a c", a=2),
                        ox_hi[:, 2 * d:2 * d + 2, 0:TP], ("ox_lo", d))
                for half in range(2):
                    for n in range(2):
                        dve.wait_ge(scalar_done, SL.value(l, ("oxs_hi", half, 2 * n + 1)))
                        for hd in (2 * n, 2 * n + 1):
                            low(sample_out(ox_lo, half, hd), head_columns(half, hd), sample_out(ox_hi, half, hd),
                                ("oxs_lo", half, n) if hd % 2 else None)
                    if half == 0:
                        for u in range(NW):
                            split(UNITS["o"] + u)
                for t in range(KT):
                    split(next_unit(UNITS["o"] + t))
                    dve.wait_ge(tensor_done, TL.value(l, ("o", "cols", t)))
                    b = (5, 6, 7, 0, 1, 2, 3)[t % 7]
                    D(tt(x[:, t, :], bank[b][:, 0:T], x[:, t, :], ALU.add), ("x_o", t))
                ffn("ffn2")
            l = DEPTH - 1
            normalise("final", x, h, rs, T)

        return {"t": (TL.at, TL.per_layer()), "v": (VL.at, VL.per_layer()), "s": (SL.at, SL.per_layer()),
                "p": (PL.at, PL.per_layer()), "stores": stores}


def pack_columns(w, width=P):
    n, m = w.shape[1] // 256, 256 // width
    return w.reshape(KT, P, n, m, width).transpose(2, 1, 3, 0, 4).reshape(n, P, SLAB)


def pack_down(w):
    return w.reshape(FT, P, 2, 512).transpose(2, 0, 1, 3).reshape(FT // 2, 4, P, 512).transpose(0, 2, 1, 3).reshape(-1, P, SLAB)


def pack_ffn(i, l, tag):
    gate, up = (i[tag + n][l].reshape(D_MODEL, FT, P) for n in ("_w_gate", "_w_up"))
    both = pack_columns(np.stack([gate, up], 2).reshape(D_MODEL, 2 * D_FF))
    return np.concatenate([both, pack_down(i[tag + "_w_down"][l])], 0)


def in_order():
    conv, attn, rwkv = 0, 512, 512 + 1152
    starts = [rwkv + 1152, rwkv + 1280] + [rwkv + 384 + P * j for j in range(J)] + [rwkv + P * j for j in range(J)]
    starts += [rwkv + 768 + P * j for j in range(J)] + [conv, conv + 256, conv + 128, conv + 384]
    starts += [attn + P * j for j in range(9)]
    return np.concatenate([np.arange(s, s + P) for s in starts])


def pad(a):
    return np.concatenate([a, np.zeros(a.shape[:-1] + (SLAB - a.shape[-1],), a.dtype)], -1)


def pack_layer(i, l):
    k, v = ([i[f"cache_win{g}_{n}"][l] for g in (1, 2, 3)] for n in "kv")
    B = DEC_BATCH

    def phases(a, dil):
        return a.reshape(B, a.shape[1] // dil, dil, 2, HD).transpose(0, 2, 1, 3, 4)[:, :4]
    kc = np.concatenate([a.reshape(B, -1, P) for a in (k[0], phases(k[1], 4), phases(k[2], 16))], 1)
    vc = np.concatenate([a.reshape(B, -1, P) for a in (v[0], phases(v[1], 4), phases(v[2], 16))], 1)
    kc = kc.transpose(0, 2, 1).reshape(B // 2, 2, P, 896).transpose(0, 2, 1, 3).reshape(B // 2, P, 1792)
    vc = vc.reshape(B // 2, 2, 7, P, P).transpose(0, 3, 1, 2, 4).reshape(B // 2, P, 1792)
    memk = i["cache_mem_k"][l].reshape(B, MEM, KT, P).transpose(0, 3, 2, 1).reshape(B, P, SLAB)
    memv = i["cache_mem_v"][l].reshape(B, 2, P, D_MODEL).transpose(0, 2, 1, 3).reshape(B, P, SLAB)
    parts = {"ffn1": pack_ffn(i, l, "ffn1"), "in": pack_columns(i["w_in"][l][:, in_order()]), "wink": pad(kc), "winv": pad(vc),
             "out": pack_columns(i["w_out"][l]), "q": pack_columns(i["xattn_w_q"][l]), "kv": np.concatenate([
                 pack_columns(i["xattn_w_kv"][l][:, :D_MODEL]), pack_columns(i["xattn_w_kv"][l][:, D_MODEL:], 256)], 0),
             "memk": memk, "memv": memv, "o": pack_columns(i["xattn_w_o"][l]), "ffn2": pack_ffn(i, l, "ffn2")}
    return np.stack([parts[name][n] for name, n in ORDER])


def pack_small(i, l):
    c0 = in_order()[:NC_TILES * P] - 1664

    def cols(v):
        return v.reshape(-1, P).T
    lora = np.concatenate([np.concatenate([i["rwkv_w_up"][l], i["rwkv_a_up"][l]], 0), i["rwkv_g_up"][l]], 1)
    parts = [cols(i["ffn1_norm"][l]), cols(i["mix_norm"][l]), cols(i["xattn_norm"][l]), cols(i["mem_norm"][l]),
             cols(i["ffn2_norm"][l]), cols(i["final_norm"]), i["conv_w"][l].reshape(TAPS, 2, P).transpose(2, 1, 0).reshape(P, -1),
             cols(i["conv_b"][l]), cols(i["conv_ln_g"][l]), cols(i["conv_ln_b"][l]), cols(i["rwkv_shift_mix"][l][c0]),
             cols(i["rwkv_w0"][l]), cols(i["rwkv_a0"][l]), cols(i["rwkv_k_k"][l]), cols(i["rwkv_k_a"][l]),
             cols(i["rwkv_r_k"][l].reshape(-1)), cols(i["rwkv_lnx_g"][l]), cols(i["rwkv_lnx_b"][l]),
             i["state_shift"][l][:, c0].reshape(DEC_BATCH, NC_TILES, P).transpose(2, 1, 0).reshape(P, -1), lora]
    return np.concatenate(parts, 1)


def tokens(xp, xs_):
    both = np.concatenate([xp.reshape(TP, D_MODEL), xs_.reshape(TS, D_MODEL)], 0)
    return both.T.reshape(KT, P, T).transpose(1, 0, 2)


def pack(inputs):
    i = {k: np.asarray(v) for k, v in inputs.items()}
    s = i["state_wkv"].reshape(DEPTH, DEC_BATCH, J, 2, HD, HD)
    arrays = {
        "x_in": tokens(i["x_prompt"], i["x_sample"]),
        "mem_in": i["mem_prompt"].reshape(MEM, KT, P).transpose(2, 1, 0),
        "stream": np.stack([pack_layer(i, l) for l in range(DEPTH)]),
        "small": np.stack([pack_small(i, l) for l in range(DEPTH)], 1),
        "consts": constants(),
        "conv_hist": i["cache_conv"].reshape(DEPTH, DEC_BATCH, HIST, 2, P).transpose(0, 4, 3, 1, 2),
        "wkv_in": s.transpose(0, 3, 5, 2, 1, 4).reshape(DEPTH, P, J, DEC_BATCH, HD),
    }
    for g in (1, 2, 3):
        for n in "kv":
            arrays[f"win{g}{n}"] = i[f"cache_win{g}_{n}"].reshape(DEPTH, DEC_BATCH, -1)
    return {k: np.ascontiguousarray(v) for k, v in arrays.items()}


SHAPES_OUT = {
    "y": (P, KT, T), "conv": (DEPTH, P, 2, HIST + DEC_BATCH * HIST), "kv": (DEPTH, P, 2 * G, T),
    "shift": (DEPTH, P, NC_TILES, 1 + DEC_BATCH), "wkv_p": (DEPTH, P, J * P), "wkv_s": (DEPTH, P, J, DEC_BATCH, HD),
    "memk": (DEPTH, P, KT, MEM), "memv": (DEPTH, P, 2, D_MODEL),
}


def build(nc, arrays, known):
    ap = {k: nc.dram_tensor(k, a.shape, F32, kind="ExternalInput").ap() for k, a in arrays.items()}
    outs = {k: nc.dram_tensor("out_" + k, s, F32, kind="ExternalOutput").ap() for k, s in SHAPES_OUT.items()}
    copies = []
    for g in (1, 2, 3):
        for n in "kv":
            size = (CACHED[g - 1] - DEC_SEQ) * P
            dst = nc.dram_tensor(f"out_win{g}{n}", (DEPTH, DEC_BATCH, size), F32, kind="ExternalOutput").ap()
            copies.append((ap[f"win{g}{n}"][:, :, DEC_SEQ * P:], dst))
    return program(nc, ap["x_in"], ap["mem_in"], ap["stream"], ap["small"], ap["consts"], ap["conv_hist"], ap["wkv_in"],
                   copies, tuple(outs.values()), known)


def unpack(r):
    B, L = DEC_BATCH, DEPTH
    y = r["out_y"].transpose(2, 1, 0).reshape(T, D_MODEL)
    conv = r["out_conv"].transpose(0, 3, 2, 1).reshape(L, HIST + B * HIST, 256)
    kv = r["out_kv"].reshape(L, 2, HD, 2, G, T).transpose(3, 4, 0, 5, 1, 2)
    shift = r["out_shift"].transpose(0, 3, 2, 1).reshape(L, 1 + B, NC_TILES * P)
    c0 = in_order()[:NC_TILES * P] - 1664
    shift_ref = np.empty_like(shift)
    shift_ref[:, :, c0] = shift

    def states(a):
        n = a.shape[3]
        a = a.reshape(L, 2, HD, J, n, 2, HD)
        a = np.stack([a[:, hh, :, :, :, hh] for hh in range(2)], 1)
        return a.transpose(0, 4, 3, 1, 5, 2).reshape(L, n, 2 * J, HD, HD)
    wins_p, wins_s = [], []
    for g in range(G):
        for n in range(2):
            new = kv[n, g]
            keep = min(GROUPS[g][0], TP)
            wins_p.append(new[:, None, TP - keep:TP])
            old = r[f"out_win{g + 1}{'kv'[n]}"].reshape(L, B, -1, 2, HD)
            wins_s.append(np.concatenate([old, new[:, TP:].reshape(L, B, DEC_SEQ, 2, HD)], 2))
    memk = r["out_memk"].transpose(0, 3, 2, 1).reshape(L, 1, MEM, 4, 256)
    memv = r["out_memv"].transpose(0, 2, 1, 3).reshape(L, 1, MEM, 4, 256)
    out = (y[:TP].reshape(1, TP, D_MODEL), y[TP:].reshape(B, DEC_SEQ, D_MODEL), conv[:, None, :HIST], *wins_p,
           shift_ref[:, :1], states(r["out_wkv_p"].reshape(L, P, J, 1, P)), memk, memv,
           conv[:, HIST:].reshape(L, B, HIST, 256), *wins_s, shift_ref[:, 1:],
           r["out_wkv_s"].reshape(L, 2, HD, J, B, HD).transpose(0, 4, 3, 1, 5, 2).reshape(L, B, 2 * J, HD, HD))
    return tuple(np.ascontiguousarray(a) for a in out)


def kernel(**inputs):
    import concourse.bacc as bacc
    from concourse.bass_utils import run_bass_kernel_spmd

    arrays = pack(inputs)
    known = build(bacc.Bacc("TRN2", target_bir_lowering=False, num_devices=1), arrays, None)
    nc = bacc.Bacc("TRN2", target_bir_lowering=False, num_devices=1)
    build(nc, arrays, known)
    r = run_bass_kernel_spmd(nc, [arrays], core_ids=[0])
    return unpack(r.results[0])
```

```python
from contextlib import ExitStack

import numpy as np

import concourse.bass as bass
from concourse import mybir

F32 = mybir.dt.float32
F32R = mybir.dt.float32r
ALU = mybir.AluOpType
ACT = mybir.ActivationFunctionType
AX_X = mybir.AxisListType.X

P = 128
DEPTH, D_MODEL, D_FF = 2, 1024, 2816
TP, DEC_BATCH, DEC_SEQ = 256, 8, 4
TS = DEC_BATCH * DEC_SEQ
T = TP + TS
PAST_LEN = 1024
MEM = 256
KT = D_MODEL // P
FT = D_FF // P
HD = 64
TAPS = 31
HIST = TAPS - 1
GROUPS = ((128, 1), (512, 4), (2048, 16))
G = len(GROUPS)
CACHED = tuple(min(w, PAST_LEN) for w, _ in GROUPS)
ATTN_SCALE, X_SCALE = HD ** -0.5, 256 ** -0.5
NORM_EPS, CONV_EPS, LNX_EPS = 1e-6, 1e-5, 64e-5
HALF_DECAY = 0.5 * float(np.exp(-0.5))
NEG = -1e30
J = 3
LEVELS = (2, 4, 8, 16, 32, 64)

K_BANKS = (1, 2, 3, 6, 0, 7)
V_BANKS = (6, 7, 6, 7, 0, 1, 2, 3)
IN_CUT = (18, 20)
C_LO, C_G, C_K, C_R, C_V = 0, 1, 2, 5, 8
NC_TILES = 11
IN_TILES = 24

SLAB = 2048
NSLOT = 4
MEMK_EARLY = 6
K_EARLY = 4
PRESUM = {"mix": 4, "xattn": KT - 1, "ffn2": KT - 1}
STAGES = (("ffn1", 33), ("in", 12), ("wink", 4), ("winv", 4), ("out", 4), ("q", 4), ("kv", 8),
          ("memk", 8), ("memv", 8), ("o", 4), ("ffn2", 33))
UNIT = SLAB // 2
NW = 3
CACHES = ("wink", "winv", "memk", "memv")
ORDER = [(_name, _i) for _name, _n in STAGES for _i in range(_n)]
for _i in range(K_EARLY // 2):
    ORDER.remove(("kv", _i))
    ORDER.insert(ORDER.index(("q", 0)), ("kv", _i))
for _i in range(MEMK_EARLY):
    ORDER.remove(("memk", _i))
    ORDER.insert(ORDER.index(("kv", _i + K_EARLY // 2)) + 1, ("memk", _i))
SLAB_AT = {key: n for n, key in enumerate(ORDER)}
NSLAB = len(ORDER)
UNITS, NUNIT, UNIT_OF_SLAB = {}, 0, {}
for _n, (_name, _i) in enumerate(ORDER):
    if _name not in CACHES:
        UNITS.setdefault(_name, NUNIT)
        UNIT_OF_SLAB[_n] = NUNIT
        NUNIT += 2


def kv_unit(i):
    return UNIT_OF_SLAB[SLAB_AT["kv", i // 2]] + i % 2


SLAB_OF_UNIT = {u + half: (n, half) for n, u in UNIT_OF_SLAB.items() for half in range(2)}
RUN_ENDS = (UNITS["out"], UNITS["o"], NUNIT)
ROUNDS = NSLAB // NSLOT
REST = NSLAB - ROUNDS * NSLOT
ARENA = 23910
NSTORE = 9

PAR, NPAR = {}, 0
for _name, _n in (("ffn1", 8), ("mix", 8), ("xattn", 8), ("mem", 8), ("ffn2", 8), ("final", 8), ("conv_w", 2 * TAPS),
                  ("conv_b", 2), ("conv_g", 2), ("conv_beta", 2), ("shift", NC_TILES), ("w0", J), ("a0", J),
                  ("k_k", J), ("k_a", J), ("r_k", J), ("lnx_g", J), ("lnx_b", J), ("state_shift", NC_TILES * 8),
                  ("lora", 2 * J * P)):
    PAR[_name] = NPAR
    NPAR += _n

CON, NCON = {}, 0
for _name, _n in (("ident", P), ("ones", P), ("heads", P), ("turn", P), ("cos", T), ("sin", T), ("mask", 2 * G * TP),
                  ("mask_s", G * (P + TS)), ("level1", 2 * P), ("levels", len(LEVELS) * P), ("strict", P), ("upper", P),
                  ("s_masks", 6 * TS), ("s_batch", DEC_BATCH), ("scan", J * T)):
    CON[_name] = NCON
    NCON += _n


def constants():
    c = np.zeros((P, NCON), np.float32)

    def put(name, a, rows=P):
        a = np.asarray(a, np.float32).reshape(rows, -1)
        c[:rows, CON[name]:CON[name] + a.shape[1]] = a

    i = np.arange(P)
    put("ident", np.eye(P))
    put("ones", np.ones((P, P)))
    put("heads", i[:, None] // HD == i[None] // HD)
    turn = np.zeros((P, P))
    for m in range(P):
        turn[m + 32 if m % HD < 32 else m - 32, m] = -1.0 if m % HD < 32 else 1.0
    put("turn", turn)
    half = HD // 2
    inv = np.power(np.float32(10000.0), -np.arange(half, dtype=np.float32) / np.float32(half)).astype(np.float32)
    pos = np.concatenate([np.arange(TP), np.tile(PAST_LEN + np.arange(DEC_SEQ), DEC_BATCH)]).astype(np.float32)
    ang = (inv[i % half][:, None] * pos[None]).astype(np.float32)
    put("cos", np.cos(ang))
    put("sin", np.sin(ang))
    mask = np.full((P, 2, G, TP), NEG)
    for qt in range(2):
        q = qt * P + i[:, None]
        k = np.arange(TP)[None]
        for g, (win, dil) in enumerate(GROUPS):
            mask[:, qt, g][(q >= k) & (q - k <= win) & ((q - k) % dil == 0)] = 0
    put("mask", mask)
    ms = np.full((DEC_BATCH, 2, DEC_SEQ, G, P + TS), NEG)
    key = np.arange(P)
    for b in range(DEC_BATCH):
        for t in range(DEC_SEQ):
            ms[b, :, t, 0, :P][:, key >= t] = 0
            ms[b, :, t, 1, :P] = 0
            ms[b, :, t, 2, :P][:, key // 64 == t % 2] = 0
            ms[b, :, t, 0, P + DEC_SEQ * b:P + DEC_SEQ * b + t + 1] = 0
            ms[b, :, t, 1:, P + DEC_SEQ * b + t] = 0
    put("mask_s", ms, rows=64)
    t, s = i[:, None], i[None]

    def level(m):
        return (t // (2 * m) == s // (2 * m)) & (t % (2 * m) >= m) & (s % (2 * m) < m)

    put("level1", np.concatenate([level(1), level(1).T], 1))
    put("levels", np.concatenate([level(m) for m in LEVELS], 1))
    put("strict", (t < s))
    put("upper", (t <= s))
    same = (t // DEC_SEQ == s // DEC_SEQ)
    small = [level(1), level(2), level(1).T, same & (t < s), same & (t <= s), same & (t <= s)]
    put("s_masks", np.concatenate([m[:TS, :TS] for m in small], 1), rows=TS)
    put("s_batch", i[:TS, None] // DEC_SEQ == np.arange(DEC_BATCH)[None], rows=TS)
    keep = np.ones((P, J, T))
    keep[:, :, 0:TP:P] = 0
    keep[:, :, TP::DEC_SEQ] = 0
    put("scan", keep)
    return c


class Line:

    def __init__(self, sem, known):
        self.sem, self.n, self.at, self.last = sem, 0, {}, None
        self.known, self.total = known if known else ({}, 1)

    def done(self, ins, name=None):
        if ins is not self.last:
            self.n += 1
            ins.then_inc(self.sem, 1)
            self.last = ins
        if name is not None:
            assert self.at.setdefault(name, self.n) == self.n, name
        return ins

    def begin_layer(self):
        self.n = 0

    def per_layer(self):
        return max((c for name, c in self.at.items() if name[0] != "final"), default=0)

    def value(self, l, name):
        return l * self.total + (self.total + (self.known.get(name, 1) if self.known else 1))

    def value_before(self, l, name):
        return l * self.total + (self.known.get(name, 1) if self.known else 1)

    def so_far(self, l):
        return l * self.total + (self.total + self.n)


def program(nc, x_in, mem_in, stream, small, consts, conv_hist, wkv_in, copies, outs, known=None):
    (y_out, conv_out, kv_out, shift_out, wkv_p_out, wkv_s_out, memk_out, memv_out) = outs
    known = known or {}
    with ExitStack() as ctx:
        def sb(name, shape):
            return ctx.enter_context(nc.sbuf_tensor(name, shape, F32))

        def sem(name):
            return ctx.enter_context(nc.semaphore(name))

        bank = [ctx.enter_context(nc.psum_tensor(f"bank{i}", [P, 512], F32)) for i in range(8)]

        slots = sb("slots", [P, NSLOT, SLAB])
        x = sb("x", [P, KT, T])

        def split_at(name, shape, offset):
            return nc.alloc_sbuf_tensor_at(name, shape, F32R, offset=offset)

        h_mem = sb("h_mem", [P, 2, KT, T])
        h_at = nc.sbuf_base - 2 * KT * T * 4
        h, h_free = h_mem[:, 0], h_mem[:, 1]
        h_lo, h_hi = split_at("h_lo", [P, KT, T], h_at), split_at("h_hi", [P, KT, T], h_at + KT * T * 4)
        w_hi = ctx.enter_context(nc.sbuf_tensor("w_hi", [P, NW, UNIT], F32R))
        w_lo = ctx.enter_context(nc.sbuf_tensor("w_lo", [P, NW, UNIT], F32R))
        par_all = sb("par_all", [P, DEPTH, NPAR])
        con = sb("con", [P, NCON])
        rs = sb("rs", [P, T])
        halves = sb("halves", [P, 2 * J])[:]
        warm = sb("warm", [P, 1])[:]
        mem_rs = sb("mem_rs", [P, MEM])[:]
        arena = sb("arena", [P, ARENA])
        arena_at = nc.sbuf_base - ARENA * 4

        def c(name, n, rows=P, at=0):
            return con[0:rows, CON[name] + at:CON[name] + at + n]

        ident, ones, heads = c("ident", P), c("ones", P), c("heads", P)

        top = [0]

        def take(*dims):
            n = int(np.prod(dims))
            v = arena[:, top[0]:top[0] + n]
            top[0] += n
            assert top[0] <= ARENA, top[0]
            if len(dims) == 1:
                return v
            names = "abcd"[:len(dims)]
            return v.rearrange(f"p ({' '.join(names)}) -> p {' '.join(names)}",
                               **{k: d for k, d in zip(names[1:], dims[1:])})

        def over(name, view_start, *dims):
            return split_at(name, [P, *dims], arena_at + view_start * 4)

        sq = take(KT, T)
        hid_hi = over("hid_hi", top[0], FT, T)
        top[0] += FT * T
        hid_lo = over("hid_lo", top[0], FT, T)
        hid = take(FT, T)
        th = take(2, T)
        th2 = take(2, T)
        top[0] = KT * T
        qx = take(KT, T)
        ox_hi = over("ox_hi", top[0], KT, T)
        top[0] += KT * T
        ox_lo, hm_hi = over("ox_lo", top[0], KT, T), over("hm_hi", top[0], KT, MEM)
        memx = sq.rearrange("p k t -> p (k t)")[:, 0:KT * MEM].rearrange("p (k t) -> p k t", k=KT)
        top[0] += KT * T
        hm_lo = over("hm_lo", top[0], KT, MEM)
        hm = take(KT, MEM)
        oxs = hm.rearrange("p k t -> p (k t)").rearrange("p (a c) -> p a c", a=2)
        kx = take(KT, MEM)
        vx = take(2, 4 * MEM)
        pxT = take(4, 2, TP)
        px = take(10, MEM)
        qz = take(KT, DEC_BATCH, 32)
        pxsT = take(2, 2, P)
        xstat = take(4, 10)
        top[0] = 0
        xs = take(NC_TILES, T)
        qkv = take(3 * G, T)
        up = take(2, HIST + TP)
        us = take(2, DEC_BATCH * (HIST + DEC_SEQ))
        a_p, b_p, k_p, r_p = (take(J, T) for _ in range(4))
        gz, oT = (take(J, T) for _ in range(2))
        bon = h_free[:, 0:J, :]
        turned = h_free[:, J, :]
        wend = take(J, 2 + DEC_BATCH)
        wmid1 = take(J, 1)
        mids = take(J, 2)
        shift_o = take(NC_TILES, 1 + DEC_BATCH)
        base2 = top[0]
        f = take(NC_TILES, 1 + TP + DEC_BATCH * (1 + DEC_SEQ))
        wid = 1 + TP + DEC_BATCH * (1 + DEC_SEQ)
        ld, cl, w_c, w_p, w_i = (take(J, T) for _ in range(5))
        aa, kk = (take(J, T) for _ in range(2))
        k2 = xs[:, C_K:C_K + J, :]
        top[0] = base2
        tmp = take(J, T)
        top[0] = base2
        lab0, tm0, xm0, lo0, ym0, lak, lrb, lrk = (take(2, J * P) for _ in range(8))
        rm, um, st = (take(J * P) for _ in range(3))
        tok = take(3, J * P)
        pairs_of = [a.rearrange("p (h c) -> p h c", h=2) for a in
                    (xs[:, 0:8, :].rearrange("p c t -> p (c t)")[:, i * 2 * J * P:(i + 1) * 2 * J * P] for i in range(3))]
        ym1 = h_free[:, J + 1:, :].rearrange("p c t -> p (c t)")[:, 0:2 * J * P].rearrange("p (h c) -> p h c", h=2)
        lab, tm, xm = ([a, b] for a, b in zip((lab0, tm0, xm0), pairs_of))
        lo, ym = [lo0, tok[:, 0:2, :]], [ym0, ym1]
        wkv_s = take(J, DEC_BATCH, HD)
        ycv, prod = take(2, T), take(2, 2, T)
        top[0] = base2
        usel, vsel = take(DEC_BATCH, P), take(DEC_BATCH, P)
        sm = take(2, 6, J * TS)
        sy = take(2, J * TS)
        tmp_s, rm2, um2 = take(J * TS), take(J * P), take(J * P)
        tok2 = take(3, J * P)
        tmp_ln = take(J, T)
        yc2 = take(2, T)
        assert top[0] <= base2 + 18 * J * P
        top[0] = base2
        vtok = tok[:, 0:2, :].rearrange("p c (g d) -> p c g d", g=G)
        vtok_s = tok[:, 2, :].rearrange("p (g d) -> p g d", g=G)
        sp_ = take(2, G * TP)
        spT = take(2, G, 2, P)
        qbd = h_free[:, J + 1, 0:G * 64].rearrange("p (g c) -> p g c", g=G)
        ss = take(G * (P + TS))
        ssT, ssn = take(G, 64), take(G, 64)
        psT, psn = take(G, 64), take(G, 64)
        astat = take(4, 6)
        assert top[0] <= base2 + 18 * J * P

        us4 = us.rearrange("p a (b t) -> p a b t", b=DEC_BATCH)
        f_p = f[:, :, 0:1 + TP]
        f_s = f[:, :, 1 + TP:].rearrange("p c (b t) -> p c b t", b=DEC_BATCH)

        def bt(ap):
            return ap.rearrange("p (b t) -> p b t", t=DEC_SEQ)

        tensor_done, vector_done, scalar_done = sem("tensor_done"), sem("vector_done"), sem("scalar_done")
        pool_done = sem("pool_done")
        slab_landed = [sem(f"slab_landed{i}") for i in range(NSLOT)]
        start_landed = sem("start_landed")
        par_landed = sem("par_landed")
        con_landed = sem("con_landed")
        layer_landed = sem("layer_landed")
        wkv_landed = sem("wkv_landed")
        mem_landed = sem("mem_landed")
        stored = sem("stored")
        copied = sem("copied")
        TL, VL, SL, PL = (Line(s, known.get(n)) for s, n in ((tensor_done, "t"), (vector_done, "v"), (scalar_done, "s"),
                                                             (pool_done, "p")))
        store_known = known.get("stores", {})
        stores = {}

        block = ctx.enter_context(nc.Block())

        @block.sync
        def _(sp):
            sp.dma_start(x[:], x_in).then_inc(start_landed, 16)
            first = CON["turn"]
            sp.dma_start(con[:, 0:first], consts[:, 0:first]).then_inc(start_landed, 16)
            gains = PAR["conv_w"]
            sp.dma_start(par_all[:, :, 0:gains], small[:, :, 0:gains]).then_inc(par_landed, 16)
            flat = stream.rearrange("l n p c -> (l n) p c")
            for l in range(DEPTH):
                for n in range(NSLAB):
                    held = n - NSLOT if n >= NSLOT else n + NSLOT * (ROUNDS - (n >= REST))
                    line, name = (VL, ("lo", UNIT_OF_SLAB[held] + 1)) if held in UNIT_OF_SLAB else (TL, ("slab", held))
                    sp.wait_ge(line.sem, line.value(l, name) if n >= NSLOT else line.value_before(l, name))
                    sp.dma_start(slots[:, n % NSLOT, :], stream[l, n]).then_inc(slab_landed[n % NSLOT], 16)
                    if l == 0 and n == NSLOT + 4:
                        sp.dma_start(con[:, first:], consts[:, first:]).then_inc(con_landed, 16)
                        sp.dma_start(par_all[:, :, gains:], small[:, :, gains:]).then_inc(con_landed, 16)
                    if n % 5 == 4 and n // 5 < len(copies):
                        src, dst = copies[n // 5]
                        sp.dma_start(dst[l], src[l]).then_inc(copied, 16)
            sp.wait_ge(copied, 16 * 6 * DEPTH)

        @block.gpsimd
        def _(pool):
            n_stores = [0]

            def store(dst, src, name):
                pool.dma_start(dst, src).then_inc(stored, 16)
                n_stores[0] += 1
                stores[name] = n_stores[0]

            pool.sem_inc(pool_done, PL.total)
            pool.wait_ge(con_landed, 32)
            for l in range(DEPTH):
                n_stores[0] = 0
                PL.begin_layer()

                def presum(tag):
                    for k in range(1, PRESUM[tag]):
                        pool.wait_ge(scalar_done, SL.value(l, (tag, "sq", k)))
                        if k > 1:
                            pool.wait_ge(pool_done, PL.value(l, (tag, "added", k - 1)))
                        PL.done(nc.gpsimd.tensor_tensor(sq[:, 0, :], sq[:, 0, :], sq[:, k, :], ALU.add), (tag, "added", k))

                presum("mix")
                pool.wait_ge(vector_done, VL.value(l, ("ffn1", "x", 1)))
                pool.wait_ge(tensor_done, TL.value(l, ("ffn1", "down", 1)))
                pool.dma_start(us4[:, :, :, 0:HIST], conv_hist[l]).then_inc(layer_landed, 16)

                pool.wait_ge(vector_done, VL.value(l, ("glu", 1)))
                par = par_all[:, l, :]

                def products(tap):
                    for ch in range(2):
                        w = par[:, PAR["conv_w"] + ch * TAPS + tap:PAR["conv_w"] + ch * TAPS + tap + 1]
                        bias = par[:, PAR["conv_b"] + ch:PAR["conv_b"] + ch + 1]
                        out = prod[:, tap % 2, ch, :] if tap else ycv[:, ch, :]
                        for o, i in ((out[:, 0:TP], up[:, ch, tap:tap + TP]), (bt(out[:, TP:T]), us4[:, ch, :, tap:tap + DEC_SEQ])):
                            if tap:
                                p_ = nc.gpsimd.tensor_scalar(o, i, w, None, ALU.mult)
                            else:
                                p_ = nc.gpsimd.tensor_scalar(o, i, w, bias, ALU.mult, ALU.add)
                            PL.done(p_)
                    PL.done(p_, ("products", tap))

                products(0)
                products(1)
                for tap in range(1, TAPS):
                    if tap + 1 < TAPS:
                        if tap > 1:
                            pool.wait_ge(pool_done, PL.value(l, ("summed", tap - 1)))
                        products(tap + 1)
                    pool.wait_ge(pool_done, PL.value(l, ("products", tap)))
                    if tap > 1:
                        pool.wait_ge(pool_done, PL.value(l, ("summed", tap - 1)))
                    PL.done(nc.gpsimd.tensor_tensor(ycv, ycv, prod[:, tap % 2], ALU.add), ("summed", tap))

                store(conv_out[l, :, :, 0:HIST], up[:, :, TP:TP + HIST], "conv_p")
                store(conv_out[l, :, :, HIST:].rearrange("p a (b t) -> p a b t", b=DEC_BATCH)[:, 0],
                      us4[:, 0, :, DEC_SEQ:], "conv_s0")
                store(conv_out[l, :, :, HIST:].rearrange("p a (b t) -> p a b t", b=DEC_BATCH)[:, 1],
                      us4[:, 1, :, DEC_SEQ:], "conv_s1")
                store(shift_out[l], shift_o, "shift")
                pool.wait_ge(vector_done, VL.value(l, "roped"))
                pool.wait_ge(scalar_done, SL.value(l, ("in", IN_TILES - 1)))
                store(kv_out[l], qkv[:, G:3 * G, :], "kv")
                pool.wait_ge(vector_done, VL.value(l, ("state", 1)))
                store(wkv_p_out[l], st, "wkv_p")
                pool.wait_ge(vector_done, VL.value(l, "wkv_s"))
                store(wkv_s_out[l], wkv_s, "wkv_s")
                pool.wait_ge(vector_done, VL.value(l, "rwkv_out"))
                pool.dma_start(memx, mem_in).then_inc(mem_landed, 16)
                presum("xattn")
                pool.wait_ge(scalar_done, SL.value(l, ("kx", KT - 1)))
                store(memk_out[l], kx, "memk")
                pool.wait_ge(scalar_done, SL.value(l, ("vx", 7)))
                store(memv_out[l], vx, "memv")
                presum("ffn2")
            assert n_stores[0] == NSTORE
            pool.wait_ge(vector_done, VL.value(DEPTH - 1, ("final", "h", KT - 1)))
            pool.dma_start(y_out, h[:]).then_inc(stored, 16)
            pool.wait_ge(stored, 16 * (NSTORE * DEPTH + 1))

        def landed(l, n):
            s = n % NSLOT
            per = ROUNDS + (s < REST)
            return slab_landed[s], l * (16 * per) + 16 * (n // NSLOT + 1)

        def raw_unit(u):
            n, half = SLAB_OF_UNIT[u]
            return slots[:, n % NSLOT, half * UNIT:(half + 1) * UNIT]

        def next_unit(u):
            return u + NW if all(not u < end <= u + NW for end in RUN_ENDS) else None

        def unit_head(u):
            return u // 2 if u < 8 else u - 4

        def sample_out(a, half, hd):
            o = TP + half * TS // 2
            return a[:, 2 * hd:2 * hd + 2, o:o + TS // 2].rearrange("p a (b t) -> p a b t", t=DEC_SEQ)

        def head_columns(half, hd):
            a = bank[2 * half + hd // 2][:, (hd % 2) * 2 * P:(hd % 2 + 1) * 2 * P]
            return a.rearrange("p (a b c) -> p a b c", a=2, b=4)[:, :, :, 4 * hd:4 * hd + 4]

        def reached(l, line, name):
            return line.sem, line.value(l, name)

        def store_value(l, name):
            return l * (16 * NSTORE) + 16 * store_known.get(name, 1)

        @block.tensor
        def _(pe):
            pe.sem_inc(tensor_done, TL.total)
            pe.wait_ge(start_landed, 32)
            mm = nc.tensor.matmul
            for l in range(DEPTH):
                TL.begin_layer()
                free = [None] * 8

                def claim(b, released_by):
                    if free[b] is not None:
                        pe.wait_ge(*reached(l, *free[b]))
                    free[b] = released_by

                def arrived(n):
                    pe.wait_ge(*landed(l, n))
                    return slots[:, n % NSLOT, :]

                def split(u, k):
                    pe.wait_ge(vector_done, VL.value(l, ("lo", u)))
                    return tuple(w[:, u % NW, :].rearrange("p (k c) -> p k c", k=k) for w in (w_hi, w_lo))

                def mm3(out, lhs, rhs, start, stop):
                    mm(out, lhs[0], rhs[0], start=start, stop=False)
                    mm(out, lhs[0], rhs[1], start=False, stop=False)
                    return mm(out, lhs[1], rhs[0], start=False, stop=stop)

                def sum_squares(tag, n=T, squares=sq):
                    first = PRESUM.get(tag, 1)
                    claim(7, (SL, (tag, "rms")))
                    if first > 1:
                        pe.wait_ge(pool_done, PL.value(l, (tag, "added", first - 1)))
                    for k in (0, *range(first, KT)):
                        pe.wait_ge(scalar_done, SL.value(l, (tag, "sq", k)))
                        i = mm(bank[7][:, 0:n], ones, squares[:, k, 0:n], start=k == 0, stop=k == KT - 1)
                    TL.done(i, (tag, "ss"))

                def ffn(tag):
                    sum_squares(tag)
                    for t in range(FT):
                        gb, ub = (t % 2) * 2, (t % 2) * 2 + 1
                        claim(gb, (VL, (tag, "gated", t)))
                        claim(ub, (VL, (tag, "hid", t)))
                        for b, o in ((gb, 0), (ub, 1)):
                            u = UNITS[tag] + 2 * t + o
                            hi, lo_ = split(u, KT)
                            for k in range(KT):
                                if t == 0 and o == 0:
                                    pe.wait_ge(vector_done, VL.value(l, (tag, "h_lo", k)))
                                i = mm3(bank[b][:, 0:T], (hi[:, k, :], lo_[:, k, :]), (h_hi[:, k, :], h_lo[:, k, :]),
                                        k == 0, k == KT - 1)
                            TL.done(i, ("unit", u))
                            TL.done(i, (tag, "up" if o else "gate", t))
                    for q in range(2 * FT):
                        half, t = divmod(q, FT)
                        u = UNITS[tag] + 2 * FT + q // 2
                        if q % 2 == 0:
                            hi, lo_ = split(u, 2)
                        if half == 0:
                            pe.wait_ge(vector_done, VL.value(l, (tag, "hid_lo", t)))
                        for d in range(4):
                            b = 4 + d if half == 0 else d
                            if t == 0:
                                claim(b, (VL, (tag, "x", half)))
                            s_ = slice(d * P, (d + 1) * P)
                            i = mm3(bank[b][:, 0:T], (hi[:, q % 2, s_], lo_[:, q % 2, s_]), (hid_hi[:, t, :], hid_lo[:, t, :]),
                                    t == 0, t == FT - 1)
                        if q % 2 == 1:
                            TL.done(i, ("unit", u))
                        if t == FT - 1:
                            TL.done(i, (tag, "down", half))

                def columns(tag, first, tiles, src, src_name, banks, reader):
                    for t in tiles:
                        b = banks[t % len(banks)]
                        claim(b, reader(t))
                        hi, lo_ = split(first + t, KT)
                        for k in range(KT):
                            if t == 0:
                                pe.wait_ge(*reached(l, *src_name(k)))
                            i = mm3(bank[b][:, 0:src[0].shape[2]], (hi[:, k, :], lo_[:, k, :]), (src[0][:, k, :], src[1][:, k, :]),
                                    k == 0, k == KT - 1)
                        TL.done(i, ("unit", first + t))
                        TL.done(i, (tag, "cols", t))

                ffn("ffn1")

                pe.wait_ge(con_landed, 32)

                sum_squares("mix")

                def in_reader(t):
                    if t in (11, 13):
                        return VL, ("glu", (t - 11) // 2)
                    return SL, ("in", t)

                def project(tiles):
                    columns("in", UNITS["in"], tiles, (h_hi, h_lo), lambda k: (VL, ("mix", "h_lo", k)), range(7), in_reader)

                project(range(IN_CUT[0]))

                lora = par_all[:, l, PAR["lora"]:PAR["lora"] + 2 * J * P]
                pe.wait_ge(scalar_done, SL.value(l, "lo_tanh"))
                pe.wait_ge(vector_done, VL.value(l, "lo_gate"))
                for kind, rows, off, src in ((0, slice(0, 64), 0, tmp[0:64, 0, :]), (1, slice(64, P), 0, xs[64:P, C_LO, :]),
                                             (2, slice(0, P), J * P, xs[:, C_G, :])):
                    for j in range(J):
                        b = (kind * J + j) % 7
                        claim(b, (SL, ("lora", kind, j)))
                        i = mm(bank[b][:, 0:T], lora[rows, off + j * P:off + (j + 1) * P], src, start=True, stop=True)
                        TL.done(i, ("lora", kind, j))

                project(range(IN_CUT[0], IN_CUT[1]))
                for j in range(J):
                    claim(j, (SL, ("kk_norm", j)))
                    pe.wait_ge(scalar_done, SL.value(l, "kk_sq"))
                    TL.done(mm(bank[j][:, 0:T], heads, tmp[:, j, :], start=True, stop=True), ("kk_ss", j))
                project(range(IN_CUT[1], IN_TILES))
                for j in range(J):
                    claim(3 + j, (SL, ("bonus", j)))
                    pe.wait_ge(vector_done, VL.value(l, ("rkr", J - 1)))
                    TL.done(mm(bank[3 + j][:, 0:T], heads, oT[:, j, :], start=True, stop=True), ("bonus", j))

                def vt(j, ct):
                    return xs[:, C_V + j, ct * P:(ct + 1) * P] if ct < 2 else xs[:, C_V + j, TP:T]

                def tile(a, j, ct):
                    return a[:, j, ct * P:(ct + 1) * P] if ct < 2 else a[:, j, TP:T]

                def hh_rows(a, hh):
                    return a[hh * HD:(hh + 1) * HD]

                pair_of = ((a_p, b_p), (b_p, a_p), (k_p, a_p), (b_p, r_p), (k_p, r_p))

                def pair(ct, kind, banks):
                    for hh in range(2):
                        claim(banks[hh], (VL, ("pair", ct, kind, hh)))
                        for j in range(J):
                            i = mm(bank[banks[hh]][:, j * P:(j + 1) * P], hh_rows(tile(pair_of[kind][0], j, ct), hh),
                                   hh_rows(tile(pair_of[kind][1], j, ct), hh), start=True, stop=True)
                        TL.done(i, ("pair", ct, kind, hh))

                def token_rows(ct, kind, b):
                    claim(b, (SL, ("tok", ct, kind)))
                    for j in range(J):
                        s_ = vt(j, ct) if kind == 2 else tile((b_p, k_p)[kind], j, ct)
                        i = nc.tensor.transpose(bank[b][:, j * P:(j + 1) * P], s_, ident)
                    TL.done(i, ("tok", ct, kind))

                def level_y(ct, m):
                    for hh in range(2):
                        b = 4 * ct + hh
                        claim(b, (SL, ("y", ct, m, hh)))
                        pe.wait_ge(vector_done, VL.value(l, ("lo", ct, m)))
                        pe.wait_ge(vector_done, VL.value(l, ("x", ct, m - 1, hh) if m else ("x0", ct, hh)))
                        for j in range(J):
                            s_ = slice(j * P, (j + 1) * P)
                            i = mm(bank[b][:, s_], lo[ct][:, hh, s_], xm[ct][:, hh, s_], start=True, stop=True)
                        TL.done(i, ("y", ct, m, hh))

                def level_inc(ct, m):
                    for hh in range(2):
                        b = 4 * ct + 2 + hh
                        claim(b, (VL, ("x", ct, m, hh)))
                        pe.wait_ge(scalar_done, SL.value(l, ("y", ct, m, hh)))
                        pe.wait_ge(vector_done, VL.value(l, ("t", ct, m - 1, hh) if m else ("t0", ct, hh)))
                        for j in range(J):
                            s_ = slice(j * P, (j + 1) * P)
                            i = mm(bank[b][:, s_], tm[ct][:, hh, s_], ym[ct][:, hh, s_], start=True, stop=True)
                        TL.done(i, ("xinc", ct, m, hh))
                        if m == len(LEVELS) - 1:
                            continue
                        b = 4 * ct + hh
                        claim(b, (VL, ("t", ct, m, hh)))
                        for j in range(J):
                            s_ = slice(j * P, (j + 1) * P)
                            i = mm(bank[b][:, s_], ym[ct][:, hh, s_], tm[ct][:, hh, s_], start=True, stop=True)
                        TL.done(i, ("tinc", ct, m, hh))

                def right_sides(ct):
                    claim(6, (SL, ("r", ct)))
                    pe.wait_ge(scalar_done, SL.value(l, ("tok", ct, 2)))
                    pe.wait_ge(vector_done, VL.value(l, ("pair", ct, 2, 1)))
                    if ct:
                        pe.wait_ge(vector_done, VL.value(l, ("state", 0)))
                    for j in range(J):
                        o = bank[6][:, j * P:(j + 1) * P]
                        if ct:
                            mm(o, tile(a_p, j, ct), st[:, j * P:(j + 1) * P], start=True, stop=False, skip_group_check=True)
                        for hh in range(2):
                            i = mm(o[:, hh * HD:(hh + 1) * HD], lak[:, hh, j * P:(j + 1) * P],
                                   tok[:, 2, j * P + hh * HD:j * P + (hh + 1) * HD], start=ct == 0, stop=True,
                                   skip_group_check=True)
                    TL.done(i, ("r", ct))

                def solved(ct):
                    claim(7, (SL, ("u", ct)))
                    pe.wait_ge(scalar_done, SL.value(l, ("r", ct)))
                    pe.wait_ge(vector_done, VL.value(l, ("x", ct, len(LEVELS) - 1, 1)))
                    for j in range(J):
                        for hh in range(2):
                            s_ = slice(j * P + hh * HD, j * P + (hh + 1) * HD)
                            i = mm(bank[7][:, s_], xm[ct][:, hh, j * P:(j + 1) * P], rm[:, s_], start=True, stop=True)
                    TL.done(i, ("u", ct))

                def outputs_and_state(ct):
                    claim(4, (SL, ("o", ct)))
                    claim(5, (VL, ("state", ct)))
                    pe.wait_ge(scalar_done, SL.value(l, ("u", ct)))
                    pe.wait_ge(scalar_done, SL.value(l, ("tok", ct, 1)))
                    pe.wait_ge(vector_done, VL.value(l, ("pair", ct, 4, 1)))
                    for j in range(J):
                        o = bank[4][:, j * P:(j + 1) * P]
                        if ct:
                            mm(o, st[:, j * P:(j + 1) * P], tile(r_p, j, ct), start=True, stop=False, skip_group_check=True)
                        for hh in range(2):
                            s_ = slice(j * P + hh * HD, j * P + (hh + 1) * HD)
                            oo = bank[4][hh * HD:(hh + 1) * HD, j * P:(j + 1) * P]
                            mm(oo, um[:, s_], lrb[:, hh, j * P:(j + 1) * P], start=ct == 0, stop=False, skip_group_check=True)
                            mm(oo, tok[:, 2, s_], lrk[:, hh, j * P:(j + 1) * P], start=False, stop=True, skip_group_check=True)
                        s_ = slice(j * P, (j + 1) * P)
                        mm(bank[5][:, s_], tok[:, 0, s_], um[:, s_], start=True, stop=False)
                        i = mm(bank[5][:, s_], tok[:, 1, s_], tok[:, 2, s_], start=False, stop=True)
                    TL.done(i, ("o_state", ct))

                def turn(i6):
                    b = 2 + i6 % 2
                    claim(b, (VL, ("rope", i6)))
                    pe.wait_ge(scalar_done, SL.value(l, ("in", 15 + i6)))
                    i = mm(bank[b][:, 0:T], c("turn", P), qkv[:, i6, :], start=True, stop=True)
                    TL.done(i, ("turn", i6))

                pe.wait_ge(vector_done, VL.value(l, "primed"))
                for ct in range(2):
                    for kind in range(2):
                        pair(ct, kind, (4 * ct + 2 * kind, 4 * ct + 2 * kind + 1))
                for m in range(len(LEVELS)):
                    level_y(0, m)
                    level_y(1, m)
                    level_inc(0, m)
                    if m == 0:
                        pe.wait_ge(vector_done, VL.value(l, "k_and_r"))
                    if m < 3:
                        pair(0, 2 + m, (2, 3))
                    elif m == 3:
                        token_rows(0, 2, 2)
                    level_inc(1, m)
                token_rows(0, 0, 0)
                token_rows(0, 1, 1)
                right_sides(0)
                pair(1, 2, (2, 3))
                solved(0)
                outputs_and_state(0)
                token_rows(1, 2, 0)
                pair(1, 3, (2, 3))
                pair(1, 4, (0, 1))
                token_rows(1, 0, 7)
                token_rows(1, 1, 2)
                right_sides(1)
                for i6 in range(3):
                    turn(i6)
                solved(1)
                for i6 in range(3, 2 * G):
                    turn(i6)
                outputs_and_state(1)

                for hh in range(2):
                    claim(hh, (VL, ("s_pair", hh)))
                    for kind, (lhs, rhs) in enumerate(((a_p, b_p), (b_p, a_p), (k_p, a_p), (b_p, r_p), (k_p, r_p))):
                        for j in range(J):
                            o = (kind * J + j) * TS
                            i = mm(bank[hh][0:TS, o:o + TS], hh_rows(tile(lhs, j, 2), hh), hh_rows(tile(rhs, j, 2), hh),
                                   start=True, stop=True)
                    TL.done(i, ("s_pair", hh))
                for kind, src in enumerate((b_p, k_p, None)):
                    claim(2 + kind, (SL, ("tok", 2, kind)))
                    for j in range(J):
                        s_ = vt(j, 2) if src is None else tile(src, j, 2)
                        i = nc.tensor.transpose(bank[2 + kind][0:TS, j * P:(j + 1) * P], s_, ident)
                    TL.done(i, ("tok", 2, kind))
                claim(5, (SL, "s_r0"))
                pe.wait_ge(wkv_landed, 16 * l + 16)
                for j in range(J):
                    for b_ in range(DEC_BATCH):
                        col = TP + b_ * DEC_SEQ
                        for hh in range(2):
                            i = mm(bank[5][hh * HD:(hh + 1) * HD, j * TS + b_ * DEC_SEQ:j * TS + (b_ + 1) * DEC_SEQ],
                                   hh_rows(wkv_s[:, j, b_], hh), hh_rows(a_p[:, j, col:col + DEC_SEQ], hh), start=True, stop=True)
                TL.done(i, "s_r0")
                claim(0, (SL, "s_y"))
                claim(1, (VL, "s_x"))
                for hh in range(2):
                    pe.wait_ge(vector_done, VL.value(l, ("s_masked", hh)))
                for hh in range(2):
                    for j in range(J):
                        s_ = slice(j * TS, (j + 1) * TS)
                        i = mm(bank[0][0:TS, (hh * J + j) * TS:(hh * J + j + 1) * TS], sm[0:TS, hh, 1, s_], sm[0:TS, hh, 2, s_],
                               start=True, stop=True)
                TL.done(i, "s_y")
                pe.wait_ge(scalar_done, SL.value(l, "s_y"))
                for hh in range(2):
                    for j in range(J):
                        s_ = slice(j * TS, (j + 1) * TS)
                        i = mm(bank[1][0:TS, (hh * J + j) * TS:(hh * J + j + 1) * TS], sm[0:TS, hh, 0, s_], sy[0:TS, hh, s_],
                               start=True, stop=True)
                TL.done(i, "s_xinc")
                claim(6, (SL, ("r", 2)))
                pe.wait_ge(scalar_done, SL.value(l, "s_r0"))
                pe.wait_ge(scalar_done, SL.value(l, ("tok", 2, 2)))
                for j in range(J):
                    o = bank[6][0:TS, j * P:(j + 1) * P]
                    mm(o, tmp_s[:, j * TS:(j + 1) * TS], ident, start=True, stop=False, skip_group_check=True)
                    for hh in range(2):
                        i = mm(o[:, hh * HD:(hh + 1) * HD], sm[0:TS, hh, 3, j * TS:(j + 1) * TS],
                               tok2[0:TS, 2, j * P + hh * HD:j * P + (hh + 1) * HD], start=False, stop=True,
                               skip_group_check=True)
                TL.done(i, ("r", 2))
                claim(7, (SL, ("u", 2)))
                pe.wait_ge(scalar_done, SL.value(l, ("r", 2)))
                pe.wait_ge(vector_done, VL.value(l, "s_x"))
                for j in range(J):
                    for hh in range(2):
                        s_ = slice(j * P + hh * HD, j * P + (hh + 1) * HD)
                        i = mm(bank[7][0:TS, s_], sm[0:TS, hh, 2, j * TS:(j + 1) * TS], rm2[0:TS, s_], start=True, stop=True)
                TL.done(i, ("u", 2))
                claim(4, (SL, ("o", 2)))
                pe.wait_ge(scalar_done, SL.value(l, ("u", 2)))
                for j in range(J):
                    for hh in range(2):
                        s_ = slice(j * P + hh * HD, j * P + (hh + 1) * HD)
                        oo = bank[4][hh * HD:(hh + 1) * HD, j * TS:(j + 1) * TS]
                        mm(oo, um2[0:TS, s_], sm[0:TS, hh, 4, j * TS:(j + 1) * TS], start=True, stop=False, skip_group_check=True)
                        mm(oo, tok2[0:TS, 2, s_], sm[0:TS, hh, 5, j * TS:(j + 1) * TS], start=False, stop=False,
                           skip_group_check=True)
                    for b_ in range(DEC_BATCH):
                        col = TP + b_ * DEC_SEQ
                        for hh in range(2):
                            i = mm(bank[4][hh * HD:(hh + 1) * HD, j * TS + b_ * DEC_SEQ:j * TS + (b_ + 1) * DEC_SEQ],
                                   hh_rows(wkv_s[:, j, b_], hh), hh_rows(r_p[:, j, col:col + DEC_SEQ], hh), start=False,
                                   stop=b_ == DEC_BATCH - 1, skip_group_check=True)
                TL.done(i, "s_o")

                def next_states(j):
                    pe.wait_ge(vector_done, VL.value(l, ("s_sel", j)))
                    b = (0, 1, 2)[j]
                    claim(b, (VL, ("s_state", j)))
                    for hh in range(2):
                        o, s_ = bank[b][hh * HD:(hh + 1) * HD, :], slice(j * P + hh * HD, j * P + (hh + 1) * HD)
                        mm(o, tok2[0:TS, 0, s_], usel[0:TS, :, hh * HD:(hh + 1) * HD], start=True, stop=False, skip_group_check=True)
                        i = mm(o, tok2[0:TS, 1, s_], vsel[0:TS, :, hh * HD:(hh + 1) * HD], start=False, stop=True,
                               skip_group_check=True)
                    TL.done(i, ("s_state", j))

                def conv_sum(step):
                    claim(7, (VL, "conv_mean") if step == "mean" else (SL, "conv_std"))
                    if step == "mean":
                        pe.wait_ge(pool_done, PL.value(l, ("summed", TAPS - 1)))
                    else:
                        pe.wait_ge(scalar_done, SL.value(l, "conv_sq"))
                    for ch in range(2):
                        i = mm(bank[7][:, 0:T], ones, (ycv if step == "mean" else yc2)[:, ch, :], start=ch == 0, stop=ch == 1)
                    TL.done(i, ("conv", step))

                def ln_sum(step):
                    for j in range(J):
                        b = (3, 5, 6)[j]
                        claim(b, (VL if step == "mu" else SL, ("ln_" + step, j)))
                        pe.wait_ge(scalar_done, SL.value(l, ("o", 2) if step == "mu" else "ln_sq"))
                        i = mm(bank[b][:, 0:T], heads, (oT if step == "mu" else tmp_ln)[:, j, :], start=True, stop=True)
                        TL.done(i, ("ln_" + step, j))

                conv_sum("mean")
                ln_sum("mu")
                next_states(0)
                conv_sum("var")
                ln_sum("var")
                next_states(1)
                for ct in range(3):
                    n, rows = (P, slice(ct * P, (ct + 1) * P)) if ct < 2 else (TS, slice(TP, T))
                    claim(4 + ct, (SL, ("vtok", ct)))
                    for g in range(G):
                        i = nc.tensor.transpose(bank[4 + ct][0:n, g * P:(g + 1) * P], qkv[:, 2 * G + g, rows], ident)
                    TL.done(i, ("vtok", ct))
                next_states(2)

                def scores(u):
                    hh, qt = divmod(u, 2)
                    n = (qt + 1) * P
                    r_ = slice(hh * HD, (hh + 1) * HD)
                    for g in range(G):
                        b = (2 * u) % 4 if qt == 0 or g < 2 else (2 * u) % 4 + 1
                        if g == 0 or (g == 2 and qt == 1):
                            claim(b, (VL, ("masked", u, int(g == 2))))
                        o = g * n if (qt == 0 or g < 2) else 0
                        i = mm(bank[b][:, o:o + n], qkv[r_, g, qt * P:(qt + 1) * P], qkv[r_, G + g, 0:n], start=True, stop=True)
                        if (qt == 1 and g == 1) or g == 2:
                            TL.done(i, ("scores", u, int(g == 2)))

                def apply_probs(u):
                    hh, qt = divmod(u, 2)
                    for kt in range(qt + 1):
                        claim(4 + kt, (SL, ("pT", u, kt)))
                        pe.wait_ge(vector_done, VL.value(l, ("probs", u)))
                        for g in range(G):
                            i = nc.tensor.transpose(bank[4 + kt][:, g * P:(g + 1) * P],
                                                    sp_[:, u % 2, g * (qt + 1) * P + kt * P:g * (qt + 1) * P + (kt + 1) * P], ident)
                        TL.done(i, ("pT", u, kt))
                    b = 6 + hh
                    claim(b, (SL, ("attn", u)))
                    for g in range(G):
                        for kt in range(qt + 1):
                            pe.wait_ge(scalar_done, SL.value(l, ("pT", u, kt)))
                            i = mm(bank[b][hh * HD:(hh + 1) * HD, g * P:(g + 1) * P], vtok[:, kt, g, hh * HD:(hh + 1) * HD],
                                   spT[:, u % 2, g, kt, :], start=kt == 0, stop=kt == qt)
                    TL.done(i, ("attn", u))

                q5 = qbd[:, :, :].rearrange("p g (b h t) -> p g b h t", b=DEC_BATCH, h=2)

                def cache_scores(pair):
                    if pair == 0:
                        claim(1, (SL, "sT"))
                        pe.wait_ge(vector_done, VL.value(l, "qbd"))
                    w = arrived(SLAB_AT["wink", pair])
                    for b_ in (2 * pair, 2 * pair + 1):
                        kc = w[:, (b_ % 2) * 896:(b_ % 2 + 1) * 896]
                        o5 = bank[1][:, 0:G * 64].rearrange("p (g b h t) -> p g b h t", g=G, b=DEC_BATCH, h=2)
                        mm(o5[:, 0, b_], kc[:, 0:P], q5[:, 0, b_], start=True, stop=True)
                        for t in range(DEC_SEQ):
                            mm(o5[:, 1, b_, :, t], kc[:, P * (1 + t):P * (2 + t)], q5[:, 1, b_, :, t], start=True, stop=True)
                        for t in range(2):
                            i = mm(o5[:, 2, b_, :, 2 * t:2 * t + 2], kc[:, P * (5 + t):P * (6 + t)], q5[:, 2, b_, :, 2 * t:2 * t + 2],
                                   start=True, stop=True)
                    TL.done(i, ("slab", SLAB_AT["wink", pair]))
                    if pair == 3:
                        for g in range(G):
                            i = mm(bank[1][0:TS, (G + g) * 64:(G + g + 1) * 64], qkv[:, G + g, TP:T], qbd[:, g, :], start=True, stop=True)
                        TL.done(i, "sT")

                pe.wait_ge(vector_done, VL.value(l, "roped"))
                for u in range(5):
                    if u < 4:
                        scores(u)
                        cache_scores(u)
                    if u:
                        apply_probs(u - 1)
                claim(2, (VL, "s_scores"))
                pe.wait_ge(scalar_done, SL.value(l, "sT"))
                for g in range(G):
                    o = g * (P + TS)
                    nc.tensor.transpose(bank[2][0:64, o:o + P], ssT[:, g, :], ident)
                    i = nc.tensor.transpose(bank[2][0:64, o + P:o + P + TS], ssn[0:TS, g, :], ident[0:TS, 0:TS])
                TL.done(i, "s_scores")
                sum_squares("mem", MEM, hm)
                claim(3, (SL, "psT"))
                claim(4, (SL, "psn"))
                pe.wait_ge(vector_done, VL.value(l, "s_probs"))
                for g in range(G):
                    o = g * (P + TS)
                    i = nc.tensor.transpose(bank[3][:, g * 64:(g + 1) * 64], ss[0:64, o:o + P], ident[0:64, 0:64])
                TL.done(i, "psT")
                for g in range(G):
                    o = g * (P + TS)
                    i = nc.tensor.transpose(bank[4][0:TS, g * 64:(g + 1) * 64], ss[0:64, o + P:o + P + TS], ident[0:64, 0:64])
                TL.done(i, "psn")
                claim(5, (SL, "s_attn"))
                pe.wait_ge(scalar_done, SL.value(l, "psT"))
                pe.wait_ge(scalar_done, SL.value(l, "psn"))
                for g in range(G):
                    mm(bank[5][:, g * 64:(g + 1) * 64], vtok_s[0:TS, g, :], psn[0:TS, g, :], start=g == 0, stop=False,
                       skip_group_check=True)
                p5 = psT.rearrange("p g (b h t) -> p g b h t", b=DEC_BATCH, h=2)
                o5 = bank[5][:, 0:G * 64].rearrange("p (g b h t) -> p g b h t", g=G, b=DEC_BATCH, h=2)
                for b_ in range(DEC_BATCH):
                    if b_ % 2 == 0:
                        w = arrived(SLAB_AT["winv", b_ // 2])
                    vc = w[:, (b_ % 2) * 896:(b_ % 2 + 1) * 896]
                    kw = dict(start=False, stop=True, skip_group_check=True)
                    mm(o5[:, 0, b_], vc[:, 0:P], p5[:, 0, b_], **kw)
                    for t in range(DEC_SEQ):
                        mm(o5[:, 1, b_, :, t], vc[:, P * (1 + t):P * (2 + t)], p5[:, 1, b_, :, t], **kw)
                    for t in range(2):
                        i = mm(o5[:, 2, b_, :, 2 * t:2 * t + 2], vc[:, P * (5 + t):P * (6 + t)], p5[:, 2, b_, :, 2 * t:2 * t + 2],
                               **kw)
                    if b_ % 2:
                        TL.done(i, ("slab", SLAB_AT["winv", b_ // 2]))
                TL.done(i, "s_attn")

                attn_tiles = range(2, 2 + G)
                for part in (0, 1):
                    for t in range(NW):
                        hi, lo_ = split(UNITS["out"] + t, KT)
                        if part == 0:
                            claim(t, (VL, ("x_out", t)))
                            pe.wait_ge(vector_done, VL.value(l, "mix_lo"))
                        else:
                            pe.wait_ge(vector_done, VL.value(l, "attn_lo"))
                        for k in attn_tiles if part else (0, 1, *range(2 + G, KT)):
                            i = mm3(bank[t][:, 0:T], (hi[:, k, :], lo_[:, k, :]), (h_hi[:, k, :], h_lo[:, k, :]),
                                    k == 0, k == attn_tiles[-1])
                        if part:
                            TL.done(i, ("unit", UNITS["out"] + t))
                            TL.done(i, ("out", "cols", t))
                columns("out", UNITS["out"], range(NW, KT), (h_hi, h_lo), lambda k: (VL, "attn_lo"), range(7),
                        lambda t: (VL, ("x_out", t)))

                def memory_keys(tiles):
                    columns("k", kv_unit(tiles[0]) - tiles[0], tiles, (hm_hi, hm_lo), lambda k: (VL, ("mem", "h_lo", k)), K_BANKS,
                            lambda t: (SL, ("kx", t)))

                memory_keys((0,))
                sum_squares("xattn")
                memory_keys((1,))
                memory_keys(range(2, K_EARLY))
                columns("q", UNITS["q"], range(KT), (h_hi, h_lo), lambda k: (VL, ("xattn", "h_lo", k)), range(7), lambda t: (SL, ("qx", t)))

                def sample_scores(b_):
                    half, q4 = divmod(b_, 4)
                    if q4 == 0:
                        pe.wait_ge(scalar_done, SL.value(l, ("qx", KT - 1)))
                        claim(4 + half, (SL, ("xexp", 8 + half)))
                    w = arrived(SLAB_AT["memk", b_]).rearrange("p (d m) -> p d m", d=KT)
                    for dt in range(KT):
                        i = mm(bank[4 + half][q4 * 32:(q4 + 1) * 32, 0:MEM], qz[:, dt, b_, :], w[:, dt, :], start=dt == 0,
                               stop=dt == KT - 1, skip_group_check=True)
                    TL.done(i, ("slab", SLAB_AT["memk", b_]))
                    if q4 == 3:
                        TL.done(i, ("xs", 8 + half))

                for n in (2, 3):
                    memory_keys((2 * n, 2 * n + 1))
                    sample_scores(n - 2)
                pe.wait_ge(scalar_done, SL.value(l, ("kx", KT - 1)))
                for u in range(8):
                    hd, qt = divmod(u, 2)
                    if qt == 0:
                        claim(hd, (SL, ("xexp", u + 1)))
                    for dt in range(2):
                        i = mm(bank[hd][:, qt * MEM:(qt + 1) * MEM], qx[:, 2 * hd + dt, qt * P:(qt + 1) * P], kx[:, 2 * hd + dt, :],
                               start=dt == 0, stop=dt == 1)
                    TL.done(i, ("xs", u))
                for n in range(4):
                    for mt in range(2):
                        claim(V_BANKS[n * 2 + mt], (SL, ("vx", n * 2 + mt)))
                    for half in range(2):
                        u = kv_unit(KT + 2 * n + half)
                        hi, lo_ = split(u, KT // 2)
                        for mt in range(2):
                            for k4 in range(KT // 2):
                                k, s_ = half * (KT // 2) + k4, slice(mt * P, (mt + 1) * P)
                                i = mm3(bank[V_BANKS[n * 2 + mt]][:, 0:256], (hm_hi[:, k, s_], hm_lo[:, k, s_]),
                                        (hi[:, k4, :], lo_[:, k4, :]), k == 0, k == KT - 1)
                            if mt:
                                TL.done(i, ("unit", u))
                            if half:
                                TL.done(i, ("vx", n * 2 + mt))
                    sample_scores(n + 2)
                for b_ in range(MEMK_EARLY, DEC_BATCH):
                    sample_scores(b_)
                def probs_T(u):
                    b = (6, 7)[u % 2]
                    claim(b, (SL, ("xpT", u)))
                    pe.wait_ge(vector_done, VL.value(l, ("xprobs", unit_head(u))))
                    for kt in range(2):
                        i = nc.tensor.transpose(bank[b][:, kt * P:(kt + 1) * P], px[:, u, kt * P:(kt + 1) * P], ident)
                    TL.done(i, ("xpT", u))

                def prompt_out(hd):
                    claim(hd, (VL, ("ox_lo", hd)))
                    pe.wait_ge(scalar_done, SL.value(l, ("xpT", 2 * hd + 1)))
                    if hd == 0:
                        pe.wait_ge(scalar_done, SL.value(l, ("vx", 7)))
                    for dt in (2 * hd, 2 * hd + 1):
                        for kt in range(2):
                            i = mm(bank[hd][:, (dt % 2) * TP:(dt % 2 + 1) * TP], vx[:, kt, dt * P:(dt + 1) * P], pxT[:, hd, kt, :],
                                   start=kt == 0, stop=kt == 1)
                    TL.done(i, ("ox", hd))

                for hd in range(4):
                    probs_T(2 * hd)
                    probs_T(2 * hd + 1)
                    if hd:
                        prompt_out(hd - 1)
                probs_T(8)
                prompt_out(3)
                probs_T(9)
                pe.wait_ge(scalar_done, SL.value(l, ("xpT", 9)))

                def channels_back(half):
                    for n in range(2):
                        b = 2 * half + n
                        claim(b, (VL, ("oxs_lo", half, n)))
                        pe.wait_ge(scalar_done, SL.value(l, ("oxs", half, n)))
                        for d in range(4):
                            dt = 4 * n + d
                            i = nc.tensor.transpose(bank[b][:, d * P:(d + 1) * P], oxs[:, half, dt * P:(dt + 1) * P], ident)
                        TL.done(i, ("oxsT", half, n))

                for b_ in range(DEC_BATCH):
                    half, q4 = divmod(b_, 4)
                    w = arrived(SLAB_AT["memv", b_]).rearrange("p (k c) -> p k c", k=2)
                    for n in range(2):
                        b = 4 + 2 * half + n
                        if q4 == 0:
                            claim(b, (SL, ("oxs", half, n)))
                        for kt in range(2):
                            i = mm(bank[b][q4 * 32:(q4 + 1) * 32, :], pxsT[:, kt, half, q4 * 32:(q4 + 1) * 32],
                                   w[:, kt, n * 512:(n + 1) * 512], start=kt == 0, stop=kt == 1, skip_group_check=True)
                        if n == 1:
                            TL.done(i, ("slab", SLAB_AT["memv", b_]))
                        if q4 == 3:
                            TL.done(i, ("oxs", half, n))
                    if b_ == 5:
                        channels_back(0)
                channels_back(1)
                columns("o", UNITS["o"], range(KT), (ox_hi, ox_lo), lambda k: (VL, ("oxs_lo", 1, 1)),
                        (5, 6, 7, 0, 1, 2, 3), lambda t: (VL, ("x_o", t)))
                ffn("ffn2")
            l = DEPTH - 1
            for k in range(KT):
                pe.wait_ge(scalar_done, SL.value(l, ("final", "sq", k)))
                i = mm(bank[7][:, 0:T], ones, sq[:, k, :], start=k == 0, stop=k == KT - 1)
            TL.done(i, ("final", "ss"))

        @block.scalar
        def _(act):
            act.sem_inc(scalar_done, SL.total)
            act.wait_ge(start_landed, 32)
            fn = nc.scalar.activation

            for l in range(DEPTH):
                SL.begin_layer()

                def copy(out, in_, name=None):
                    return SL.done(nc.scalar.copy(out, in_), name)

                def split(u):
                    if u is None:
                        return
                    act.wait_ge(*landed(l, SLAB_OF_UNIT[u][0]))
                    if u >= NW:
                        act.wait_ge(tensor_done, TL.value(l, ("unit", u - NW)))
                    else:
                        held = max(v for v in range(NUNIT) if v % NW == u % NW)
                        act.wait_ge(tensor_done, TL.value_before(l, ("unit", held)))
                    copy(w_hi[:, u % NW, :], raw_unit(u), ("hi", u))

                def square(tag, src, n, k, out=sq):
                    SL.done(fn(out[:, k, 0:n], src[:, k, 0:n], ACT.Square), (tag, "sq", k))

                def root(tag, rs_, n):
                    SL.done(fn(warm, con[:, CON["ones"]:CON["ones"] + 1], ACT.Sqrt))
                    act.wait_ge(tensor_done, TL.value(l, (tag, "ss")))
                    SL.done(fn(rs_[:, 0:n], bank[7][:, 0:n], ACT.Sqrt, bias=NORM_EPS, scale=1.0 / D_MODEL), (tag, "rms"))

                def rms(tag, src, rs_, n, ready, between=lambda: None, hi=None, meanwhile=lambda k: None):
                    for k in range(KT):
                        if tag == "mix" and k < 4:
                            continue
                        ready(k)
                        square(tag, src, n, k)
                    between()
                    root(tag, rs_, n)
                    if hi is not None:
                        for k in range(KT):
                            meanwhile(k)
                            act.wait_ge(vector_done, VL.value(l, (tag, "h", k)))
                            copy(hi[:, k, 0:n], h[:, k, 0:n], (tag, "h_hi", k))

                def ffn(tag, ready, between=lambda: None):
                    first = UNITS[tag]
                    rms(tag, x, rs, T, ready, between, h_hi)
                    for t in range(FT):
                        act.wait_ge(tensor_done, TL.value(l, (tag, "gate", t)))
                        if t >= 2:
                            act.wait_ge(vector_done, VL.value(l, (tag, "gated", t - 2)))
                        SL.done(fn(th[:, t % 2, :], bank[(t % 2) * 2][:, 0:T], ACT.Tanh, scale=0.5), (tag, "tanh", t))
                        split(next_unit(first + 2 * t))
                        split(next_unit(first + 2 * t + 1))
                        act.wait_ge(vector_done, VL.value(l, (tag, "hid", t)))
                        copy(hid_hi[:, t, :], hid[:, t, :], (tag, "hid_hi", t))
                    for u in range(first + 2 * FT, first + 3 * FT):
                        split(next_unit(u))
                        if tag == "ffn1" and u == first + 2 * FT + FT // 2 + 3:
                            act.wait_ge(vector_done, VL.value(l, (tag, "x", 0)))
                            for k in range(4):
                                square("mix", x, T, k)

                ffn("ffn1", lambda k: act.wait_ge(vector_done, VL.value_before(l, ("ffn2", "x", 1))),
                    lambda: [split(u) for u in range(NW)])

                rms("mix", x, rs, T, lambda k: act.wait_ge(vector_done, VL.value(l, ("ffn1", "x", k // 4))), hi=h_hi)
                def project(t):
                    b = t % 7
                    if t in (11, 13):
                        split(next_unit(UNITS["in"] + t))
                        return
                    act.wait_ge(tensor_done, TL.value(l, ("in", "cols", t)))
                    if t < NC_TILES:
                        copy(f_p[:, t, 1:], bank[b][:, 0:TP])
                        copy(f_s[:, t, :, 1:], bt(bank[b][:, TP:T]), ("in", t))
                    elif t in (12, 14):
                        SL.done(fn(w_i[:, (t - 12) // 2, :], bank[b][:, 0:T], ACT.Tanh, scale=0.5), ("in", t))
                    else:
                        copy(qkv[:, t - 15, :], bank[b][:, 0:T], ("in", t))
                    split(next_unit(UNITS["in"] + t))
                for t in range(IN_CUT[0] - 2):
                    project(t)
                act.wait_ge(vector_done, VL.value(l, "shift_out"))
                SL.done(fn(tmp[:, 1, :], xs[:, C_G, :], ACT.Tanh, scale=0.5), "g_tanh")
                SL.done(fn(tmp[0:64, 0, :], xs[0:64, C_LO, :], ACT.Tanh), "lo_tanh")
                for t in range(IN_CUT[0] - 2, IN_CUT[0]):
                    project(t)
                act.wait_ge(vector_done, VL.value(l, "halves"))
                for kind in range(3):
                    for j in range(J):
                        b = (kind * J + j) % 7
                        act.wait_ge(tensor_done, TL.value(l, ("lora", kind, j)))
                        if kind == 2:
                            copy(gz[:, j, :], bank[b][:, 0:T], ("lora", kind, j))
                        else:
                            SL.done(fn((ld, aa)[kind][:, j, :], bank[b][:, 0:T], ACT.Tanh, scale=0.5,
                                       bias=halves[:, kind * J + j:kind * J + j + 1]), ("lora", kind, j))
                act.wait_ge(vector_done, VL.value(l, "kk"))
                SL.done(fn(tmp, kk, ACT.Square), "kk_sq")
                for t in range(IN_CUT[0], IN_CUT[1]):
                    project(t)
                for j in range(J):
                    act.wait_ge(tensor_done, TL.value(l, ("kk_ss", j)))
                    SL.done(fn(tmp[:, j, :], bank[j][:, 0:T], ACT.Sqrt), ("kk_norm", j))
                project(IN_CUT[1])
                act.wait_ge(vector_done, VL.value(l, "centred"))
                SL.done(fn(w_c, cl, ACT.Exp), "w_c")
                SL.done(fn(w_i, cl, ACT.Exp, scale=-1.0), "w_i")
                act.wait_ge(vector_done, VL.value(l, "before"))
                SL.done(fn(w_p, ld, ACT.Exp), "w_p")
                SL.done(fn(wmid1, mids[:, :, 1:2], ACT.Exp), "w_mid")
                for t in range(IN_CUT[1] + 1, IN_TILES):
                    project(t)
                for j in range(J):
                    act.wait_ge(tensor_done, TL.value(l, ("bonus", j)))
                    copy(bon[:, j, :], bank[3 + j][:, 0:T], ("bonus", j))
                act.wait_ge(vector_done, VL.value(l, "primed"))
                act.dma_start(wkv_s, wkv_in[l]).then_inc(wkv_landed, 16)
                def token_rows(ct, kind, b):
                    act.wait_ge(tensor_done, TL.value(l, ("tok", ct, kind)))
                    copy(tok[:, kind], bank[b][:, 0:J * P], ("tok", ct, kind))

                for m in range(len(LEVELS)):
                    for ct in range(2):
                        for hh in range(2):
                            act.wait_ge(tensor_done, TL.value(l, ("y", ct, m, hh)))
                            copy(ym[ct][:, hh], bank[4 * ct + hh][:, 0:J * P], ("y", ct, m, hh))
                    if m == 3:
                        token_rows(0, 2, 2)
                token_rows(0, 0, 0)
                token_rows(0, 1, 1)
                for ct in range(2):
                    if ct:
                        token_rows(1, 2, 0)
                        token_rows(1, 0, 7)
                        token_rows(1, 1, 2)
                    act.wait_ge(tensor_done, TL.value(l, ("r", ct)))
                    copy(rm, bank[6][:, 0:J * P], ("r", ct))
                    act.wait_ge(tensor_done, TL.value(l, ("u", ct)))
                    copy(um, bank[7][:, 0:J * P], ("u", ct))
                    act.wait_ge(tensor_done, TL.value(l, ("o_state", ct)))
                    copy(oT[:, :, ct * P:(ct + 1) * P], bank[4][:, 0:J * P].rearrange("p (j t) -> p j t", j=J), ("o", ct))
                for kind in range(3):
                    act.wait_ge(tensor_done, TL.value(l, ("tok", 2, kind)))
                    copy(tok2[0:TS, kind], bank[2 + kind][0:TS, 0:J * P], ("tok", 2, kind))
                act.wait_ge(tensor_done, TL.value(l, "s_r0"))
                copy(tmp_s, bank[5][:, 0:J * TS], "s_r0")
                act.wait_ge(tensor_done, TL.value(l, "s_y"))
                copy(sy[0:TS], bank[0][0:TS, 0:2 * J * TS].rearrange("p (h c) -> p h c", h=2), "s_y")
                act.wait_ge(tensor_done, TL.value(l, ("r", 2)))
                copy(rm2[0:TS], bank[6][0:TS, 0:J * P], ("r", 2))
                act.wait_ge(tensor_done, TL.value(l, ("u", 2)))
                copy(um2[0:TS], bank[7][0:TS, 0:J * P], ("u", 2))
                act.wait_ge(tensor_done, TL.value(l, "s_o"))
                copy(oT[:, :, TP:T], bank[4][:, 0:J * TS].rearrange("p (j t) -> p j t", j=J), ("o", 2))
                act.wait_ge(vector_done, VL.value(l, "conv_mean"))
                SL.done(fn(yc2, ycv, ACT.Square), "conv_sq")
                act.wait_ge(vector_done, VL.value(l, ("ln_mu", J - 1)))
                SL.done(fn(tmp_ln, oT, ACT.Square), "ln_sq")
                act.wait_ge(tensor_done, TL.value(l, ("conv", "var")))
                SL.done(fn(yc2[:, 0, :], bank[7][:, 0:T], ACT.Sqrt, bias=CONV_EPS, scale=1.0 / 256), "conv_std")
                for j in range(J):
                    act.wait_ge(tensor_done, TL.value(l, ("ln_var", j)))
                    SL.done(fn(tmp_ln[:, j, :], bank[(3, 5, 6)[j]][:, 0:T], ACT.Sqrt, bias=LNX_EPS, scale=1.0 / HD), ("ln_var", j))
                for ct in range(3):
                    act.wait_ge(tensor_done, TL.value(l, ("vtok", ct)))
                    if ct < 2:
                        copy(vtok[:, ct], bank[4 + ct][:, 0:G * P].rearrange("p (g c) -> p g c", g=G), ("vtok", ct))
                    else:
                        copy(vtok_s[0:TS], bank[4 + ct][0:TS, 0:G * P].rearrange("p (g c) -> p g c", g=G), ("vtok", ct))
                act.wait_ge(vector_done, VL.value(l, "conv_norm"))
                SL.done(fn(yc2, ycv, ACT.Tanh, scale=0.5), "conv_tanh")
                act.wait_ge(vector_done, VL.value(l, "rwkv_out"))
                copy(h_hi[:, 0:2, :], h[:, 0:2, :])
                copy(h_hi[:, 5:5 + J, :], h[:, 5:5 + J, :], "mix_hi")

                def probs(u):
                    qt = u % 2
                    n = G * (qt + 1) * P
                    act.wait_ge(vector_done, VL.value(l, ("nmax", u)))
                    SL.done(fn(sp_[:, qt, 0:n], sp_[:, qt, 0:n], ACT.Exp, scale=ATTN_SCALE, bias=astat[:, 1, u:u + 1],
                               accum_out=astat[:, 2, u:u + 1]), ("exp", u))

                for u in range(5):
                    if u < 4:
                        probs(u)
                    if u:
                        if u == 1:
                            act.wait_ge(mem_landed, 16 * l + 16)
                        square("mem", memx, MEM, 2 * u - 2, hm)
                        square("mem", memx, MEM, 2 * u - 1, hm)
                        v = u - 1
                        hh, qt = divmod(v, 2)
                        for kt in range(qt + 1):
                            act.wait_ge(tensor_done, TL.value(l, ("pT", v, kt)))
                            copy(spT[:, v % 2, :, kt, :], bank[4 + kt][:, 0:G * P].rearrange("p (g c) -> p g c", g=G), ("pT", v, kt))
                        act.wait_ge(tensor_done, TL.value(l, ("attn", v)))
                        r_ = slice(hh * HD, (hh + 1) * HD)
                        copy(h[r_, 2:2 + G, qt * P:(qt + 1) * P], bank[6 + hh][r_, 0:G * P].rearrange("p (g c) -> p g c", g=G),
                             ("attn", v))
                act.wait_ge(tensor_done, TL.value(l, "sT"))
                copy(ssT, bank[1][:, 0:G * 64].rearrange("p (g c) -> p g c", g=G))
                copy(ssn[0:TS], bank[1][0:TS, G * 64:2 * G * 64].rearrange("p (g c) -> p g c", g=G), "sT")
                act.wait_ge(vector_done, VL.value(l, ("nmax", 4)))
                SL.done(fn(ss[0:64], ss[0:64], ACT.Exp, scale=ATTN_SCALE, bias=astat[0:64, 1, 4:5],
                           accum_out=astat[0:64, 2, 4:5]), ("exp", 4))
                act.wait_ge(tensor_done, TL.value(l, "psT"))
                copy(psT, bank[3][:, 0:G * 64].rearrange("p (g c) -> p g c", g=G), "psT")
                act.wait_ge(tensor_done, TL.value(l, "psn"))
                copy(psn[0:TS], bank[4][0:TS, 0:G * 64].rearrange("p (g c) -> p g c", g=G), "psn")
                for u in range(NW):
                    split(UNITS["out"] + u)
                root("mem", mem_rs, MEM)
                for k in range(KT):
                    act.wait_ge(vector_done, VL.value(l, ("mem", "h", k)))
                    copy(hm_hi[:, k, :], hm[:, k, :], ("mem", "h_hi", k))
                act.wait_ge(tensor_done, TL.value(l, "s_attn"))
                for hh in range(2):
                    r_ = slice(hh * HD, (hh + 1) * HD)
                    o4 = bank[5][r_, 0:G * 64].rearrange("p (g b h t) -> p g b h t", g=G, b=DEC_BATCH, h=2)
                    for g in range(G):
                        copy(bt(h[r_, 2 + g, TP:T]), o4[:, g, :, hh, :], "s_attn" if (hh, g) == (1, G - 1) else None)

                act.wait_ge(scalar_done, SL.value(l, "s_attn"))
                copy(h_hi[:, 2:2 + G, :], h[:, 2:2 + G, :], "attn_hi")

                def out_done(k):
                    if k:
                        split(next_unit(UNITS["out"] + k - 1))
                    act.wait_ge(vector_done, VL.value(l, ("x_out", k)))

                def memory_keys(t):
                    act.wait_ge(tensor_done, TL.value(l, ("k", "cols", t)))
                    copy(kx[:, t, :], bank[K_BANKS[t % 6]][:, 0:MEM], ("kx", t))
                    split(next_unit(kv_unit(t)))

                act.wait_ge(stored, store_value(l, "wkv_s"))
                rms("xattn", x, rs, T, out_done, lambda: split(next_unit(UNITS["out"] + KT - 1)), h_hi,
                    lambda k: memory_keys(k // 4) if k % 4 == 0 else None)
                for t in range(2, K_EARLY):
                    memory_keys(t)
                for t in range(KT):
                    act.wait_ge(tensor_done, TL.value(l, ("q", "cols", t)))
                    copy(qx[:, t, :], bank[t % 7][:, 0:T])
                    if t == 0:
                        act.wait_ge(vector_done, VL.value(l, "qz_clear"))
                    copy(qz[:, t, :, 4 * (t // 2):4 * (t // 2) + 4], bt(bank[t % 7][:, TP:T]), ("qx", t))
                    split(next_unit(UNITS["q"] + t))
                for t in range(K_EARLY, KT):
                    memory_keys(t)

                def xexp(u):
                    src = bank[u // 2][:, (u % 2) * MEM:(u % 2 + 1) * MEM] if u < 8 else bank[u - 4][:, 0:MEM]
                    act.wait_ge(vector_done, VL.value(l, ("xnmax", unit_head(u))))
                    SL.done(fn(px[:, u, :], src, ACT.Exp, scale=X_SCALE, bias=xstat[:, 1, u:u + 1],
                               accum_out=xstat[:, 2, u:u + 1]), ("xexp", u))

                for n in range(4):
                    xexp(2 * n)
                    split(next_unit(kv_unit(KT + 2 * n)))
                    xexp(2 * n + 1)
                    for mt in range(2):
                        m = 2 * n + mt
                        act.wait_ge(tensor_done, TL.value(l, ("vx", m)))
                        copy(vx[:, mt, n * 256:(n + 1) * 256], bank[V_BANKS[m]][:, 0:256], ("vx", m))
                    split(next_unit(kv_unit(KT + 2 * n + 1)))
                xexp(8)
                xexp(9)

                def probs_T(u):
                    act.wait_ge(tensor_done, TL.value(l, ("xpT", u)))
                    out = pxT[:, u // 2, :, (u % 2) * P:(u % 2 + 1) * P] if u < 8 else pxsT[:, :, u - 8, :]
                    copy(out, bank[6 + u % 2][:, 0:2 * P].rearrange("p (k c) -> p k c", k=2), ("xpT", u))

                def prompt_out(hd):
                    act.wait_ge(tensor_done, TL.value(l, ("ox", hd)))
                    copy(ox_hi[:, 2 * hd:2 * hd + 2, 0:TP], bank[hd][:, :].rearrange("p (a c) -> p a c", a=2), ("ox", hd))

                for hd in range(4):
                    probs_T(2 * hd)
                    probs_T(2 * hd + 1)
                    if hd:
                        prompt_out(hd - 1)
                probs_T(8)
                probs_T(9)
                prompt_out(3)
                for half in range(2):
                    for n in range(2):
                        act.wait_ge(tensor_done, TL.value(l, ("oxs", half, n)))
                        copy(oxs[:, half, n * 512:(n + 1) * 512], bank[4 + 2 * half + n][:, :], ("oxs", half, n))
                    if half:
                        split(UNITS["o"])
                    for n in range(2):
                        act.wait_ge(tensor_done, TL.value(l, ("oxsT", half, n)))
                        for hd in (2 * n, 2 * n + 1):
                            copy(sample_out(ox_hi, half, hd), head_columns(half, hd), ("oxs_hi", half, hd))

                for u in range(1, NW):
                    split(UNITS["o"] + u)

                def ready2(k):
                    if k:
                        split(next_unit(UNITS["o"] + k - 1))
                    act.wait_ge(vector_done, VL.value(l, ("x_o", k)))
                    if k == 0:
                        act.wait_ge(stored, store_value(l, "memv"))
                ffn("ffn2", ready2, lambda: split(next_unit(UNITS["o"] + KT - 1)))
            l = DEPTH - 1
            rms("final", x, rs, T, lambda k: act.wait_ge(vector_done, VL.value(l, ("ffn2", "x", k // 4))))

        @block.vector
        def _(dve):
            dve.sem_inc(vector_done, VL.total)
            dve.wait_ge(start_landed, 32)
            dve.wait_ge(par_landed, 16)
            tt, ts, stt = nc.vector.tensor_tensor, nc.vector.tensor_scalar, nc.vector.scalar_tensor_tensor
            cp = nc.vector.tensor_copy

            for l in range(DEPTH):
                VL.begin_layer()

                def settle():
                    dve.wait_ge(vector_done, VL.so_far(l))

                D = VL.done
                par = par_all[:, l, :]

                def pr(name, i):
                    return par[:, PAR[name] + i:PAR[name] + i + 1]

                def low(out, src, hi, name=None):
                    D(tt(out, src, hi.bitcast(F32), ALU.subtract), name)

                def split(u):
                    if u is not None:
                        dve.wait_ge(scalar_done, SL.value(l, ("hi", u)))
                        low(w_lo[:, u % NW, :], raw_unit(u), w_hi[:, u % NW, :], ("lo", u))

                def normalise(tag, src, dst, rs_, n, parts=None, meanwhile=lambda k: None):
                    dve.wait_ge(scalar_done, SL.value(l, (tag, "rms")))
                    D(nc.vector.reciprocal(rs_[:, 0:n], rs_[:, 0:n]))
                    settle()
                    for k in range(KT + 1):
                        meanwhile(k)
                        if k < KT:
                            D(stt(dst[:, k, 0:n], src[:, k, 0:n], pr(tag, k), rs_[:, 0:n], ALU.mult, ALU.mult), (tag, "h", k))
                        if k and parts:
                            dve.wait_ge(scalar_done, SL.value(l, (tag, "h_hi", k - 1)))
                            low(parts[1][:, k - 1, 0:n], dst[:, k - 1, 0:n], parts[0][:, k - 1, 0:n], (tag, "h_lo", k - 1))

                def ffn(tag):
                    first = UNITS[tag]
                    normalise(tag, x, h, rs, T, (h_hi, h_lo))
                    for t in range(FT):
                        dve.wait_ge(scalar_done, SL.value(l, (tag, "tanh", t)))
                        D(stt(th2[:, t % 2, :], th[:, t % 2, :], 1.0, bank[(t % 2) * 2][:, 0:T], ALU.add, ALU.mult),
                          (tag, "gated", t))
                        split(next_unit(first + 2 * t))
                        settle()
                        dve.wait_ge(tensor_done, TL.value(l, (tag, "up", t)))
                        D(tt(hid[:, t, :], th2[:, t % 2, :], bank[(t % 2) * 2 + 1][:, 0:T], ALU.mult), (tag, "hid", t))
                        split(next_unit(first + 2 * t + 1))
                        dve.wait_ge(scalar_done, SL.value(l, (tag, "hid_hi", t)))
                        low(hid_lo[:, t, :], hid[:, t, :], hid_hi[:, t, :], (tag, "hid_lo", t))
                    for half in range(2):
                        for u in range(first + 2 * FT + half * FT // 2, first + 2 * FT + (half + 1) * FT // 2):
                            split(next_unit(u))
                        dve.wait_ge(tensor_done, TL.value(l, (tag, "down", half)))
                        for d in range(4):
                            k = 4 * half + d
                            D(stt(x[:, k, :], bank[4 + d if half == 0 else d][:, 0:T], 0.25, x[:, k, :], ALU.mult, ALU.add),
                              (tag, "x", half) if d == 3 else None)

                for u in range(NW):
                    split(u)
                ffn("ffn1")

                dve.wait_ge(con_landed, 32)
                D(ts(halves, par[:, PAR["w0"]:PAR["w0"] + 2 * J], 0.5, None, ALU.mult), "halves")
                normalise("mix", x, h, rs, T, (h_hi, h_lo))
                D(nc.vector.memset(f_p[:, :, 0:1], 0.0))
                D(cp(f_s[:, :, :, 0], par[:, PAR["state_shift"]:PAR["state_shift"] + NC_TILES * 8]
                     .rearrange("p (c b) -> p c b", b=DEC_BATCH)))
                D(nc.vector.memset(up[:, :, 0:HIST], 0.0))
                settle()
                for t in range(NC_TILES):
                    dve.wait_ge(scalar_done, SL.value(l, ("in", t)))
                    D(tt(xs[:, t, 0:TP], f_p[:, t, 0:TP], f_p[:, t, 1:], ALU.subtract))
                    D(tt(bt(xs[:, t, TP:T]), f_s[:, t, :, 0:DEC_SEQ], f_s[:, t, :, 1:], ALU.subtract))
                    settle()
                    D(stt(xs[:, t, 0:TP], xs[:, t, 0:TP], pr("shift", t), f_p[:, t, 1:], ALU.mult, ALU.add))
                    D(stt(bt(xs[:, t, TP:T]), bt(xs[:, t, TP:T]), pr("shift", t), f_s[:, t, :, 1:], ALU.mult, ALU.add), ("xs", t))
                    split(next_unit(UNITS["in"] + t))
                D(cp(shift_o[:, :, 0:1], f_p[:, :, TP:TP + 1]))
                D(cp(shift_o[:, :, 1:], f_s[:, :, :, DEC_SEQ]), "shift_out")
                for ch in range(2):
                    split(next_unit(UNITS["in"] + 11 + 2 * ch))
                    dve.wait_ge(scalar_done, SL.value(l, ("in", 12 + 2 * ch)))
                    D(ts(w_i[:, ch, :], w_i[:, ch, :], 0.5, 0.5, ALU.mult, ALU.add))
                    settle()
                    b = 11 + 2 * ch
                    dve.wait_ge(tensor_done, TL.value(l, ("in", "cols", b)))
                    if ch == 0:
                        dve.wait_ge(layer_landed, 16 * l + 16)
                    D(tt(up[:, ch, HIST:], w_i[:, ch, 0:TP], bank[b % 7][:, 0:TP], ALU.mult))
                    D(tt(us4[:, ch, :, HIST:], bt(w_i[:, ch, TP:T]), bt(bank[b % 7][:, TP:T]), ALU.mult), ("glu", ch))
                    split(next_unit(UNITS["in"] + 12 + 2 * ch))
                split(next_unit(UNITS["in"] + 15))
                dve.wait_ge(scalar_done, SL.value(l, "g_tanh"))
                D(ts(xs[:, C_G, :], tmp[:, 1, :], 0.5, 0.5, ALU.mult, ALU.add), "lo_gate")
                for j in range(J):
                    D(ts(kk[:, j, :], xs[:, C_K + j, :], pr("k_k", j), None, ALU.mult), "kk" if j == J - 1 else None)
                split(next_unit(UNITS["in"] + 16))
                split(next_unit(UNITS["in"] + 17))
                for j in range(J):
                    dve.wait_ge(scalar_done, SL.value(l, ("lora", 0, j)))
                D(ts(ld, ld, -HALF_DECAY, -HALF_DECAY, ALU.mult, ALU.add))
                settle()
                fl = lambda a: a.rearrange("p j t -> p (j t)")
                D(nc.vector.tensor_tensor_scan(fl(cl), c("scan", J * T), fl(ld), 0.0, ALU.mult, ALU.add))
                settle()
                for ct in range(2):
                    D(cp(mids[:, :, ct:ct + 1], cl[:, :, ct * P + 63:ct * P + 64]))
                settle()
                for ct in range(2):
                    for j in range(J):
                        D(ts(cl[:, j, ct * P:(ct + 1) * P], cl[:, j, ct * P:(ct + 1) * P], mids[:, j, ct:ct + 1], None, ALU.subtract),
                          "centred" if (ct, j) == (1, J - 1) else None)
                settle()
                D(tt(ld, cl, ld, ALU.subtract), "before")
                split(next_unit(UNITS["in"] + IN_CUT[0]))
                split(next_unit(UNITS["in"] + IN_CUT[0] + 1))
                for j in range(J):
                    dve.wait_ge(scalar_done, SL.value(l, ("lora", 1, j)))
                D(ts(aa, aa, 0.5, 0.5, ALU.mult, ALU.add))
                settle()
                for j in range(J):
                    D(ts(a_p[:, j, :], aa[:, j, :], -1.0, pr("k_a", j), ALU.add, ALU.mult))
                settle()
                D(stt(k2, a_p, 1.0, k2, ALU.add, ALU.mult))
                settle()
                for j in range(J):
                    D(stt(oT[:, j, :], xs[:, C_R + j, :], pr("r_k", j), k2[:, j, :], ALU.mult, ALU.mult), ("rkr", j))
                split(next_unit(UNITS["in"] + IN_CUT[1]))
                for j in range(J):
                    dve.wait_ge(scalar_done, SL.value(l, ("kk_norm", j)))
                D(ts(tmp, tmp, 1e-12, None, ALU.max))
                settle()
                D(nc.vector.reciprocal(tmp, tmp))
                settle()
                D(tt(kk, kk, tmp, ALU.mult))
                settle()
                dve.wait_ge(scalar_done, SL.value(l, "w_p"))
                D(stt(a_p, kk, -1.0, w_p, ALU.mult, ALU.mult))
                D(tt(b_p, kk, aa, ALU.mult))
                settle()
                D(tt(b_p, b_p, w_i, ALU.mult), "primed")
                D(tt(k_p, k2, w_i, ALU.mult))
                D(tt(r_p, xs[:, C_R:C_R + J, :], w_c, ALU.mult), "k_and_r")
                dve.wait_ge(scalar_done, SL.value(l, "w_mid"))
                D(tt(wend[:, :, 0:1], w_c[:, :, P - 1:P], wmid1, ALU.mult))
                D(cp(wend[:, :, 1:2], w_c[:, :, TP - 1:TP]))
                D(cp(wend[:, :, 2:], w_c[:, :, TP + DEC_SEQ - 1:T:DEC_SEQ]))
                settle()

                def b3(mask, n=J):
                    return mask.unsqueeze(1).to_broadcast([mask.shape[0], n, mask.shape[1]])

                def j3(a):
                    return a.rearrange("p (j s) -> p j s", j=J)

                def pair(ct, kind, banks):
                    for hh in range(2):
                        src = j3(bank[banks[hh]][:, 0:J * P])
                        dve.wait_ge(tensor_done, TL.value(l, ("pair", ct, kind, hh)))
                        if kind == 0:
                            D(cp(lab[ct][:, hh], bank[banks[hh]][:, 0:J * P]))
                            D(tt(j3(tm[ct][:, hh]), src, b3(c("level1", P)), ALU.mult), ("pair", ct, kind, hh))
                        elif kind == 1:
                            D(tt(j3(xm[ct][:, hh]), src, b3(c("level1", P, at=P)), ALU.mult), ("pair", ct, kind, hh))
                        else:
                            D(tt(j3((lak, lrb, lrk)[kind - 2][:, hh]), src, b3(c("strict" if kind == 2 else "upper", P)), ALU.mult),
                              ("pair", ct, kind, hh))

                def low_blocks(ct, m):
                    lab6, lo6 = (a[ct].rearrange("p h (j s) -> p (h j) s", j=J) for a in (lab, lo))
                    if m:
                        dve.wait_ge(tensor_done, TL.value(l, ("y", ct, m - 1, 1)))
                    D(tt(lo6, lab6, b3(c("levels", P, at=m * P), 2 * J), ALU.mult), ("lo", ct, m))

                def level(ct, m):
                    for hh in range(2):
                        dve.wait_ge(tensor_done, TL.value(l, ("xinc", ct, m, hh)))
                        D(tt(xm[ct][:, hh], xm[ct][:, hh], bank[4 * ct + 2 + hh][:, 0:J * P], ALU.add), ("x", ct, m, hh))
                    for hh in range(2):
                        if m < len(LEVELS) - 1:
                            dve.wait_ge(tensor_done, TL.value(l, ("tinc", ct, m, hh)))
                            D(tt(tm[ct][:, hh], tm[ct][:, hh], bank[4 * ct + hh][:, 0:J * P], ALU.add), ("t", ct, m, hh))

                def state(ct):
                    dve.wait_ge(tensor_done, TL.value(l, ("o_state", ct)))
                    if ct:
                        D(tt(st, st, bank[5][:, 0:J * P], ALU.add))
                        settle()
                    for j in range(J):
                        s_ = slice(j * P, (j + 1) * P)
                        D(stt(st[:, s_], st[:, s_] if ct else bank[5][:, s_], wend[:, j, ct:ct + 1], heads, ALU.mult, ALU.mult),
                          ("state", ct) if j == J - 1 else None)

                def rope(i6):
                    dve.wait_ge(tensor_done, TL.value(l, ("turn", i6)))
                    D(tt(turned, bank[2 + i6 % 2][:, 0:T], c("sin", T), ALU.mult), ("rope", i6))
                    D(tt(qkv[:, i6, :], qkv[:, i6, :], c("cos", T), ALU.mult))
                    settle()
                    D(tt(qkv[:, i6, :], qkv[:, i6, :], turned, ALU.add), "roped" if i6 == 2 * G - 1 else None)
                    settle()

                for ct in range(2):
                    for kind in range(2):
                        pair(ct, kind, (4 * ct + 2 * kind, 4 * ct + 2 * kind + 1))
                    settle()
                    for hh in range(2):
                        D(tt(j3(tm[ct][:, hh]), j3(tm[ct][:, hh]), b3(ident), ALU.add), ("t0", ct, hh))
                        D(tt(j3(xm[ct][:, hh]), j3(xm[ct][:, hh]), b3(ident), ALU.add), ("x0", ct, hh))
                    low_blocks(ct, 0)
                for m in range(len(LEVELS)):
                    if m < len(LEVELS) - 1:
                        low_blocks(0, m + 1)
                    level(0, m)
                    if m < 3:
                        pair(0, 2 + m, (2, 3))
                    if m < len(LEVELS) - 1:
                        low_blocks(1, m + 1)
                    level(1, m)
                pair(1, 2, (2, 3))
                state(0)
                pair(1, 3, (2, 3))
                pair(1, 4, (0, 1))
                for i6 in range(2 * G):
                    rope(i6)
                state(1)

                D(nc.vector.memset(qbd, 0.0))
                settle()
                q5 = qbd.rearrange("p g (b h t) -> p g b h t", b=DEC_BATCH, h=2)
                for hh in range(2):
                    r_ = slice(hh * HD, (hh + 1) * HD)
                    for g in range(G):
                        D(cp(q5[r_, g, :, hh, :], bt(qkv[r_, g, TP:T])), "qbd" if (hh, g) == (1, G - 1) else None)

                sm_mask = c("s_masks", 6 * TS, rows=TS).rearrange("p (k s) -> p k s", k=6)
                i32 = ident[0:TS, 0:TS]
                for hh in range(2):
                    dve.wait_ge(tensor_done, TL.value(l, ("s_pair", hh)))
                    pv = bank[hh][0:TS, 0:5 * J * TS].rearrange("p (k j s) -> p k j s", k=5, j=J)
                    so = sm[0:TS, hh].rearrange("p k (j s) -> p k j s", j=J)
                    D(tt(so[:, 0], pv[:, 0], b3(sm_mask[:, 0]), ALU.mult))
                    D(tt(so[:, 1], pv[:, 0], b3(sm_mask[:, 1]), ALU.mult))
                    D(tt(so[:, 2:6], pv[:, 1:5], sm_mask[:, 2:6].unsqueeze(2).to_broadcast([TS, 4, J, TS]), ALU.mult), ("s_pair", hh))
                    settle()
                    D(tt(so[:, 0], so[:, 0], b3(i32), ALU.add))
                    D(tt(so[:, 2], so[:, 2], b3(i32), ALU.add), ("s_masked", hh))
                settle()
                dve.wait_ge(tensor_done, TL.value(l, "s_xinc"))
                D(tt(sm[0:TS, :, 2], sm[0:TS, :, 2], bank[1][0:TS, 0:2 * J * TS].rearrange("p (h c) -> p h c", h=2), ALU.add), "s_x")
                sel = c("s_batch", DEC_BATCH, rows=TS).unsqueeze(2).to_broadcast([TS, DEC_BATCH, P])

                def select(j):
                    s_ = slice(j * P, (j + 1) * P)
                    if j:
                        dve.wait_ge(tensor_done, TL.value(l, ("s_state", j - 1)))
                    D(tt(vsel[0:TS], b3(tok2[0:TS, 2, s_], DEC_BATCH), sel, ALU.mult))
                    dve.wait_ge(scalar_done, SL.value(l, ("u", 2)))
                    D(tt(usel[0:TS], b3(um2[0:TS, s_], DEC_BATCH), sel, ALU.mult), ("s_sel", j))

                def next_states(j):
                    dve.wait_ge(tensor_done, TL.value(l, ("s_state", j)))
                    w = wkv_s[:, j]
                    D(tt(w, w, bank[j][:, :].rearrange("p (b v) -> p b v", b=DEC_BATCH), ALU.add), ("s_state", j))
                    settle()
                    D(tt(w, w, wend[:, j, 2:].unsqueeze(2).to_broadcast([P, DEC_BATCH, HD]), ALU.mult), "wkv_s" if j == J - 1 else None)

                dve.wait_ge(scalar_done, SL.value(l, ("tok", 2, 2)))
                select(0)
                dve.wait_ge(tensor_done, TL.value(l, ("conv", "mean")))
                for ch in range(2):
                    D(stt(ycv[:, ch, :], bank[7][:, 0:T], -1.0 / 256, ycv[:, ch, :], ALU.mult, ALU.add),
                      "conv_mean" if ch else None)
                for j in range(J):
                    dve.wait_ge(tensor_done, TL.value(l, ("ln_mu", j)))
                    D(stt(oT[:, j, :], bank[(3, 5, 6)[j]][:, 0:T], -1.0 / HD, oT[:, j, :], ALU.mult, ALU.add), ("ln_mu", j))
                next_states(0)
                select(1)
                dve.wait_ge(scalar_done, SL.value(l, "conv_std"))
                D(nc.vector.reciprocal(yc2[:, 0, :], yc2[:, 0, :]))
                settle()
                for ch in range(2):
                    D(tt(ycv[:, ch, :], ycv[:, ch, :], yc2[:, 0, :], ALU.mult))
                settle()
                for ch in range(2):
                    D(ts(ycv[:, ch, :], ycv[:, ch, :], pr("conv_g", ch), pr("conv_beta", ch), ALU.mult, ALU.add),
                      "conv_norm" if ch else None)
                next_states(1)
                select(2)
                for j in range(J):
                    dve.wait_ge(scalar_done, SL.value(l, ("ln_var", j)))
                D(nc.vector.reciprocal(tmp_ln, tmp_ln))
                D(tt(bon, bon, xs[:, C_V:C_V + J, :], ALU.mult))
                settle()
                D(tt(oT, oT, tmp_ln, ALU.mult))
                settle()
                for j in range(J):
                    D(ts(oT[:, j, :], oT[:, j, :], pr("lnx_g", j), pr("lnx_b", j), ALU.mult, ALU.add))
                settle()
                D(tt(oT, oT, bon, ALU.add))
                next_states(2)
                dve.wait_ge(scalar_done, SL.value(l, "conv_tanh"))
                D(ts(yc2, yc2, 0.5, 0.5, ALU.mult, ALU.add))
                D(tt(h[:, 5:5 + J, :], oT, gz, ALU.mult))
                settle()
                D(tt(h[:, 0:2, :], yc2, ycv, ALU.mult), "rwkv_out")
                mask = c("mask", 2 * G * TP).rearrange("p (q g k) -> p q g k", q=2, g=G)

                def softmax_in(u, s_, rows=P):
                    settle()
                    D(nc.vector.tensor_reduce(astat[0:rows, 0, u:u + 1], s_, AX_X, ALU.max))
                    settle()
                    D(ts(astat[0:rows, 1, u:u + 1], astat[0:rows, 0, u:u + 1], -ATTN_SCALE, None, ALU.mult), ("nmax", u))

                def softmax_out(u, s_, name, rows=P):
                    dve.wait_ge(scalar_done, SL.value(l, ("exp", u)))
                    D(nc.vector.reciprocal(astat[0:rows, 3, u:u + 1], astat[0:rows, 2, u:u + 1]))
                    settle()
                    D(ts(s_, s_, astat[0:rows, 3, u:u + 1], None, ALU.mult), name)

                def unit(u):
                    qt = u % 2
                    return sp_[:, qt, 0:G * (qt + 1) * P]

                def masked(u):
                    qt = u % 2
                    b = (2 * u) % 4
                    if u >= 2:
                        dve.wait_ge(tensor_done, TL.value(l, ("pT", u - 2, (u - 2) % 2)))
                    if qt == 0:
                        dve.wait_ge(tensor_done, TL.value(l, ("scores", u, 1)))
                        D(tt(unit(u).rearrange("p (g k) -> p g k", g=G), bank[b][:, 0:G * P].rearrange("p (g k) -> p g k", g=G),
                             mask[:, 0, :, 0:P], ALU.add), ("masked", u, 0))
                    else:
                        dve.wait_ge(tensor_done, TL.value(l, ("scores", u, 0)))
                        D(tt(sp_[:, 1, 0:2 * TP], bank[b][:, :], mask[:, 1, 0:2, :].rearrange("p g k -> p (g k)"), ALU.add),
                          ("masked", u, 0))
                        dve.wait_ge(tensor_done, TL.value(l, ("scores", u, 1)))
                        D(tt(sp_[:, 1, 2 * TP:], bank[b + 1][:, 0:TP], mask[:, 1, 2, :], ALU.add), ("masked", u, 1))
                    softmax_in(u, unit(u))

                for pair_ in range(2):
                    masked(2 * pair_)
                    if pair_ == 0:
                        dve.wait_ge(scalar_done, SL.value(l, "mix_hi"))
                        low(h_lo[:, 0:2, :], h[:, 0:2, :], h_hi[:, 0:2, :])
                        low(h_lo[:, 5:5 + J, :], h[:, 5:5 + J, :], h_hi[:, 5:5 + J, :], "mix_lo")
                    masked(2 * pair_ + 1)
                    for u in (2 * pair_, 2 * pair_ + 1):
                        softmax_out(u, unit(u), ("probs", u))
                dve.wait_ge(tensor_done, TL.value(l, "s_scores"))
                D(tt(ss[0:64], bank[2][0:64, 0:G * (P + TS)], c("mask_s", G * (P + TS), rows=64), ALU.add), "s_scores")
                softmax_in(4, ss[0:64], 64)
                softmax_out(4, ss[0:64], "s_probs", 64)
                for u in range(NW):
                    split(UNITS["out"] + u)
                normalise("mem", memx, hm, mem_rs, MEM, (hm_hi, hm_lo))
                dve.wait_ge(scalar_done, SL.value(l, "attn_hi"))
                low(h_lo[:, 2:2 + G, :], h[:, 2:2 + G, :], h_hi[:, 2:2 + G, :], "attn_lo")

                for t in range(KT):
                    if t:
                        split(next_unit(UNITS["out"] + t - 1))
                    dve.wait_ge(tensor_done, TL.value(l, ("out", "cols", t)))
                    D(tt(x[:, t, :], bank[t % 7][:, 0:T], x[:, t, :], ALU.add), ("x_out", t))

                dve.wait_ge(stored, store_value(l, "wkv_s"))
                D(nc.vector.memset(qz, 0.0), "qz_clear")
                split(next_unit(UNITS["out"] + KT - 1))
                normalise("xattn", x, h, rs, T, (h_hi, h_lo), lambda k: split(next_unit(kv_unit(k // 4))) if k in (0, 4) else None)
                for t in range(2, K_EARLY):
                    split(next_unit(kv_unit(t)))
                for t in range(KT):
                    split(next_unit(UNITS["q"] + t))
                for t in range(K_EARLY, KT):
                    split(next_unit(kv_unit(t)))
                def two_units(hd):
                    if hd < 4:
                        return bank[hd][:, :].rearrange("p (q m) -> p q m", q=2), slice(2 * hd, 2 * hd + 2)
                    return bank[hd][:, 0:MEM].unsqueeze(1), slice(hd + 4, hd + 5)

                def row_max(hd):
                    src, u = two_units(hd)
                    dve.wait_ge(tensor_done, TL.value(l, ("xs", u.stop - 1)))
                    D(nc.vector.tensor_reduce(xstat[:, 0, u], src, AX_X, ALU.max))
                    settle()
                    D(ts(xstat[:, 1, u], xstat[:, 0, u], -X_SCALE, None, ALU.mult), ("xnmax", hd))

                def weigh(hd):
                    src, u = two_units(hd)
                    n = u.stop - u.start
                    dve.wait_ge(scalar_done, SL.value(l, ("xexp", u.stop - 1)))
                    D(nc.vector.reciprocal(xstat[:, 3, u], xstat[:, 2, u]))
                    settle()
                    D(tt(px[:, u, :], px[:, u, :], xstat[:, 3, u].unsqueeze(2).to_broadcast([P, n, MEM]), ALU.mult), ("xprobs", hd))

                row_max(0)
                for u in range(8):
                    if u % 2 == 0 and u < 6:
                        row_max(u // 2 + 1)
                    split(next_unit(kv_unit(KT + u)))
                    if u % 2:
                        weigh(u // 2)
                for hd in (4, 5):
                    row_max(hd)
                    weigh(hd)
                for d in range(4):
                    dve.wait_ge(scalar_done, SL.value(l, ("ox", d)))
                    low(ox_lo[:, 2 * d:2 * d + 2, 0:TP], bank[d][:, :].rearrange("p (a c) -> p a c", a=2),
                        ox_hi[:, 2 * d:2 * d + 2, 0:TP], ("ox_lo", d))
                for half in range(2):
                    for n in range(2):
                        dve.wait_ge(scalar_done, SL.value(l, ("oxs_hi", half, 2 * n + 1)))
                        for hd in (2 * n, 2 * n + 1):
                            low(sample_out(ox_lo, half, hd), head_columns(half, hd), sample_out(ox_hi, half, hd),
                                ("oxs_lo", half, n) if hd % 2 else None)
                    for u in (range(1) if half == 0 else range(1, NW)):
                        split(UNITS["o"] + u)
                for t in range(KT):
                    if t:
                        split(next_unit(UNITS["o"] + t - 1))
                    dve.wait_ge(tensor_done, TL.value(l, ("o", "cols", t)))
                    b = (5, 6, 7, 0, 1, 2, 3)[t % 7]
                    D(tt(x[:, t, :], bank[b][:, 0:T], x[:, t, :], ALU.add), ("x_o", t))
                split(next_unit(UNITS["o"] + KT - 1))
                ffn("ffn2")
            l = DEPTH - 1
            normalise("final", x, h, rs, T)

        return {"t": (TL.at, TL.per_layer()), "v": (VL.at, VL.per_layer()), "s": (SL.at, SL.per_layer()),
                "p": (PL.at, PL.per_layer()), "stores": stores}


def pack_columns(w, width=P):
    n, m = w.shape[1] // 256, 256 // width
    return w.reshape(KT, P, n, m, width).transpose(2, 1, 3, 0, 4).reshape(n, P, SLAB)


def pack_down(w):
    return w.reshape(FT, P, 2, 512).transpose(2, 0, 1, 3).reshape(FT // 2, 4, P, 512).transpose(0, 2, 1, 3).reshape(-1, P, SLAB)


def pack_ffn(i, l, tag):
    gate, up = (i[tag + n][l].reshape(D_MODEL, FT, P) for n in ("_w_gate", "_w_up"))
    both = pack_columns(np.stack([gate, up], 2).reshape(D_MODEL, 2 * D_FF))
    return np.concatenate([both, pack_down(i[tag + "_w_down"][l])], 0)


def in_order():
    conv, attn, rwkv = 0, 512, 512 + 1152
    starts = [rwkv + 1152, rwkv + 1280] + [rwkv + 384 + P * j for j in range(J)] + [rwkv + P * j for j in range(J)]
    starts += [rwkv + 768 + P * j for j in range(J)] + [conv, conv + 256, conv + 128, conv + 384]
    starts += [attn + P * j for j in range(9)]
    return np.concatenate([np.arange(s, s + P) for s in starts])


def pad(a):
    return np.concatenate([a, np.zeros(a.shape[:-1] + (SLAB - a.shape[-1],), a.dtype)], -1)


def pack_layer(i, l):
    k, v = ([i[f"cache_win{g}_{n}"][l] for g in (1, 2, 3)] for n in "kv")
    B = DEC_BATCH

    def phases(a, dil):
        return a.reshape(B, a.shape[1] // dil, dil, 2, HD).transpose(0, 2, 1, 3, 4)[:, :4]
    kc = np.concatenate([a.reshape(B, -1, P) for a in (k[0], phases(k[1], 4), phases(k[2], 16))], 1)
    vc = np.concatenate([a.reshape(B, -1, P) for a in (v[0], phases(v[1], 4), phases(v[2], 16))], 1)
    kc = kc.transpose(0, 2, 1).reshape(B // 2, 2, P, 896).transpose(0, 2, 1, 3).reshape(B // 2, P, 1792)
    vc = vc.reshape(B // 2, 2, 7, P, P).transpose(0, 3, 1, 2, 4).reshape(B // 2, P, 1792)
    memk = i["cache_mem_k"][l].reshape(B, MEM, KT, P).transpose(0, 3, 2, 1).reshape(B, P, SLAB)
    memv = i["cache_mem_v"][l].reshape(B, 2, P, D_MODEL).transpose(0, 2, 1, 3).reshape(B, P, SLAB)
    parts = {"ffn1": pack_ffn(i, l, "ffn1"), "in": pack_columns(i["w_in"][l][:, in_order()]), "wink": pad(kc), "winv": pad(vc),
             "out": pack_columns(i["w_out"][l]), "q": pack_columns(i["xattn_w_q"][l]), "kv": np.concatenate([
                 pack_columns(i["xattn_w_kv"][l][:, :D_MODEL]), pack_columns(i["xattn_w_kv"][l][:, D_MODEL:], 256)], 0),
             "memk": memk, "memv": memv, "o": pack_columns(i["xattn_w_o"][l]), "ffn2": pack_ffn(i, l, "ffn2")}
    return np.stack([parts[name][n] for name, n in ORDER])


def pack_small(i, l):
    c0 = in_order()[:NC_TILES * P] - 1664

    def cols(v):
        return v.reshape(-1, P).T
    lora = np.concatenate([np.concatenate([i["rwkv_w_up"][l], i["rwkv_a_up"][l]], 0), i["rwkv_g_up"][l]], 1)
    parts = [cols(i["ffn1_norm"][l]), cols(i["mix_norm"][l]), cols(i["xattn_norm"][l]), cols(i["mem_norm"][l]),
             cols(i["ffn2_norm"][l]), cols(i["final_norm"]), i["conv_w"][l].reshape(TAPS, 2, P).transpose(2, 1, 0).reshape(P, -1),
             cols(i["conv_b"][l]), cols(i["conv_ln_g"][l]), cols(i["conv_ln_b"][l]), cols(i["rwkv_shift_mix"][l][c0]),
             cols(i["rwkv_w0"][l]), cols(i["rwkv_a0"][l]), cols(i["rwkv_k_k"][l]), cols(i["rwkv_k_a"][l]),
             cols(i["rwkv_r_k"][l].reshape(-1)), cols(i["rwkv_lnx_g"][l]), cols(i["rwkv_lnx_b"][l]),
             i["state_shift"][l][:, c0].reshape(DEC_BATCH, NC_TILES, P).transpose(2, 1, 0).reshape(P, -1), lora]
    return np.concatenate(parts, 1)


def tokens(xp, xs_):
    both = np.concatenate([xp.reshape(TP, D_MODEL), xs_.reshape(TS, D_MODEL)], 0)
    return both.T.reshape(KT, P, T).transpose(1, 0, 2)


def pack(inputs):
    i = {k: np.asarray(v) for k, v in inputs.items()}
    s = i["state_wkv"].reshape(DEPTH, DEC_BATCH, J, 2, HD, HD)
    arrays = {
        "x_in": tokens(i["x_prompt"], i["x_sample"]),
        "mem_in": i["mem_prompt"].reshape(MEM, KT, P).transpose(2, 1, 0),
        "stream": np.stack([pack_layer(i, l) for l in range(DEPTH)]),
        "small": np.stack([pack_small(i, l) for l in range(DEPTH)], 1),
        "consts": constants(),
        "conv_hist": i["cache_conv"].reshape(DEPTH, DEC_BATCH, HIST, 2, P).transpose(0, 4, 3, 1, 2),
        "wkv_in": s.transpose(0, 3, 5, 2, 1, 4).reshape(DEPTH, P, J, DEC_BATCH, HD),
    }
    for g in (1, 2, 3):
        for n in "kv":
            arrays[f"win{g}{n}"] = i[f"cache_win{g}_{n}"].reshape(DEPTH, DEC_BATCH, -1)
    return {k: np.ascontiguousarray(v) for k, v in arrays.items()}


SHAPES_OUT = {
    "y": (P, KT, T), "conv": (DEPTH, P, 2, HIST + DEC_BATCH * HIST), "kv": (DEPTH, P, 2 * G, T),
    "shift": (DEPTH, P, NC_TILES, 1 + DEC_BATCH), "wkv_p": (DEPTH, P, J * P), "wkv_s": (DEPTH, P, J, DEC_BATCH, HD),
    "memk": (DEPTH, P, KT, MEM), "memv": (DEPTH, P, 2, D_MODEL),
}


def build(nc, arrays, known):
    ap = {k: nc.dram_tensor(k, a.shape, F32, kind="ExternalInput").ap() for k, a in arrays.items()}
    outs = {k: nc.dram_tensor("out_" + k, s, F32, kind="ExternalOutput").ap() for k, s in SHAPES_OUT.items()}
    copies = []
    for g in (1, 2, 3):
        for n in "kv":
            size = (CACHED[g - 1] - DEC_SEQ) * P
            dst = nc.dram_tensor(f"out_win{g}{n}", (DEPTH, DEC_BATCH, size), F32, kind="ExternalOutput").ap()
            copies.append((ap[f"win{g}{n}"][:, :, DEC_SEQ * P:], dst))
    return program(nc, ap["x_in"], ap["mem_in"], ap["stream"], ap["small"], ap["consts"], ap["conv_hist"], ap["wkv_in"],
                   copies, tuple(outs.values()), known)


def unpack(r):
    B, L = DEC_BATCH, DEPTH
    y = r["out_y"].transpose(2, 1, 0).reshape(T, D_MODEL)
    conv = r["out_conv"].transpose(0, 3, 2, 1).reshape(L, HIST + B * HIST, 256)
    kv = r["out_kv"].reshape(L, 2, HD, 2, G, T).transpose(3, 4, 0, 5, 1, 2)
    shift = r["out_shift"].transpose(0, 3, 2, 1).reshape(L, 1 + B, NC_TILES * P)
    c0 = in_order()[:NC_TILES * P] - 1664
    shift_ref = np.empty_like(shift)
    shift_ref[:, :, c0] = shift

    def states(a):
        n = a.shape[3]
        a = a.reshape(L, 2, HD, J, n, 2, HD)
        a = np.stack([a[:, hh, :, :, :, hh] for hh in range(2)], 1)
        return a.transpose(0, 4, 3, 1, 5, 2).reshape(L, n, 2 * J, HD, HD)
    wins_p, wins_s = [], []
    for g in range(G):
        for n in range(2):
            new = kv[n, g]
            keep = min(GROUPS[g][0], TP)
            wins_p.append(new[:, None, TP - keep:TP])
            old = r[f"out_win{g + 1}{'kv'[n]}"].reshape(L, B, -1, 2, HD)
            wins_s.append(np.concatenate([old, new[:, TP:].reshape(L, B, DEC_SEQ, 2, HD)], 2))
    memk = r["out_memk"].transpose(0, 3, 2, 1).reshape(L, 1, MEM, 4, 256)
    memv = r["out_memv"].transpose(0, 2, 1, 3).reshape(L, 1, MEM, 4, 256)
    out = (y[:TP].reshape(1, TP, D_MODEL), y[TP:].reshape(B, DEC_SEQ, D_MODEL), conv[:, None, :HIST], *wins_p,
           shift_ref[:, :1], states(r["out_wkv_p"].reshape(L, P, J, 1, P)), memk, memv,
           conv[:, HIST:].reshape(L, B, HIST, 256), *wins_s, shift_ref[:, 1:],
           r["out_wkv_s"].reshape(L, 2, HD, J, B, HD).transpose(0, 4, 3, 1, 5, 2).reshape(L, B, 2 * J, HD, HD))
    return tuple(np.ascontiguousarray(a) for a in out)


def kernel(**inputs):
    import concourse.bacc as bacc
    from concourse.bass_utils import run_bass_kernel_spmd

    arrays = pack(inputs)
    known = build(bacc.Bacc("TRN2", target_bir_lowering=False, num_devices=1), arrays, None)
    nc = bacc.Bacc("TRN2", target_bir_lowering=False, num_devices=1)
    build(nc, arrays, known)
    r = run_bass_kernel_spmd(nc, [arrays], core_ids=[0])
    return unpack(r.results[0])
```
